# Optimizing a Trainium2 kernel written in Bass

```python
import math
import jax, jax.numpy as jnp
from jax import lax
import numpy as np

D_MODEL = 1024
BATCH = 1
SEQ = 1024
DEPTH = 2
DEC_BATCH = 8
DEC_SEQ = 8
PAST_LEN = 1024
PAGE_SIZE = 128

N_EVEN = (DEPTH + 1) // 2
N_ODD = DEPTH // 2
H_A = 8
DH_A = 64
FOX_W = H_A * DH_A
Q_BLOCK = 128
H_B = 8
DH_B = 64
RW_W = H_B * DH_B
R_W = 64
R_A = 64
R_V = 32
R_G = 128
RW_GN_EPS = 64e-5
H_C = 8
DK_C = 128
DV_C = 128
GDN_K = H_C * DK_C
GDN_V = H_C * DV_C
GDN_QKV = 2 * GDN_K + GDN_V
CONV_C = 4
GDN_CHUNK = 64
D_FF = 2816
CONV_F = 3
EPS = 1e-6

FOX_COLS = 4 * FOX_W + H_A
RW_COLS = 3 * RW_W + R_W + R_A + R_G
EV_IN = FOX_COLS + RW_COLS
EV_MIX = FOX_W + RW_W
OD_IN = GDN_QKV + GDN_V + 2 * H_C

kernel_name = 'fox_rwkv7_gdn_convffn_hybrid_step'

F32 = jnp.float32

def rmsnorm(x, g, eps=EPS):
    xf = x.astype(F32)
    y = xf * lax.rsqrt(jnp.mean(xf * xf, axis=-1, keepdims=True) + eps)
    return (y * g.astype(F32)).astype(x.dtype)

def l2norm(x, eps=1e-6):
    xf = x.astype(F32)
    return xf * lax.rsqrt(jnp.sum(xf * xf, axis=-1, keepdims=True) + eps)

def split_cols(p, sizes):
    offs = [int(o) for o in np.cumsum(sizes)[:-1]]
    return jnp.split(p, offs, axis=-1)

def causal_dwconv(prev, x, w):
    width = w.shape[0]
    T = x.shape[1]
    xx = jnp.concatenate([prev.astype(x.dtype), x], axis=1)
    y = xx[:, 0:T] * w[0]
    for i in range(1, width):
        y = y + xx[:, i:i + T] * w[i]
    return y, xx[:, T:]

def fox_attend_prompt(q, k, v, logf):
    B, T, H, Dh = q.shape
    n_blk = T // Q_BLOCK
    scale = Dh ** -0.5
    Fk = jnp.cumsum(logf, axis=1).transpose(0, 2, 1)
    qb = q.reshape(B, n_blk, Q_BLOCK, H, Dh).transpose(1, 0, 2, 3, 4)
    Fqb = Fk.reshape(B, H, n_blk, Q_BLOCK).transpose(2, 0, 1, 3)
    kpos = jnp.arange(T)

    def one_block(args):
        qi, Fq, blk = args
        s = jnp.einsum('bqhd,bkhd->bhqk', qi, k, preferred_element_type=F32) * scale
        s = s + Fq[..., :, None] - Fk[..., None, :]
        qpos = blk * Q_BLOCK + jnp.arange(Q_BLOCK)
        s = jnp.where(kpos[None, :] <= qpos[:, None], s, -jnp.inf)
        p = jax.nn.softmax(s, axis=-1)
        return jnp.einsum('bhqk,bkhd->bqhd', p.astype(v.dtype), v)

    o = lax.map(one_block, (qb, Fqb, jnp.arange(n_blk)))
    return o.transpose(1, 0, 2, 3, 4).reshape(B, T, H, Dh)

def fox_attend_sample(q, k, v, logf, pool_k, pool_v, pool_lf, page_table):
    B, T, H, Dh = q.shape
    k_past = pool_k[page_table].reshape(B, -1, H, Dh)
    v_past = pool_v[page_table].reshape(B, -1, H, Dh)
    lf_past = pool_lf[page_table].reshape(B, -1, H)
    P = k_past.shape[1]
    k_all = jnp.concatenate([k_past.astype(k.dtype), k], axis=1)
    v_all = jnp.concatenate([v_past.astype(v.dtype), v], axis=1)
    Fk = jnp.cumsum(jnp.concatenate([lf_past.astype(F32), logf], axis=1), axis=1).transpose(0, 2, 1)
    Fq = Fk[..., P:]
    s = jnp.einsum('bqhd,bkhd->bhqk', q, k_all, preferred_element_type=F32) * (Dh ** -0.5)
    s = s + Fq[..., :, None] - Fk[..., None, :]
    mask = jnp.arange(P + T)[None, :] <= (P + jnp.arange(T))[:, None]
    p = jax.nn.softmax(jnp.where(mask, s, -jnp.inf), axis=-1)
    return jnp.einsum('bhqk,bkhd->bqhd', p.astype(v_all.dtype), v_all)

def rwkv7_scan(S0, r, w, k, v, a, b):
    def step(S, inp):
        rt, wt, kt, vt, at, bt = inp
        sa = jnp.einsum('bhij,bhj->bhi', S, at)
        S = S * wt[:, :, None, :] + sa[..., None] * bt[:, :, None, :] + vt[..., None] * kt[:, :, None, :]
        return S, jnp.einsum('bhij,bhj->bhi', S, rt)
    xs = tuple(t.transpose(1, 0, 2, 3) for t in (r, w, k, v, a, b))
    S, y = lax.scan(step, S0, xs)
    return y.transpose(1, 0, 2, 3), S

def rwkv7_mix(p, shift_prev, S0, v_first, e, W):
    B, T, _ = p.shape
    p_prev = jnp.concatenate([shift_prev[:, None, :].astype(p.dtype), p[:, :-1]], axis=1)
    ps = p + (p_prev - p) * W['rw_mu'][e]
    r, k, v, wd, ad, gd = split_cols(ps, [RW_W, RW_W, RW_W, R_W, R_A, R_G])
    w_log = -jax.nn.softplus(-(W['rw_w0'][e] + jnp.tanh(wd) @ W['rw_w2'][e]).astype(F32)) - 0.5
    decay = jnp.exp(-jnp.exp(w_log))
    a = jax.nn.sigmoid((W['rw_a0'][e] + ad @ W['rw_a2'][e]).astype(F32))
    g = jax.nn.sigmoid(gd) @ W['rw_g2'][e]
    if e == 0:
        v_first = v
    else:
        gate = jax.nn.sigmoid(W['rw_v0'][e - 1] + (v @ W['rw_v1'][e - 1]) @ W['rw_v2'][e - 1])
        v = v + (v_first - v) * gate
    hs = (B, T, H_B, DH_B)
    hw = (H_B, DH_B)
    rf = r.astype(F32).reshape(hs)
    kf = k.astype(F32).reshape(hs)
    vf = v.astype(F32).reshape(hs)
    af = a.reshape(hs)
    kk = l2norm(kf * W['rw_k_k'][e].reshape(hw))
    kf = kf * (1.0 + (af - 1.0) * W['rw_k_a'][e].reshape(hw))
    y, S = rwkv7_scan(S0.astype(F32), rf, decay.reshape(hs), kf, vf, -kk, kk * af)
    mu = jnp.mean(y, axis=-1, keepdims=True)
    var = jnp.mean(jnp.square(y - mu), axis=-1, keepdims=True)
    y = (y - mu) * lax.rsqrt(var + RW_GN_EPS)
    y = y * W['rw_ln_w'][e].reshape(hw) + W['rw_ln_b'][e].reshape(hw)
    y = y + jnp.sum(rf * kf * W['rw_r_k'][e], axis=-1, keepdims=True) * vf
    y = y.reshape(B, T, RW_W).astype(p.dtype) * g
    return y, p[:, -1], S, v_first

def gated_delta_chunked(q, k, v, g, beta, S0):
    B, T, H, Dk = q.shape
    Dv = v.shape[-1]
    C = math.gcd(T, GDN_CHUNK)
    N = T // C

    def chunks(t):
        return t.reshape(B, N, C, H, -1).transpose(1, 0, 3, 2, 4)
    qc, kc, vc = chunks(q), chunks(k), chunks(v)
    gc = g.reshape(B, N, C, H).transpose(1, 0, 3, 2)
    bc = beta.reshape(B, N, C, H).transpose(1, 0, 3, 2)
    G = jnp.cumsum(gc, axis=-1)
    tril = jnp.tril(jnp.ones((C, C), bool))
    strict = jnp.tril(jnp.ones((C, C), bool), -1)
    diff = G[..., :, None] - G[..., None, :]
    gamma = jnp.where(tril, jnp.exp(jnp.where(tril, diff, 0.0)), 0.0)
    kb = kc * bc[..., None]
    M = jnp.where(strict, jnp.einsum('nbhid,nbhjd->nbhij', kb, kc) * gamma, 0.0)
    eye = jnp.eye(C, dtype=F32)
    Tinv = lax.linalg.triangular_solve(eye + M, jnp.broadcast_to(eye, M.shape), left_side=True, lower=True)
    u = Tinv @ (vc * bc[..., None])
    wk = Tinv @ (kb * jnp.exp(G)[..., None])
    A = jnp.where(tril, jnp.einsum('nbhid,nbhjd->nbhij', qc, kc) * gamma, 0.0)

    def step(S, inp):
        qi, ki, ui, wi, Gi, Ai = inp
        v_new = ui - wi @ S
        o = (qi * jnp.exp(Gi)[..., None]) @ S + Ai @ v_new
        Gl = Gi[..., -1:]
        S = S * jnp.exp(Gl)[..., None] + jnp.einsum('bhcd,bhce->bhde', ki * jnp.exp(Gl - Gi)[..., None], v_new)
        return S, o
    S, o = lax.scan(step, S0, (qc, kc, u, wk, G, A))
    return o.transpose(1, 0, 3, 2, 4).reshape(B, T, H, Dv), S

def gdn_mix(p, conv_prev, S0, o_idx, W):
    B, T, _ = p.shape
    qkv, z, bl, al = split_cols(p, [GDN_QKV, GDN_V, H_C, H_C])
    qkv, new_conv = causal_dwconv(conv_prev, qkv, W['gdn_conv_w'][o_idx])
    qkv = jax.nn.silu(qkv)
    q, k, v = split_cols(qkv, [GDN_K, GDN_K, GDN_V])
    q = l2norm(q.reshape(B, T, H_C, DK_C)) * (DK_C ** -0.5)
    k = l2norm(k.reshape(B, T, H_C, DK_C))
    v = v.astype(F32).reshape(B, T, H_C, DV_C)
    beta = jax.nn.sigmoid(bl.astype(F32))
    g = -jnp.exp(W['gdn_A_log'][o_idx].astype(F32)) * jax.nn.softplus(al.astype(F32) + W['gdn_dt_bias'][o_idx])
    o, S = gated_delta_chunked(q, k, v, g, beta, S0.astype(F32))
    o = rmsnorm(o, W['gdn_norm_w'][o_idx]) * jax.nn.silu(z.astype(F32).reshape(B, T, H_C, DV_C))
    return o.reshape(B, T, GDN_V).astype(p.dtype), new_conv, S

def run_trunk(x, fox_past, rw_state, rw_shift, gdn_state, gdn_conv, ffn_conv, page_table, W):
    B, T, _ = x.shape
    fk, fv, flf, rwS, rwSh, gS, gCv, fCv = [], [], [], [], [], [], [], []
    v_first = None
    for layer in range(DEPTH):
        xn = rmsnorm(x, W['norm_mix'][layer])
        if layer % 2 == 0:
            e = layer // 2
            p = xn @ W['ev_w_in'][e]
            q, k, v, og, fl = split_cols(p[..., :FOX_COLS], [FOX_W, FOX_W, FOX_W, FOX_W, H_A])
            q = rmsnorm(q.reshape(B, T, H_A, DH_A), W['fox_q_gain'][e])
            k = rmsnorm(k.reshape(B, T, H_A, DH_A), W['fox_k_gain'][e])
            v = v.reshape(B, T, H_A, DH_A)
            logf = jax.nn.log_sigmoid(fl.astype(F32) + W['fox_b_f'][e])
            if fox_past is None:
                o = fox_attend_prompt(q, k, v, logf)
            else:
                o = fox_attend_sample(q, k, v, logf, fox_past[0][e], fox_past[1][e], fox_past[2][e], page_table)
            o_a = o.reshape(B, T, FOX_W) * jax.nn.sigmoid(og)
            o_b, sh, S, v_first = rwkv7_mix(p[..., FOX_COLS:], rw_shift[e], rw_state[e], v_first, e, W)
            mix = jnp.concatenate([o_a, o_b], axis=-1) @ W['ev_w_out'][e]
            fk.append(k)
            fv.append(v)
            flf.append(logf)
            rwS.append(S)
            rwSh.append(sh)
        else:
            o_idx = layer // 2
            p = xn @ W['od_w_in'][o_idx]
            o_c, cv, S = gdn_mix(p, gdn_conv[o_idx], gdn_state[o_idx], o_idx, W)
            mix = o_c @ W['od_w_out'][o_idx]
            gS.append(S)
            gCv.append(cv)
        x = x + mix
        xn = rmsnorm(x, W['norm_ffn'][layer])
        h = xn @ W['ffn_w_up'][layer]
        h, buf = causal_dwconv(ffn_conv[layer], h, W['ffn_conv_w'][layer])
        h = h + W['ffn_conv_b'][layer]
        u, gt = jnp.split(h, 2, axis=-1)
        x = x + (jax.nn.silu(gt) * u) @ W['ffn_w_down'][layer]
        fCv.append(buf)
    y = rmsnorm(x, W['norm_out'])
    return (y, jnp.stack(fk), jnp.stack(fv), jnp.stack(flf), jnp.stack(rwS), jnp.stack(rwSh),
            jnp.stack(gS), jnp.stack(gCv), jnp.stack(fCv))

def setup_inputs(seed: int = 0) -> dict:
    key = jax.random.key(seed)
    ks = iter(jax.random.split(key, 64))

    def nrm(shape, s=1.0):
        return s * jax.random.normal(next(ks), shape, F32)

    def uni(shape, lo, hi):
        return jax.random.uniform(next(ks), shape, F32, lo, hi)

    n_pages = PAST_LEN // PAGE_SIZE
    n_used = DEC_BATCH * n_pages
    n_pool = n_used + n_used // 4
    page_table = jax.random.permutation(next(ks), n_pool)[:n_used].reshape(DEC_BATCH, n_pages).astype(jnp.int32)
    dt = jnp.exp(uni((N_ODD, H_C), math.log(1e-3), math.log(1e-1)))
    d = D_MODEL
    return {
        'x_prompt': nrm((BATCH, SEQ, d)),
        'x_sample': nrm((DEC_BATCH, DEC_SEQ, d)),
        'cache_fox_k': nrm((N_EVEN, n_pool, PAGE_SIZE, H_A, DH_A)),
        'cache_fox_v': nrm((N_EVEN, n_pool, PAGE_SIZE, H_A, DH_A)),
        'cache_fox_logf': jax.nn.log_sigmoid(4.0 + nrm((N_EVEN, n_pool, PAGE_SIZE, H_A))),
        'state_rwkv': nrm((N_EVEN, DEC_BATCH, H_B, DH_B, DH_B), 0.5),
        'state_rwkv_shift': nrm((N_EVEN, DEC_BATCH, RW_COLS)),
        'state_gdn': nrm((N_ODD, DEC_BATCH, H_C, DK_C, DV_C), 0.1),
        'state_gdn_conv': nrm((N_ODD, DEC_BATCH, CONV_C - 1, GDN_QKV)),
        'state_ffn_conv': nrm((DEPTH, DEC_BATCH, CONV_F - 1, 2 * D_FF)),
        'page_table': page_table,
        'norm_mix': 1.0 + nrm((DEPTH, d), 0.05),
        'norm_ffn': 1.0 + nrm((DEPTH, d), 0.05),
        'norm_out': 1.0 + nrm((d,), 0.05),
        'ev_w_in': nrm((N_EVEN, d, EV_IN), d ** -0.5),
        'ev_w_out': nrm((N_EVEN, EV_MIX, d), EV_MIX ** -0.5),
        'fox_b_f': uni((N_EVEN, H_A), 2.0, 6.0),
        'fox_q_gain': 1.0 + nrm((N_EVEN, DH_A), 0.05),
        'fox_k_gain': 1.0 + nrm((N_EVEN, DH_A), 0.05),
        'rw_mu': uni((N_EVEN, RW_COLS), 0.0, 1.0),
        'rw_w0': uni((N_EVEN, RW_W), -6.0, -1.0),
        'rw_w2': nrm((N_EVEN, R_W, RW_W), 0.1 * R_W ** -0.5),
        'rw_a0': nrm((N_EVEN, RW_W), 0.1),
        'rw_a2': nrm((N_EVEN, R_A, RW_W), R_A ** -0.5),
        'rw_g2': nrm((N_EVEN, R_G, RW_W), R_G ** -0.5),
        'rw_k_k': 0.85 + nrm((N_EVEN, RW_W), 0.05),
        'rw_k_a': 1.0 + nrm((N_EVEN, RW_W), 0.05),
        'rw_r_k': nrm((N_EVEN, H_B, DH_B), 0.1),
        'rw_ln_w': 1.0 + nrm((N_EVEN, RW_W), 0.05),
        'rw_ln_b': nrm((N_EVEN, RW_W), 0.01),
        'rw_v0': 0.5 + nrm((N_EVEN - 1, RW_W), 0.1),
        'rw_v1': nrm((N_EVEN - 1, RW_W, R_V), RW_W ** -0.5),
        'rw_v2': nrm((N_EVEN - 1, R_V, RW_W), 0.1 * R_V ** -0.5),
        'od_w_in': nrm((N_ODD, d, OD_IN), d ** -0.5),
        'od_w_out': nrm((N_ODD, GDN_V, d), GDN_V ** -0.5),
        'gdn_conv_w': nrm((N_ODD, CONV_C, GDN_QKV), CONV_C ** -0.5),
        'gdn_A_log': jnp.log(uni((N_ODD, H_C), 1.0, 16.0)),
        'gdn_dt_bias': dt + jnp.log(-jnp.expm1(-dt)),
        'gdn_norm_w': 1.0 + nrm((N_ODD, DV_C), 0.05),
        'ffn_w_up': nrm((DEPTH, d, 2 * D_FF), d ** -0.5),
        'ffn_conv_w': nrm((DEPTH, CONV_F, 2 * D_FF), CONV_F ** -0.5),
        'ffn_conv_b': nrm((DEPTH, 2 * D_FF), 0.02),
        'ffn_w_down': nrm((DEPTH, D_FF, d), D_FF ** -0.5),
    }

def reference(x_prompt, x_sample, cache_fox_k, cache_fox_v, cache_fox_logf, state_rwkv, state_rwkv_shift,
              state_gdn, state_gdn_conv, state_ffn_conv, page_table, norm_mix, norm_ffn, norm_out,
              ev_w_in, ev_w_out, fox_b_f, fox_q_gain, fox_k_gain, rw_mu, rw_w0, rw_w2, rw_a0, rw_a2, rw_g2,
              rw_k_k, rw_k_a, rw_r_k, rw_ln_w, rw_ln_b, rw_v0, rw_v1, rw_v2, od_w_in, od_w_out, gdn_conv_w,
              gdn_A_log, gdn_dt_bias, gdn_norm_w, ffn_w_up, ffn_conv_w, ffn_conv_b, ffn_w_down):
    W = dict(norm_mix=norm_mix, norm_ffn=norm_ffn, norm_out=norm_out, ev_w_in=ev_w_in, ev_w_out=ev_w_out,
             fox_b_f=fox_b_f, fox_q_gain=fox_q_gain, fox_k_gain=fox_k_gain, rw_mu=rw_mu, rw_w0=rw_w0,
             rw_w2=rw_w2, rw_a0=rw_a0, rw_a2=rw_a2, rw_g2=rw_g2, rw_k_k=rw_k_k, rw_k_a=rw_k_a, rw_r_k=rw_r_k,
             rw_ln_w=rw_ln_w, rw_ln_b=rw_ln_b, rw_v0=rw_v0, rw_v1=rw_v1, rw_v2=rw_v2, od_w_in=od_w_in,
             od_w_out=od_w_out, gdn_conv_w=gdn_conv_w, gdn_A_log=gdn_A_log, gdn_dt_bias=gdn_dt_bias,
             gdn_norm_w=gdn_norm_w, ffn_w_up=ffn_w_up, ffn_conv_w=ffn_conv_w, ffn_conv_b=ffn_conv_b,
             ffn_w_down=ffn_w_down)
    Bp = x_prompt.shape[0]
    dt = x_prompt.dtype
    (y_prompt, fk_p, fv_p, flf_p, rw_p, rwsh_p, gdn_p, gcv_p, fcv_p) = run_trunk(
        x_prompt, None,
        jnp.zeros((N_EVEN, Bp, H_B, DH_B, DH_B), F32),
        jnp.zeros((N_EVEN, Bp, RW_COLS), dt),
        jnp.zeros((N_ODD, Bp, H_C, DK_C, DV_C), F32),
        jnp.zeros((N_ODD, Bp, CONV_C - 1, GDN_QKV), dt),
        jnp.zeros((DEPTH, Bp, CONV_F - 1, 2 * D_FF), dt),
        page_table, W)
    (y_sample, fk_s, fv_s, flf_s, rw_s, rwsh_s, gdn_s, gcv_s, fcv_s) = run_trunk(
        x_sample, (cache_fox_k, cache_fox_v, cache_fox_logf), state_rwkv, state_rwkv_shift,
        state_gdn, state_gdn_conv, state_ffn_conv, page_table, W)
    return (y_prompt, y_sample, fk_p, fv_p, flf_p, fk_s, fv_s, flf_s, rw_p, rw_s, rwsh_p, rwsh_s,
            gdn_p, gdn_s, gcv_p, gcv_s, fcv_p, fcv_s)


_drawn_inputs = setup_inputs


def setup_inputs(seed=0):
    import zlib

    import numpy as np

    out = dict(_drawn_inputs(seed))
    spreads = {}
    factors = {'cache_fox_logf': 5.414, 'fox_q_gain': 8.0, 'rw_w2': 8.0, 'rw_ln_b': 8.0}
    for name, (base, spread) in spreads.items():
        noise = np.random.default_rng([zlib.crc32(name.encode()), seed]).standard_normal(out[name].shape)
        drawn = base * np.exp(spread * noise) if base else spread * noise
        out[name] = __import__('jax').numpy.asarray(drawn.astype(out[name].dtype))
    for name, factor in factors.items():
        out[name] = (out[name] * factor).astype(out[name].dtype)
    return out
```

```python
from contextlib import ExitStack

import concourse.bass as bass
from concourse import mybir

F32 = mybir.dt.float32
F32R = mybir.dt.float32r
I32 = mybir.dt.int32
ACT = mybir.ActivationFunctionType
ALU = mybir.AluOpType
AX = mybir.AxisListType

P = 128
D = 1024
KD = D // P
SEQ = 1024
NB, TS = 8, 8
NS = NB * TS
NTOK = SEQ + NS
NT = SEQ // P
GROUPS = [(0, 364), (364, 364), (728, 360)]
GW = 364
H, DH = 8, 64
FOX_W = H * DH
FOX_COLS = 4 * FOX_W + H
RW_W = H * DH
R_W, R_A, R_G = 64, 64, 128
RW_COLS = 3 * RW_W + R_W + R_A + R_G
EV_IN = FOX_COLS + RW_COLS
PAST, PAGE = 1024, 128
NPG = PAST // PAGE
N_POOL = NB * NPG + NB * NPG // 4
DK = 128
GDN_W = H * DK
GDN_QKV = 3 * GDN_W
OD_IN = GDN_QKV + GDN_W + 2 * H
D_FF = 2816
NF = D_FF // P
EPS = 1e-6
RW_GN_EPS = 64e-5
RW_DECAY = -0.6065306597126334
NEG = -1e30


class Phase:

    used = []

    def __init__(self, nc, name):
        self.nc, self.name, self.ctx = nc, name, ExitStack()
        self.sems = []

    def __enter__(self):
        self.ctx.__enter__()
        return self

    def __exit__(self, *e):
        Phase.used += self.sems
        return self.ctx.__exit__(*e)

    def sb(self, name, shape, dt=F32):
        return self.ctx.enter_context(self.nc.sbuf_tensor(f"{self.name}_{name}", shape, dt))

    def ps(self, name, shape, dt=F32):
        return self.ctx.enter_context(self.nc.psum_tensor(f"{self.name}_{name}", shape, dt))

    def sem(self, name):
        self.sems.append(self.nc.alloc_semaphore(name=f"{self.name}_{name}"))
        return self.sems[-1]

    def block(self):
        if Phase.used:
            self.nc.clear_and_free_semaphores(Phase.used)
            Phase.used = []
        return self.ctx.enter_context(self.nc.Block())


class Chain:

    def __init__(self, eng, sem, per=0):
        self.eng, self.sem, self.per, self.n, self.base = eng, sem, per, 0, 0

    def turn(self, i):
        self.base, self.n = i * self.per, 0

    def __call__(self, ins):
        self.n += 1
        ins.then_inc(self.sem, 1)
        self.eng.wait_ge(self.sem, self.base + self.n)

    def close(self):
        assert self.n == self.per, (self.n, self.per)


def bc(ap, axis, n):
    shape = list(ap.shape)
    new = ap.unsqueeze(axis)
    shape.insert(axis, n)
    return new.to_broadcast(shape)


def build_constants(nc, C):
    with Phase(nc, "const") as ph:
        s = ph.sem("made")
        block = ph.block()

        @block.gpsimd
        def _(pool):
            step = Chain(pool, s)
            step(pool.memset(C["ident"][:], 0.0))
            step(pool.affine_select(C["ident"][:], C["ident"][:], [[-1, P]], ALU.not_equal, 1.0,
                                    base=0, channel_multiplier=1))
            step(pool.memset(C["ones"][:], 1.0))
            step(pool.affine_select(C["tri"][:], C["ones"][:], [[1, P]], ALU.is_ge, 0.0,
                                    base=0, channel_multiplier=-1))
            step(pool.memset(C["half"][:], -0.5))
            view = C["blk"][:NS, :NS].rearrange("p (a t) -> p a t", t=TS)
            step(pool.memset(C["blk"][:], 1.0))
            step(pool.affine_select(view, view, [[-TS, NB], [0, TS]], ALU.is_ge, 0.0, base=0, channel_multiplier=1))
            step(pool.affine_select(view, view, [[TS, NB], [0, TS]], ALU.is_ge, 0.0, base=TS - 1,
                                    channel_multiplier=-1))
            step(pool.affine_select(C["blk_low"][:NS, :NS], C["blk"][:NS, :NS], [[-1, NS]], ALU.is_ge, 0.0, base=0,
                                    channel_multiplier=1))
            step(pool.affine_select(C["blk_tri"][:NS, :NS], C["blk"][:NS, :NS], [[1, NS]], ALU.is_ge, 0.0, base=0,
                                    channel_multiplier=-1))


def load_x(nc, C, x, xT):
    with Phase(nc, "ldx") as ph:
        xt = ph.sb("xt", [P, 2, D])
        pt = ph.ps("pt", [P, 2, KD, P])
        x_in = [ph.sem(f"x_in{b}") for b in range(2)]
        x_read, turned, stored = ph.sem("x_read"), ph.sem("turned"), ph.sem("stored")
        block = ph.block()

        @block.sync
        def _(sp):
            for i in range(NT + 1):
                rows = P if i < NT else NS
                if i >= 2:
                    sp.wait_ge(turned, i - 1)
                sp.dma_start(xt[:rows, i % 2, :], x[i * P:i * P + rows, :]).then_inc(x_in[i % 2], 16)

        @block.tensor
        def _(pe):
            for i in range(NT + 1):
                rows = P if i < NT else NS
                pe.wait_ge(x_in[i % 2], 16 * (i // 2 + 1))
                if i >= 2:
                    pe.wait_ge(stored, i - 1)
                for k in range(KD):
                    mm = pe.transpose(pt[:, i % 2, k, :rows], xt[:rows, i % 2, k * P:(k + 1) * P],
                                      C["ident"][:rows, :rows])
                mm.then_inc(turned, 1)

        @block.scalar
        def _(act):
            for i in range(NT + 1):
                rows = P if i < NT else NS
                act.wait_ge(turned, i + 1)
                act.copy(xT[:, :, i * P:i * P + rows], pt[:, i % 2, :, :rows]).then_inc(stored, 1)


def store_y(nc, C, xT, gain, y):
    with Phase(nc, "sty") as ph:
        pt = ph.ps("pt", [P, 2, KD, P])
        rows_sb = ph.sb("rows", [P, 2, D])
        junk = ph.sb("junk", [P, D])
        gb = ph.sb("gain_rows", [P, D])
        ss, ms, rstd = (ph.sb(n, [P, NT + 1]) for n in ("ss", "ms", "rstd"))
        gain_in, turned, squared, meaned, rooted, scaled, done = (
            ph.sem(n) for n in ("gain_in", "turned", "squared", "meaned", "rooted", "scaled", "done"))
        out = [ph.sem(f"out{b}") for b in range(2)]
        block = ph.block()
        N = NT + 1

        @block.sync
        def _(sp):
            sp.dma_start(gb[:], gain.unsqueeze(0).partition_broadcast(P)).then_inc(gain_in, 16)
            for i in range(N):
                rows = P if i < NT else NS
                sp.wait_ge(done, i + 1)
                sp.dma_start(y[i * P:i * P + rows, :], rows_sb[:rows, i % 2, :]).then_inc(out[i % 2], 16)
            sp.wait_ge(out[0], 16 * ((N + 1) // 2))
            sp.wait_ge(out[1], 16 * (N // 2))

        @block.tensor
        def _(pe):
            for i in range(N):
                rows = P if i < NT else NS
                if i >= 2:
                    pe.wait_ge(scaled, i - 1)
                for k in range(KD):
                    mm = pe.transpose(pt[:rows, i % 2, k, :], xT[:, k, i * P:i * P + rows], C["ident"][:])
                mm.then_inc(turned, 1)

        @block.scalar
        def _(act):
            for i in range(N):
                rows = P if i < NT else NS
                act.wait_ge(turned, i + 1)
                if i:
                    act.wait_ge(squared, i)
                act.activation(junk[:rows, :], pt[:rows, i % 2].rearrange("p k t -> p (k t)"), ACT.Square,
                               accum_out=ss[:rows, i:i + 1]).then_inc(squared, 1)
                act.wait_ge(rooted, i + 1)
                if i >= 2:
                    act.wait_ge(out[i % 2], 16 * (i // 2))
                act.activation(rows_sb[:rows, i % 2, :], pt[:rows, i % 2].rearrange("p k t -> p (k t)"),
                               ACT.Copy, scale=rstd[:rows, i:i + 1]).then_inc(scaled, 1)

        @block.gpsimd
        def _(pool):
            for i in range(N):
                rows = P if i < NT else NS
                pool.wait_ge(meaned, i + 1)
                pool.tensor_tensor(rstd[:rows, i:i + 1], ms[:rows, i:i + 1], C["half"][:rows, 0:1],
                                   ALU.pow).then_inc(rooted, 1)

        @block.vector
        def _(dve):
            dve.wait_ge(gain_in, 16)
            for i in range(N):
                rows = P if i < NT else NS
                dve.wait_ge(squared, i + 1)
                dve.tensor_scalar(ms[:rows, i:i + 1], ss[:rows, i:i + 1], 1.0 / D, EPS, ALU.mult,
                                  ALU.add).then_inc(meaned, 1)
                dve.wait_ge(scaled, i + 1)
                dve.tensor_tensor(rows_sb[:rows, i % 2, :], rows_sb[:rows, i % 2, :], gb[:rows, :],
                                  ALU.mult).then_inc(done, 1)


def norm(nc, C, name, xT, gain, xh, xl):
    with Phase(nc, name) as ph:
        sq = ph.sb("sq", [P, 2, KD, GW])
        xn = ph.sb("xn", [P, KD, GW])
        ms = ph.sb("ms", [P, 2, GW])
        rstd = ph.sb("rstd", [P, 2, GW])
        g = ph.sb("g", [P, KD])
        half = ph.sb("half", [P, GW])
        sums = [ph.ps(f"sum{b}", [P, 512]) for b in range(2)]
        (g_in, half_set, squared, summed, meaned, rooted, normed, high, low) = (
            ph.sem(n) for n in ("g_in", "half_set", "squared", "summed", "meaned", "rooted", "normed",
                                "high", "low"))
        block = ph.block()

        @block.sync
        def _(sp):
            with nc.allow_non_contiguous_dma(reason="a gain per partition"):
                sp.dma_start(g[:], gain.rearrange("(k p) -> p k", p=P)).then_inc(g_in, 16)

        @block.scalar
        def _(act):
            def square(i):
                c0, w = GROUPS[i]
                if i >= 2:
                    act.wait_ge(summed, i - 1)
                act.activation(sq[:, i % 2, :, :w], xT[:, :, c0:c0 + w], ACT.Square).then_inc(squared, 1)
            square(0)
            for i, (c0, w) in enumerate(GROUPS):
                if i + 1 < len(GROUPS):
                    square(i + 1)
                act.wait_ge(normed, i + 1)
                act.copy(xh[:, :, c0:c0 + w], xn[:, :, :w]).then_inc(high, 1)

        @block.tensor
        def _(pe):
            for i, (c0, w) in enumerate(GROUPS):
                pe.wait_ge(squared, i + 1)
                if i >= 2:
                    pe.wait_ge(meaned, i - 1)
                for k in range(KD):
                    mm = pe.matmul(sums[i % 2][:, :w], C["ones"][:], sq[:, i % 2, k, :w], start=(k == 0),
                                   stop=(k == KD - 1))
                mm.then_inc(summed, 1)

        @block.gpsimd
        def _(pool):
            pool.memset(half[:], -0.5).then_inc(half_set, 1)
            pool.wait_ge(half_set, 1)
            for i, (c0, w) in enumerate(GROUPS):
                pool.wait_ge(meaned, i + 1)
                pool.tensor_tensor(rstd[:, i % 2, :w], ms[:, i % 2, :w], half[:, :w], ALU.pow).then_inc(rooted, 1)

        @block.vector
        def _(dve):
            dve.wait_ge(g_in, 16)
            for i, (c0, w) in enumerate(GROUPS):
                dve.wait_ge(summed, i + 1)
                dve.tensor_scalar(ms[:, i % 2, :w], sums[i % 2][:, :w], 1.0 / D, EPS, ALU.mult,
                                  ALU.add).then_inc(meaned, 1)
                dve.wait_ge(rooted, i + 1)
                for k in range(KD):
                    ins = dve.scalar_tensor_tensor(xn[:, k, :w], xT[:, k, c0:c0 + w], g[:, k:k + 1],
                                                   rstd[:, i % 2, :w], ALU.mult, ALU.mult)
                ins.then_inc(normed, 1)
                dve.wait_ge(high, i + 1)
                dve.tensor_tensor(xl[:, :, c0:c0 + w], xn[:, :, :w], xh[:, :, c0:c0 + w],
                                  ALU.subtract).then_inc(low, 1)
                dve.wait_ge(low, i + 1)


def split_all(nc, name, srcs, xh, xl):
    with Phase(nc, name) as ph:
        high = ph.sem("high")
        block = ph.block()
        tiles = [src[:, k, :] for src in srcs for k in range(KD // len(srcs))]

        @block.scalar
        def _(act):
            for k in range(KD):
                act.copy(xh[:, k, :], tiles[k]).then_inc(high, 1)

        @block.vector
        def _(dve):
            for k in range(KD):
                dve.wait_ge(high, k + 1)
                dve.tensor_tensor(xl[:, k, :], tiles[k], xh[:, k, :], ALU.subtract)


def project_rows(nc, name, xh, xl, w, col0, cw, n, dst, dst0, func=None):
    with Phase(nc, name) as ph:
        loops, ragged = divmod(n, 2)
        NBUF, NACC = 2, 3
        ws = ph.sb("ws", [P, KD, cw])
        wh = ph.sb("wh", [P, NBUF, KD, cw], F32R)
        wl = ph.sb("wl", [P, NBUF, KD, cw], F32R)
        o = ph.sb("o", [P, NACC, cw])
        acc = [ph.ps(f"acc{b}", [P, 512]) for b in range(NACC)]
        w_in = ph.sem("w_in")
        high, low, summed, evicted, pace = (ph.sem(s) for s in ("high", "low", "summed", "evicted", "pace"))
        out = [ph.sem(f"out{b}") for b in range(NACC)]
        block = ph.block()
        wv = w.rearrange("(k p) c -> p k c", p=P)
        N = NT + 1

        def chunks(eng, body):
            if loops > 1:
                with eng.Fori(0, loops) as j:
                    for b in range(2):
                        body(j * 2 + b, b, j)
            elif loops:
                body(0, 0, 0)
                body(1, 1, 0)
            if ragged:
                body(n - 1, 0, loops)

        @block.sync
        def _(sp):
            def body(c, b, j):
                sp.wait_ge(low, c + 1)
                sp.dma_start(ws[:], wv[:, :, bass.ds(c * cw + col0, cw)]).then_inc(w_in, 16)
            chunks(sp, body)

        @block.gpsimd
        def _(pool):
            pool.sem_inc(low, 1)

            def body(c, b, j):
                pool.wait_ge(w_in, c * 16 + 16)
                pool.wait_ge(summed, c * N + N)
                pool.sem_inc(pace, 1)
                pool.tensor_copy(wh[:, b], ws[:]).then_inc(high, 1)
                pool.wait_ge(high, c + 1)
                pool.tensor_tensor(wl[:, b], ws[:], wh[:, b], ALU.subtract).then_inc(low, 1)
            chunks(pool, body)

        @block.tensor
        def _(pe):
            pe.sem_inc(summed, NBUF * N)

            def body(c, b, j):
                pe.wait_ge(low, c + 2)
                for t in range(N):
                    rows = P if t < NT else NS
                    cols = slice(t * P, t * P + rows)
                    ps = acc[t % NACC][:rows, :cw]
                    pe.wait_ge(evicted, c * N + (t + 1))
                    for k in range(KD):
                        pe.matmul(ps, xh[:, k, cols], wh[:, b, k], start=(k == 0), stop=False)
                        pe.matmul(ps, xh[:, k, cols], wl[:, b, k], start=False, stop=False)
                        mm = pe.matmul(ps, xl[:, k, cols], wh[:, b, k], start=False, stop=(k == KD - 1))
                    mm.then_inc(summed, 1)
            chunks(pe, body)

        def free_buffers(eng):
            eng.sem_inc(evicted, NACC)
            for b in range(NACC):
                eng.sem_inc(out[b], 16)

        def evict(eng, c, t):
            rows = P if t < NT else NS
            eng.wait_ge(summed, c * N + (NBUF * N + t + 1))
            eng.wait_ge(out[t % NACC], c * (16 * N // NACC) + (16 * (t // NACC) + 16))
            dst_, src = o[:rows, t % NACC, :], acc[t % NACC][:rows, :cw]
            ins = eng.activation(dst_, src, func) if func else eng.tensor_copy(dst_, src)
            ins.then_inc(evicted, 1)

        @block.vector
        def _(dve):
            if func:
                return
            free_buffers(dve)

            def body(c, b, j):
                for t in range(N):
                    evict(dve, c, t)
            chunks(dve, body)

        @block.scalar
        def _(act):
            if func:
                free_buffers(act)

            def body(c, b, j):
                for t in range(N):
                    rows = P if t < NT else NS
                    if func:
                        evict(act, c, t)
                    act.wait_ge(evicted, c * N + (NACC + t + 1))
                    act.dma_start(dst[t * P:t * P + rows, bass.ds(c * cw + dst0, cw)],
                                  o[:rows, t % NACC, :]).then_inc(out[t % NACC], 16)
            chunks(act, body)
            for b in range(NACC):
                act.wait_ge(out[b], 16 * N // NACC * n + 16)


def project_back(nc, name, mh, ml, w, xT):
    with Phase(nc, name) as ph:
        G = len(GROUPS)
        ws = ph.sb("ws", [P, 2, KD, P])
        wh = ph.sb("wh", [P, 2, KD, P], F32R)
        wl = ph.sb("wl", [P, 2, KD, P], F32R)
        acc = [ph.ps(f"acc{b}", [P, 512]) for b in range(2 * G)]
        w_in = [ph.sem(f"w_in{b}") for b in range(2)]
        high, low, summed, added, pace = (ph.sem(n) for n in ("high", "low", "summed", "added", "pace"))
        block = ph.block()
        wv = w.rearrange("(k p) c -> p k c", p=P)

        def tiles(eng, body):
            with eng.Fori(0, KD // 2) as j:
                for b in range(2):
                    body(j * 2 + b, b, j)

        @block.sync
        def _(sp):
            def body(c, b, j):
                sp.wait_ge(low, c + 1)
                sp.dma_start(ws[:, b], wv[:, :, bass.ds(c * P, P)]).then_inc(w_in[b], 16)
            tiles(sp, body)

        @block.gpsimd
        def _(pool):
            pool.sem_inc(low, 2)

            def body(c, b, j):
                pool.wait_ge(w_in[b], j * 16 + 16)
                pool.wait_ge(summed, c * G + G)
                pool.sem_inc(pace, 1)
                pool.tensor_copy(wh[:, b], ws[:, b]).then_inc(high, 1)
                pool.wait_ge(high, c + 1)
                pool.tensor_tensor(wl[:, b], ws[:, b], wh[:, b], ALU.subtract).then_inc(low, 1)
            tiles(pool, body)

        @block.tensor
        def _(pe):
            pe.sem_inc(summed, 2 * G)

            def body(c, b, j):
                pe.wait_ge(low, c + 3)
                for g, (c0, w_) in enumerate(GROUPS):
                    pe.wait_ge(added, c * G + (g + 1))
                    ps = acc[G * b + g][:, :w_]
                    for k in range(KD):
                        pe.matmul(ps, wh[:, b, k], mh[:, k, c0:c0 + w_], start=(k == 0), stop=False)
                        pe.matmul(ps, wh[:, b, k], ml[:, k, c0:c0 + w_], start=False, stop=False)
                        mm = pe.matmul(ps, wl[:, b, k], mh[:, k, c0:c0 + w_], start=False, stop=(k == KD - 1))
                    mm.then_inc(summed, 1)
            tiles(pe, body)

        @block.vector
        def _(dve):
            dve.sem_inc(added, 2 * G)

            def body(c, b, j):
                for g, (c0, w_) in enumerate(GROUPS):
                    dve.wait_ge(summed, c * G + (2 * G + g + 1))
                    x = xT[:, bass.ds(c, 1), c0:c0 + w_].rearrange("p o t -> p (o t)")
                    dve.tensor_tensor(x, acc[G * b + g][:, :w_], x, ALU.add).then_inc(added, 1)
            tiles(dve, body)


def load_prev(nc, C, name, state, n_tiles, T1, prev, conv_w, taps, cw_sb, conv_b):
    rows = NB * T1
    with Phase(nc, name) as ph:
        st = ph.sb("st", [rows, n_tiles * P])
        wr = ph.sb("wr", [taps + 1, n_tiles * P])
        pp = ph.ps("pp", [P, 2048])
        pw = ph.ps("pw", [P, 512])
        got, turned, copied = ph.sem("got"), ph.sem("turned"), ph.sem("copied")
        block = ph.block()
        per = 512 // rows
        nw = taps + (1 if conv_b is not None else 0)
        assert n_tiles * nw <= 512 and (n_tiles + per - 1) // per <= 4

        @block.sync
        def _(sp):
            sp.dma_start(st[:], state.rearrange("b r f -> (b r) f")).then_inc(got, 16)
            sp.dma_start(wr[:taps, :], conv_w).then_inc(got, 16)
            if conv_b is not None:
                sp.dma_start(wr[taps:taps + 1, :], conv_b.unsqueeze(0)).then_inc(got, 16)

        @block.tensor
        def _(pe):
            pe.wait_ge(got, 16 * (3 if conv_b is not None else 2))
            for f in range(n_tiles):
                at = f // per * 512 + f % per * rows
                pe.transpose(pp[:, at:at + rows], st[:, f * P:(f + 1) * P], C["ident"][:rows, :rows])
                mm = pe.transpose(pw[:, f * nw:f * nw + nw], wr[:nw, f * P:(f + 1) * P],
                                  C["ident"][:nw, :nw])
            mm.then_inc(turned, 1)

        @block.scalar
        def _(act):
            act.wait_ge(turned, 1)
            for f0 in range(0, n_tiles, per):
                m = min(per, n_tiles - f0)
                at = f0 // per * 512
                act.copy(prev[:, f0:f0 + m, :], pp[:, at:at + m * rows].rearrange("p (f r) -> p f r", r=rows))
            pwv = pw[:, :n_tiles * nw].rearrange("p (f r) -> p f r", r=nw)
            act.copy(cw_sb[:], pwv)


def store_tail(nc, C, name, tail, n_tiles, T1, new_p, new_s):
    rows = T1 * (1 + NB)
    with Phase(nc, name) as ph:
        tr = ph.sb("tr", [rows, n_tiles * P])
        pt = [ph.ps(f"pt{b}", [P, 512]) for b in range(2)]
        turned, copied, out = ph.sem("turned"), ph.sem("copied"), ph.sem("out")
        block = ph.block()
        n4 = n_tiles // 4

        @block.tensor
        def _(pe):
            for q in range(n4):
                if q >= 2:
                    pe.wait_ge(copied, q - 1)
                for f in range(4):
                    mm = pe.transpose(pt[q % 2][:rows, f * P:(f + 1) * P], tail[:, 4 * q + f, :], C["ident"][:])
                mm.then_inc(turned, 1)

        @block.scalar
        def _(act):
            for q in range(n4):
                act.wait_ge(turned, q + 1)
                act.copy(tr[:, q * 512:(q + 1) * 512], pt[q % 2][:rows, :]).then_inc(copied, 1)

        @block.sync
        def _(sp):
            sp.wait_ge(copied, n4)
            sp.dma_start(new_p, tr[:T1, :]).then_inc(out, 16)
            sp.dma_start(new_s.rearrange("b r f -> (b r) f"), tr[T1:, :]).then_inc(out, 16)
            sp.wait_ge(out, 32)


def conv_up(nc, C, name, xh, xl, w, taps, cw_sb, prev, tail, dst=None, wd=None, xT=None):
    ffn = wd is not None
    T1 = taps - 1
    turns = (NF if ffn else GDN_QKV // P) // 2
    slots = [(s, half) for s in range(2) for half in range(2 if ffn else 1)]
    R = len(slots)
    SW = T1 + TS
    G = len(GROUPS)
    nw = taps + (1 if ffn else 0)
    with Phase(nc, name) as ph:
        ws = ph.sb("ws", [P, 2, KD, P])
        wh = ph.sb("wh", [P, 2, KD, P], F32R)
        wl = ph.sb("wl", [P, 2, KD, P], F32R)
        hp = ph.sb("hp", [P, 2, T1 + SEQ])
        hs = ph.sb("hs", [P, 2, NB, SW])
        cur = ph.sb("cur", [P, 2, nw])
        conv = ph.sb("conv", [P, 2, NTOK])
        zero = ph.sb("zero", [P, 1])
        if ffn:
            gate = ph.sb("gate", [P, NTOK])
            gh = ph.sb("gh", [P, 2, NTOK], F32R)
            gl = ph.sb("gl", [P, 2, NTOK], F32R)
            ds = ph.sb("ds", [P, 2, D])
            dh = ph.sb("dh", [P, 2, D], F32R)
            dl = ph.sb("dl", [P, 2, D], F32R)
        acc = [ph.ps(f"acc{b}", [P, 512]) for b in range(2 * G)]
        dn = [ph.ps(f"dn{b}", [P, 512]) for b in range(2)]
        w_in = [ph.sem(f"w_in{b}") for b in range(2)]
        out = [ph.sem(f"out{b}") for b in range(2)]
        (high, low, staged, summed, evicted, tap0, tapped, silued, gated, g_high, g_low, d_in, d_high, d_low,
         down, added, zeroed, pace, step_sem) = (ph.sem(s) for s in (
             "high", "low", "staged", "summed", "evicted", "tap0", "tapped", "silued", "gated", "g_high", "g_low",
             "d_in", "d_high", "d_low", "down", "added", "zeroed", "pace", "tap_step"))
        block = ph.block()
        wv = w.rearrange("(k p) c -> p k c", p=P)

        def turned_loop(eng, body):
            body(0, True)
            with eng.Fori(1, turns) as i:
                body(i, False)

        @block.sync
        def _(sp):
            def body(i, first):
                for r, (s, half) in enumerate(slots):
                    sp.wait_ge(low, i * R + (r + 1))
                    sp.dma_start(ws[:, r % 2], wv[:, :, bass.ds(i * (2 * P) + (s * P + half * D_FF), P)])\
                        .then_inc(w_in[r % 2], 16)
                if ffn:
                    sp.wait_ge(d_low, i + 1)
                    sp.dma_start(ds[:], wd[bass.ds(i * (2 * P), 2 * P), :].rearrange("(s p) c -> p s c", p=P))\
                        .then_inc(d_in, 16)
            turned_loop(sp, body)

        @block.gpsimd
        def _(pool):
            pool.sem_inc(low, 2)
            pool.sem_inc(d_low, 1)
            pool.memset(hp[:, :, 0:T1], 0.0).then_inc(zeroed, 1)

            def body(i, first):
                for r, (s, half) in enumerate(slots):
                    b = r % 2
                    pool.wait_ge(w_in[b], i * (8 * R) + (16 * (r // 2) + 16))
                    pool.wait_ge(summed, i * (R * G) + (r + 1) * G)
                    pool.sem_inc(pace, 1)
                    pool.tensor_copy(wh[:, b], ws[:, b]).then_inc(high, 1)
                    pool.wait_ge(high, i * R + (r + 1))
                    pool.tensor_tensor(wl[:, b], ws[:, b], wh[:, b], ALU.subtract).then_inc(low, 1)
                    pool.wait_ge(tapped, i * R + (r + 1))
                    pool.sem_inc(pace, 1)
                    tile = bass.ds(i * 2 + (s + half * NF), 1)
                    pool.tensor_copy(cur[:, b:b + 1, :], cw_sb[:, tile, :])
                    pool.tensor_copy(hs[:, b:b + 1, :, 0:T1], prev[:, tile, :].rearrange(
                        "p o (b r) -> p o b r", r=T1)).then_inc(staged, 1)
                if ffn:
                    pool.wait_ge(d_in, i * 16 + 16)
                    if not first:
                        pool.wait_ge(down, i * (KD * G))
                    pool.sem_inc(pace, 1)
                    pool.tensor_copy(dh[:], ds[:]).then_inc(d_high, 1)
                    pool.wait_ge(d_high, i + 1)
                    pool.tensor_tensor(dl[:], ds[:], dh[:], ALU.subtract).then_inc(d_low, 1)
            turned_loop(pool, body)

        @block.tensor
        def _(pe):
            pe.sem_inc(summed, 2 * G)

            def up(i, r):
                b = r % 2
                pe.wait_ge(low, i * R + (r + 3))
                for g, (c0, w_) in enumerate(GROUPS):
                    pe.wait_ge(evicted, i * (R * G) + (r * G + g + 1))
                    ps = acc[G * b + g][:, :w_]
                    for k in range(KD):
                        pe.matmul(ps, wh[:, b, k], xh[:, k, c0:c0 + w_], start=(k == 0), stop=False)
                        pe.matmul(ps, wh[:, b, k], xl[:, k, c0:c0 + w_], start=False, stop=False)
                        mm = pe.matmul(ps, wl[:, b, k], xh[:, k, c0:c0 + w_], start=False, stop=(k == KD - 1))
                    mm.then_inc(summed, 1)

            def down_products(i):
                pe.wait_ge(d_low, i + 2)
                pe.wait_ge(g_low, i * 2 + 2)
                for t in range(KD):
                    for g, (c0, w_) in enumerate(GROUPS):
                        m = t * G + g
                        pe.wait_ge(added, i * (KD * G) + (m + 1))
                        ps = dn[m % 2][:, :w_]
                        for s in range(2):
                            cols = slice(t * P, (t + 1) * P)
                            pe.matmul(ps, dh[:, s, cols], gh[:, s, c0:c0 + w_], start=(s == 0), stop=False)
                            pe.matmul(ps, dh[:, s, cols], gl[:, s, c0:c0 + w_], start=False, stop=False)
                            mm = pe.matmul(ps, dl[:, s, cols], gh[:, s, c0:c0 + w_], start=False, stop=(s == 1))
                        mm.then_inc(down, 1)

            def body(i, first):
                for r in range(R):
                    if ffn and r == 2 and not first:
                        down_products(i - 1)
                    up(i, r)
            turned_loop(pe, body)
            if ffn:
                down_products(turns - 1)

        @block.scalar
        def _(act):
            act.sem_inc(evicted, 2 * G)
            for b in range(2):
                act.sem_inc(out[b], 16)
            act.wait_ge(zeroed, 1)

            def body(i, first):
                for r, (s, half) in enumerate(slots):
                    b = r % 2
                    act.wait_ge(tapped, i * R + (r + 1))
                    for g, (c0, w_) in enumerate(GROUPS):
                        act.wait_ge(summed, i * (R * G) + (2 * G + r * G + g + 1))
                        wp = min(w_, SEQ - c0)
                        ins = act.copy(hp[:, b, T1 + c0:T1 + c0 + wp], acc[G * b + g][:, :wp])
                        if wp < w_:
                            ins = act.copy(hs[:, b, :, T1:], acc[G * b + g][:, wp:w_].rearrange(
                                "p (b t) -> p b t", t=TS))
                        ins.then_inc(evicted, 1)
                    act.wait_ge(evicted, i * (R * G) + (2 * G + (r + 1) * G))
                    act.wait_ge(staged, i * R + (r + 1))
                    if ffn:
                        act.wait_ge(gated, i * 2 + (s + 1))
                    else:
                        act.wait_ge(out[b], i * 16 + 16)
                    bias = cur[:, b, taps:taps + 1] if ffn else 0.0
                    act.activation(conv[:, b, 0:SEQ], hp[:, b, 0:SEQ], ACT.Identity, bias=bias,
                                   scale=cur[:, b, 0:1])
                    act.activation(conv[:, b, SEQ:].rearrange("p (b t) -> p b t", t=TS), hs[:, b, :, 0:TS],
                                   ACT.Identity, bias=bias, scale=cur[:, b, 0:1]).then_inc(tap0, 1)
                    if not ffn:
                        act.wait_ge(tapped, i * R + (r + 3))
                        act.activation(conv[:, b, :], conv[:, b, :], ACT.Silu).then_inc(silued, 1)
                        act.wait_ge(silued, i * R + (r + 1))
                        act.dma_start(dst[bass.ds(i * 2 + r, 1), :, :].rearrange("o p t -> p (o t)"),
                                      conv[:, b, :]).then_inc(out[b], 16)
                    elif half:
                        act.wait_ge(tapped, i * R + (r + 3))
                        act.activation(gate[:], conv[:, 1, :], ACT.Silu).then_inc(silued, 1)
                        act.wait_ge(gated, i * 2 + (s + 2))
                        if not first:
                            act.wait_ge(down, i * (KD * G))
                        act.copy(gh[:, s, :], gate[:]).then_inc(g_high, 1)
            turned_loop(act, body)
            if not ffn:
                for b in range(2):
                    act.wait_ge(out[b], 16 * turns + 16)

        @block.vector
        def _(dve):
            dve.sem_inc(tapped, 2)
            if ffn:
                dve.sem_inc(gated, 1)
                dve.sem_inc(added, 2)
            step = Chain(dve, step_sem, per=R * (T1 - 1))

            def taps_of(i, r, s, half):
                b = r % 2
                dve.wait_ge(tap0, i * R + (r + 1))
                tile = bass.ds(i * 2 + (s + half * NF), 1)
                dve.tensor_copy(tail[:, tile, 0:T1], hp[:, b:b + 1, SEQ:SEQ + T1])
                dve.tensor_copy(tail[:, tile, T1:].rearrange("p o (b r) -> p o b r", r=T1),
                                hs[:, b:b + 1, :, TS:TS + T1])
                cp, cs = conv[:, b, 0:SEQ], conv[:, b, SEQ:].rearrange("p (b t) -> p b t", t=TS)
                for j in range(1, taps):
                    dve.scalar_tensor_tensor(cp, hp[:, b, j:j + SEQ], cur[:, b, j:j + 1], cp, ALU.mult, ALU.add)
                    ins = dve.scalar_tensor_tensor(cs, hs[:, b, :, j:j + TS], cur[:, b, j:j + 1], cs,
                                                   ALU.mult, ALU.add)
                    if j < taps - 1:
                        step(ins)
                ins.then_inc(tapped, 1)

            def add_down(i):
                for m in range(KD * G):
                    t, g = divmod(m, G)
                    c0, w_ = GROUPS[g]
                    dve.wait_ge(down, i * (KD * G) + (m + 1))
                    dve.tensor_tensor(xT[:, t, c0:c0 + w_], dn[m % 2][:, :w_], xT[:, t, c0:c0 + w_],
                                      ALU.add).then_inc(added, 1)

            def body(i, first):
                step.turn(i)
                for r, (s, half) in enumerate(slots):
                    if ffn and r == 1 and not first:
                        add_down(i - 1)
                    taps_of(i, r, s, half)
                    if half:
                        dve.wait_ge(silued, i * 2 + (s + 1))
                        if s or not first:
                            dve.wait_ge(g_low, i * 2 + s)
                        dve.tensor_tensor(gate[:], gate[:], conv[:, 0, :], ALU.mult).then_inc(gated, 1)
                        dve.wait_ge(g_high, i * 2 + (s + 1))
                        dve.tensor_tensor(gl[:, s, :], gate[:], gh[:, s, :], ALU.subtract).then_inc(g_low, 1)
                step.close()
            turned_loop(dve, body)
            if ffn:
                add_down(turns - 1)


def fox_prep(nc, C, p, q_gain, k_gain, b_f, qkA, sog, qTs, kTs, lfs, fk, fv, flf):
    A = DH + 2
    with Phase(nc, "fxp") as ph:
        pf = ph.sb("pf", [P, 2, FOX_COLS])
        gains = ph.sb("gains", [P, 2, DH])
        bf = ph.sb("bf", [P, H])
        sq = ph.sb("sq", [P, 2 * H * DH])
        ss, ms, rstd = (ph.sb(n, [P, 2 * H]) for n in ("ss", "ms", "rstd"))
        fl, nab, e1, l1, lf, lfsum = (ph.sb(n, [P, H]) for n in ("fl", "nab", "e1", "l1", "lf", "lfsum"))
        qa = ph.sb("qa", [P, 2 * H, A])
        qs = ph.sb("qs", [P, 2 * H, DH])
        ps = ph.ps("ps", [P, 4, 4, P])
        psF = ph.ps("psF", [P, 512])
        pf_in = [ph.sem(f"pf_in{b}") for b in range(2)]
        (params_in, fv_out, meaned, rooted, scaled, gained, nabbed, logged, lf_done, summed, filled, turned, stored_a, stored_d, outs, e1_done) = (ph.sem(s) for s in (
             "params_in", "fv_out", "meaned", "rooted", "scaled", "gained", "nabbed", "logged", "lf_done", "summed",
             "filled", "turned", "stored_a", "stored_d", "outs", "e1_done"))
        dve_step = ph.sem("dve_step")
        block = ph.block()

        def rows_of(i):
            return P if i < NT else NS

        @block.sync
        def _(sp):
            sp.dma_start(gains[:, 0, :], q_gain.partition_broadcast(P)).then_inc(params_in, 16)
            sp.dma_start(gains[:, 1, :], k_gain.partition_broadcast(P)).then_inc(params_in, 16)
            sp.dma_start(bf[:], b_f.partition_broadcast(P)).then_inc(params_in, 16)
            for i in range(NT + 1):
                r = rows_of(i)
                if i >= 2:
                    sp.wait_ge(scaled, i - 1)
                sp.dma_start(pf[:r, i % 2, :], p[i * P:i * P + r, 0:FOX_COLS]).then_inc(pf_in[i % 2], 16)
            sp.dma_start(fv, p[:, 2 * FOX_W:3 * FOX_W]).then_inc(fv_out, 16)
            sp.dma_start(sog[:, 0:NT, :], p[0:SEQ, 3 * FOX_W:4 * FOX_W].rearrange("(n p) c -> p n c", p=P))\
                .then_inc(fv_out, 16)
            sp.dma_start(sog[:NS, NT, :], p[SEQ:, 3 * FOX_W:4 * FOX_W]).then_inc(fv_out, 16)
            sp.wait_ge(fv_out, 48)

        @block.gpsimd
        def _(pool):
            pool.wait_ge(params_in, 48)
            pool.tensor_scalar(gains[:, 0, :], gains[:, 0, :], DH ** -0.5, None, ALU.mult).then_inc(params_in, 1)
            pool.wait_ge(params_in, 49)
            for i in range(NT + 1):
                r = rows_of(i)
                pool.wait_ge(meaned, i + 1)
                pool.tensor_tensor(rstd[:r], ms[:r], C["half"][:r, :2 * H], ALU.pow).then_inc(rooted, 1)
                pool.wait_ge(scaled, i + 1)
                for n in range(2):
                    t = (qa if i < NT else qs)[:r, n * H:(n + 1) * H, 0:DH]
                    ins = pool.tensor_tensor(t, t, bc(gains[:r, n, :], 1, H), ALU.mult)
                ins.then_inc(gained, 1)

        @block.scalar
        def _(act):
            for i in range(NT + 1):
                r = rows_of(i)
                b = i % 2
                act.wait_ge(nabbed, i + 1)
                act.activation(e1[:r], nab[:r], ACT.Exp).then_inc(e1_done, 1)
                act.wait_ge(e1_done, i + 1)
                act.activation(l1[:r], e1[:r], ACT.Ln, bias=1.0).then_inc(logged, 1)
                act.wait_ge(turned, i + 1)
                if i < NT:
                    ins = act.copy(qkA[:A, 0:8, i * P:(i + 1) * P], ps[:A, 0:2].rearrange("p a b t -> p (a b) t"))
                else:
                    ins = act.copy(qTs[:], ps[:, 0, :, :NS])
                ins.then_inc(stored_a, 1)
                act.dma_start(fk[i * P:i * P + r, :].rearrange("t (h d) -> t h d", d=DH),
                              (qa if i < NT else qs)[:r, H:, 0:DH]).then_inc(outs, 16)
                act.dma_start(flf[i * P:i * P + r, :], lf[:r]).then_inc(outs, 16)
            act.wait_ge(outs, 32 * (NT + 1))

        @block.tensor
        def _(pe):
            for i in range(NT + 1):
                r = rows_of(i)
                if i < NT:
                    pe.wait_ge(lf_done, i + 1)
                    pe.matmul(psF[:, :H], C["tri"][:], lf[:], start=True, stop=False)
                    pe.matmul(psF[:, :H], C["ones"][:], lfsum[:], start=False, stop=True).then_inc(summed, 1)
                pe.wait_ge(filled, i + 1)
                pe.wait_ge(gained, i + 1)
                if i:
                    pe.wait_ge(stored_a, i)
                    pe.wait_ge(stored_d, i)
                if i < NT:
                    for n in range(2 * H):
                        mm = pe.transpose(ps[:A, n // 4, n % 4, :], qa[:, n, :], C["ident"][:])
                else:
                    for n in range(H):
                        mm = pe.transpose(ps[:, n // 4, n % 4, :NS],
                                          qs[:NS, 2 * n:2 * n + 2, :].rearrange("p a d -> p (a d)"),
                                          C["ident"][:NS, :NS])
                mm.then_inc(turned, 1)

        @block.vector
        def _(dve):
            step = Chain(dve, dve_step)
            step(dve.memset(lfsum[:], 0.0))
            dve.memset(qa[:], 1.0).then_inc(dve_step, 1)
            step.n += 1
            dve.wait_ge(dve_step, step.n)
            dve.wait_ge(params_in, 49)
            for i in range(NT + 1):
                r = rows_of(i)
                b = i % 2
                dve.wait_ge(pf_in[b], 16 * (i // 2 + 1))
                if i:
                    dve.wait_ge(outs, 32 * i)
                step(dve.tensor_tensor(fl[:r], pf[:r, b, 4 * FOX_W:], bf[:r], ALU.add))
                dve.scalar_tensor_tensor(nab[:r], fl[:r], -1.0, fl[:r], ALU.mult, ALU.min).then_inc(nabbed, 1)
                step(dve.tensor_tensor(sq[:r], pf[:r, b, 0:2 * FOX_W], pf[:r, b, 0:2 * FOX_W], ALU.mult))
                step(dve.tensor_reduce(ss[:r], sq[:r].rearrange("p (h d) -> p h d", d=DH), AX.X, ALU.add))
                dve.tensor_scalar(ms[:r], ss[:r], 1.0 / DH, EPS, ALU.mult, ALU.add).then_inc(meaned, 1)
                dve.wait_ge(logged, i + 1)
                if i < NT:
                    dve.scalar_tensor_tensor(lf[:], fl[:], 0.0, l1[:], ALU.min, ALU.subtract).then_inc(lf_done, 1)
                else:
                    step(dve.scalar_tensor_tensor(lf[:r], fl[:r], 0.0, l1[:r], ALU.min, ALU.subtract))
                    dve.tensor_copy(lfs[:], lf[:r])
                dve.wait_ge(rooted, i + 1)
                if i:
                    dve.wait_ge(turned, i)
                dst = qa if i < NT else qs
                dve.tensor_tensor(dst[:r, :, 0:DH], pf[:r, b, 0:2 * FOX_W].rearrange("p (h d) -> p h d", d=DH),
                                  bc(rstd[:r], 2, DH), ALU.mult).then_inc(scaled, 1)
                if i < NT:
                    dve.wait_ge(summed, i + 1)
                    dve.tensor_copy(qa[:, 0:H, DH], psF[:, :H])
                    dve.tensor_scalar(qa[:, H:, DH + 1], psF[:, :H], -1.0, None, ALU.mult)
                    step(dve.tensor_tensor(lfsum[:], lfsum[:], lf[:], ALU.add))
                dve.memset(ss[:r, 0:1], 0.0).then_inc(filled, 1)
                dve.wait_ge(turned, i + 1)
                if i < NT:
                    ins = dve.tensor_copy(qkA[:A, 8:16, i * P:(i + 1) * P], ps[:A, 2:4].rearrange(
                        "p a b t -> p (a b) t"))
                else:
                    ins = dve.tensor_copy(kTs[:], ps[:, 1, :, :NS])
                ins.then_inc(stored_d, 1)
                dve.wait_ge(stored_d, i + 1)


def fox_prompt(nc, C, qkA, sog, fv, mixT):
    A = DH + 2
    U = 2 * NT
    with Phase(nc, "fx") as ph:
        v = ph.sb("v", [P, NT, FOX_W])
        qh = ph.sb("qh", [P, 2, SEQ])
        kh = ph.sb("kh", [P, 2, SEQ])
        mask = ph.sb("mask", [P, P])
        pr = ph.sb("pr", [P, 2, SEQ])
        pT = ph.sb("pT", [P, 2, NT, P])
        o = ph.sb("o", [P, NT, 2, DH])
        vh = ph.sb("vh", [P, 2, NT, DH])
        mx, rs, ri = (ph.sb(n, [P, 2]) for n in ("mx", "rs", "ri"))
        S = [ph.ps(f"S{b}", [P, 2, 512]) for b in range(2)]
        psT = ph.ps("psT", [P, NT, P])
        psO = ph.ps("psO", [P, 512])
        psM = ph.ps("psM", [P, 4, P])
        (v_in, masked, staged, scored, maxed, expd, turned, copied, valued, rinv, gated, o_turned, mixed) = (
            ph.sem(s) for s in ("v_in", "masked", "staged", "scored", "maxed", "expd", "turned", "copied",
                                "valued", "rinv", "gated", "o_turned", "mixed"))
        block = ph.block()
        turns = H // 2

        @block.sync
        def _(sp):
            sp.dma_start(v[:], fv[0:SEQ, :].rearrange("(t p) c -> p t c", p=P)).then_inc(v_in, 16)

        @block.gpsimd
        def _(pool):
            pool.memset(mask[:], 0.0).then_inc(masked, 1)
            pool.wait_ge(masked, 1)
            pool.affine_select(mask[:], mask[:], [[-1, P]], ALU.is_ge, NEG, base=0,
                               channel_multiplier=1).then_inc(masked, 1)

        @block.tensor
        def _(pe):
            pe.sem_inc(scored, 2)
            pe.sem_inc(valued, 2)
            pe.sem_inc(o_turned, 2)
            pe.wait_ge(masked, 2)

            def score(i, u):
                hb, qt = divmod(u, NT)
                if qt == 0:
                    pe.wait_ge(staged, i * 2 + (hb + 1))
                pe.wait_ge(expd, i * U + (u + 1))
                L = (qt + 1) * P
                for c0 in range(0, L, 512):
                    w = min(512, L - c0)
                    diag = c0 + w == L
                    mm = pe.matmul(S[u % 2][:, c0 // 512, :w], qh[:A, hb, qt * P:(qt + 1) * P],
                                   kh[:A, hb, c0:c0 + w], start=True, stop=not diag)
                    if diag:
                        mm = pe.matmul(S[u % 2][:, c0 // 512, w - P:w], C["ident"][:], mask[:], start=False,
                                       stop=True)
                mm.then_inc(scored, 1)

            def body(i):
                score(i, 0)
                for u in range(U):
                    hb, qt = divmod(u, NT)
                    if u + 1 < U:
                        score(i, u + 1)
                    pe.wait_ge(expd, i * U + (u + 3))
                    pe.wait_ge(copied, i * U + (u + 1))
                    for kt in range(qt + 1):
                        mm = pe.transpose(psT[:, kt, :], pr[:, u % 2, kt * P:(kt + 1) * P], C["ident"][:])
                    mm.then_inc(turned, 1)
                    pe.wait_ge(copied, i * U + (u + 2))
                    pe.wait_ge(gated, i * U + (u + 1))
                    for kt in range(qt + 1):
                        mm = pe.matmul(psO[:, 0:DH], pT[:, u % 2, kt, :], vh[:, hb, kt, :], start=(kt == 0),
                                       stop=(kt == qt))
                    mm.then_inc(valued, 1)
                pe.wait_ge(gated, i * U + (U + 1))
                for half in range(2):
                    pe.wait_ge(mixed, i * 2 + (half + 1))
                    for t in range(4):
                        mm = pe.transpose(psM[:, t, :], o[:, half * 4 + t].rearrange("p h d -> p (h d)"),
                                          C["ident"][:])
                    mm.then_inc(o_turned, 1)
            with pe.Fori(0, turns) as i:
                body(i)

        @block.scalar
        def _(act):
            act.sem_inc(expd, 2)
            act.sem_inc(mixed, 1)

            def body(i):
                for u in range(U):
                    hb, qt = divmod(u, NT)
                    L = (qt + 1) * P
                    act.wait_ge(maxed, i * U + (u + 1))
                    act.activation(pr[:, u % 2, :L], S[u % 2].rearrange("p a b -> p (a b)")[:, :L], ACT.Exp,
                                   bias=mx[:, u % 2:u % 2 + 1], accum_out=rs[:, u % 2:u % 2 + 1])\
                        .then_inc(expd, 1)
                    act.wait_ge(turned, i * U + (u + 1))
                    act.wait_ge(valued, i * U + (u + 1))
                    act.copy(pT[:, u % 2, :qt + 1, :], psT[:, :qt + 1, :]).then_inc(copied, 1)
                for half in range(2):
                    act.wait_ge(o_turned, i * 2 + (half + 3))
                    act.copy(mixT[:, bass.ds(i, 1), half * 512:(half + 1) * 512].rearrange("p o t -> p (o t)"),
                             psM.rearrange("p a b -> p (a b)")).then_inc(mixed, 1)
            act.sem_inc(copied, 1)
            with act.Fori(0, turns) as i:
                body(i)

        @block.vector
        def _(dve):
            dve.sem_inc(gated, 1)
            dve.wait_ge(v_in, 16)

            def stage(i, hb):
                dve.wait_ge(valued, i * U + 2)
                h = i * 2 + hb
                dve.tensor_copy(qh[:A, hb:hb + 1, :], qkA[:A, bass.ds(h, 1), :])
                dve.tensor_copy(kh[:A, hb:hb + 1, :], qkA[:A, bass.ds(h + H, 1), :])
                dve.tensor_copy(vh[:, hb], v[:, :, bass.ds(h * DH, DH)]).then_inc(staged, 1)

            def body(i):
                stage(i, 0)
                stage(i, 1)
                for u in range(U):
                    hb, qt = divmod(u, NT)
                    L = (qt + 1) * P
                    b = u % 2
                    dve.wait_ge(scored, i * U + (u + 3))
                    dve.tensor_reduce(mx[:, b:b + 1], S[b].rearrange("p a b -> p (a b)")[:, :L], AX.X, ALU.max,
                                      negate=True).then_inc(maxed, 1)
                    if u:
                        finish(i, u - 1)
                finish(i, U - 1)

            def finish(i, u):
                hb, qt = divmod(u, NT)
                b = u % 2
                dve.wait_ge(expd, i * U + (u + 3))
                dve.reciprocal(ri[:, b:b + 1], rs[:, b:b + 1]).then_inc(rinv, 1)
                dve.wait_ge(rinv, i * U + (u + 1))
                dve.wait_ge(valued, i * U + (u + 3))
                if qt == 0 and hb == 0:
                    dve.wait_ge(o_turned, i * 2 + 2)
                dve.scalar_tensor_tensor(o[:, qt, hb, :], psO[:, 0:DH], ri[:, b:b + 1],
                                         sog[:, qt, bass.ds((i * 2 + hb) * DH, DH)], ALU.mult, ALU.mult)\
                    .then_inc(gated, 1)
            with dve.Fori(0, turns) as i:
                body(i)


def fox_sample(nc, C, qTs, kTs, lfs, sog, fv, pool_k, pool_v, pool_lf, page_table, mixT):
    HQ = H * TS
    NK = PAST + TS
    with Phase(nc, "fs") as ph:
        table = ph.sb("table", [1, NB * NPG], I32)
        kp = ph.sb("kp", [P, 2, NPG, FOX_W])
        vp = ph.sb("vp", [P, 2, NPG, FOX_W])
        lp = ph.sb("lp", [P, 2, NPG, H])
        vn = ph.sb("vn", [TS, 2, FOX_W])
        qx_all = ph.sb("qx_all", [P, NB, 4, HQ])
        qx = ph.sb("qx", [P, 4, HQ])
        kn = ph.sb("kn", [P, 4, TS])
        lx = ph.sb("lx", [P, NPG, H, TS])
        lnx = ph.sb("lnx", [NS, H, TS])
        sel = ph.sb("sel", [NS, TS])
        kT = ph.sb("kT", [P, 2, 4, P])
        ones_row = ph.sb("ones_row", [HQ, PAST])
        onehot = ph.sb("onehot", [HQ, TS])
        causal = ph.sb("causal", [HQ, TS])
        F = ph.sb("F", [HQ, NK])
        fq = ph.sb("fq", [HQ, 1])
        fqt = ph.sb("fqt", [HQ, TS])
        st = ph.sb("st", [HQ, NK])
        pr = ph.sb("pr", [HQ, NK])
        mx, rs, ri = (ph.sb(n, [HQ, 1]) for n in ("mx", "rs", "ri"))
        pT = ph.sb("pT", [P, NPG + 1, HQ])
        headmask = ph.sb("headmask", [HQ, H, DH])
        om = ph.sb("om", [HQ, FOX_W])
        red = ph.sb("red", [P, 4, NS])
        sgT = ph.sb("sgT", [P, 4, NS])
        psK = [ph.ps(f"psK{b}", [P, 4, P]) for b in range(2)]
        S = ph.ps("S", [P, 1024])
        L = ph.ps("L", [P, 1024])
        N = ph.ps("N", [P, 512])
        O = ph.ps("O", [P, 512])
        k_in = [ph.sem(f"k_in{b}") for b in range(2)]
        v_in = [ph.sem(f"v_in{b}") for b in range(2)]
        l_in = [ph.sem(f"l_in{b}") for b in range(2)]
        (table_in, consts, staged, k_turned, k_copied, scored, l_turned, scanned, shifted, expd, p_turned,
         p_copied, valued, masked, o_turned, reduced, gate_turned) = (ph.sem(s) for s in (
             "table_in", "consts", "staged", "k_turned", "k_copied", "scored", "l_turned", "scanned", "shifted",
             "expd", "p_turned", "p_copied", "valued", "masked", "o_turned", "reduced", "gate_turned"))
        dve_step, pace = ph.sem("dve_step"), ph.sem("pace")
        block = ph.block()

        def sequences(eng, body):
            with eng.Fori(0, NB // 2) as j:
                for b in range(2):
                    body(j * 2 + b, b, j)

        @block.sync
        def _(sp):
            sp.dma_start(table[:], page_table.rearrange("b n -> (b n)").unsqueeze(0)).then_inc(table_in, 16)
            sp.wait_ge(table_in, 16)

            def body(i, b, j):
                sp.wait_ge(l_turned, i + 1)
                sp.wait_ge(k_turned, i * NPG + NPG)
                sp.wait_ge(valued, i + 1)
                for g in range(NPG):
                    page = sp.value_load(table[0:1, bass.ds(i * NPG + g, 1)], min_val=0, max_val=N_POOL - 1)
                    sp.dma_start(lp[:, b, g, :], pool_lf[bass.ds(page, 1)].rearrange("o p h -> p (o h)"))\
                        .then_inc(l_in[b], 16)
                    sp.dma_start(kp[:, b, g, :], pool_k[bass.ds(page, 1)].rearrange("o p c -> p (o c)"))\
                        .then_inc(k_in[b], 16)
                    sp.dma_start(vp[:, b, g, :], pool_v[bass.ds(page, 1)].rearrange("o p c -> p (o c)"))\
                        .then_inc(v_in[b], 16)
                sp.dma_start(vn[:, b, :], fv[bass.ds(i * TS + SEQ, TS), :]).then_inc(v_in[b], 16)
            sequences(sp, body)

        @block.gpsimd
        def _(pool):
            step = Chain(pool, consts)
            step(pool.memset(qx_all[:], 0.0))
            step(pool.memset(headmask[:], 1.0))
            step(pool.affine_select(headmask[:], headmask[:], [[-TS, H], [0, DH]], ALU.is_ge, 0.0, base=0,
                                    channel_multiplier=1))
            step(pool.affine_select(headmask[:], headmask[:], [[TS, H], [0, DH]], ALU.is_ge, 0.0, base=TS - 1,
                                    channel_multiplier=-1))
            step(pool.memset(ones_row[:], 1.0))

        @block.tensor
        def _(pe):
            pe.sem_inc(l_turned, 2)
            pe.sem_inc(k_turned, 2 * NPG)
            pe.sem_inc(valued, 2)
            for m in range(4):
                mm = pe.transpose(psK[0][:, m, :NS], sog[:NS, NT, m * P:(m + 1) * P], C["ident"][:NS, :NS])
            mm.then_inc(gate_turned, 1)
            pe.wait_ge(k_copied, 2)

            def body(i, b, j):
                pe.wait_ge(staged, i + 1)
                pe.wait_ge(scanned, i + 1)
                pe.sem_inc(pace, 1)
                for g in range(NPG):
                    pe.transpose(L[:HQ, g * P:(g + 1) * P], lx[:, g].rearrange("p h q -> p (h q)"), C["ident"][:])
                pe.matmul(N[:HQ, TS:2 * TS], lnx.rearrange("p h q -> p (h q)"), sel[:], start=True, stop=True)\
                    .then_inc(l_turned, 1)
                pe.wait_ge(k_in[b], j * (16 * NPG) + 16 * NPG)
                pe.wait_ge(shifted, i + 1)
                for g in range(NPG + 1):
                    if g < NPG:
                        pe.wait_ge(k_copied, i * NPG + (g + 1))
                        for m in range(4):
                            mm = pe.transpose(psK[g % 2][:, m, :], kp[:, b, g, m * P:(m + 1) * P], C["ident"][:])
                        mm.then_inc(k_turned, 1)
                    if g:
                        pe.wait_ge(k_copied, i * NPG + (g + 2))
                        for m in range(4):
                            mm = pe.matmul(S[:HQ, (g - 1) * P:g * P], qx[:, m, :], kT[:, (g - 1) % 2, m, :],
                                           start=(m == 0), stop=(m == 3))
                        mm.then_inc(scored, 1)
                pe.wait_ge(scanned, i + 2)
                for m in range(4):
                    mm = pe.matmul(N[:HQ, 0:TS], qx[:, m, :], kn[:, m, :], start=(m == 0), stop=(m == 3))
                mm.then_inc(scored, 1)
                pe.wait_ge(expd, i + 1)
                pe.sem_inc(pace, 1)
                for g in range(NPG):
                    mm = pe.transpose(psK[0].rearrange("p a b -> p (a b)")[:, g * HQ:(g + 1) * HQ],
                                      pr[:, g * P:(g + 1) * P], C["ident"][:HQ, :HQ])
                mm = pe.transpose(N[:TS, P:P + HQ], pr[:, PAST:], C["ident"][:HQ, :HQ])
                mm.then_inc(p_turned, 1)
                pe.wait_ge(p_copied, i + 1)
                pe.wait_ge(v_in[b], j * (16 * NPG + 16) + (16 * NPG + 16))
                for g in range(NPG):
                    pe.matmul(O[:HQ, :], pT[:, g, :], vp[:, b, g, :], start=(g == 0), stop=False)
                pe.matmul(O[:HQ, :], pT[:TS, NPG, :], vn[:, b, :], start=False, stop=True).then_inc(valued, 1)
                pe.wait_ge(masked, i + 1)
                pe.sem_inc(pace, 1)
                for m in range(4):
                    mm = pe.transpose(psK[0][:, m, :HQ], om[:, m * P:(m + 1) * P], C["ident"][:HQ, :HQ])
                mm.then_inc(o_turned, 1)
                pe.wait_ge(reduced, i + 1)
            sequences(pe, body)

        @block.scalar
        def _(act):
            act.wait_ge(gate_turned, 1)
            act.copy(sgT[:], psK[0][:, :, :NS]).then_inc(k_copied, 2)

            def body(i, b, j):
                for g in range(NPG):
                    act.wait_ge(k_turned, i * NPG + (2 * NPG + g + 1))
                    act.wait_ge(scored, i * (NPG + 1) + (g + 1))
                    act.copy(kT[:, g % 2], psK[g % 2][:]).then_inc(k_copied, 1)
                act.wait_ge(shifted, i + 2)
                act.activation(pr[:], st[:], ACT.Exp, bias=mx[:], accum_out=rs[:]).then_inc(expd, 1)
                act.wait_ge(p_turned, i + 1)
                act.copy(pT[:, 0:NPG, :].rearrange("p g q -> p (g q)"), psK[0].rearrange("p a b -> p (a b)"))
                act.copy(pT[:TS, NPG, :], N[:TS, P:P + HQ]).then_inc(p_copied, 1)
            act.sem_inc(scored, 2)
            sequences(act, body)

        @block.vector
        def _(dve):
            dve.sem_inc(scanned, 1)
            dve.sem_inc(shifted, 1)
            step = Chain(dve, dve_step, per=7)
            dve.wait_ge(consts, 5)
            for m in range(4):
                for q in range(2):
                    rows = slice(q * DH, (q + 1) * DH)
                    h = 2 * m + q
                    dve.tensor_copy(qx_all[rows, :, m, h * TS:(h + 1) * TS],
                                    qTs[rows, m, :].rearrange("p (b t) -> p b t", t=TS))
            dve.tensor_copy(lnx[:], bc(lfs[:], 2, TS))
            dve.tensor_reduce(onehot[:], C["ident"][:HQ, :HQ].rearrange("p (a t) -> p t a", t=TS), AX.X, ALU.add)
            dve.tensor_reduce(causal[:], C["blk_low"][:HQ, :HQ].rearrange("p (a t) -> p t a", t=TS), AX.X, ALU.add)\
                .then_inc(consts, 1)
            dve.wait_ge(consts, 6)
            dve.tensor_scalar(causal[:], causal[:], 1.0, -NEG, ALU.subtract, ALU.mult).then_inc(consts, 1)
            dve.wait_ge(consts, 7)

            def body(i, b, j):
                step.turn(i)
                dve.wait_ge(l_in[b], j * (16 * NPG) + 16 * NPG)
                dve.tensor_copy(lx.rearrange("p g h q -> p (g h) q"),
                                bc(lp[:, b].rearrange("p g h -> p (g h)"), 2, TS))
                dve.tensor_copy(sel[:], C["ident"][:NS, bass.ds(i * TS, TS)])
                dve.tensor_copy(kn[:], kTs[:, :, bass.ds(i * TS, TS)])
                dve.tensor_copy(qx[:], qx_all[:, bass.ds(i, 1)].rearrange("p o m q -> p (o m) q")).then_inc(staged, 1)
                dve.wait_ge(l_turned, i + 3)
                step(dve.tensor_tensor_scan(F[:, :PAST], ones_row[:], L[:HQ, :], 0.0, ALU.mult, ALU.add))
                dve.tensor_tensor_scan(F[:, PAST:], ones_row[:, :TS], N[:HQ, TS:2 * TS], F[:, PAST - 1:PAST],
                                       ALU.mult, ALU.add).then_inc(scanned, 1)
                dve.wait_ge(scanned, i + 2)
                step(dve.tensor_tensor(fqt[:], F[:, PAST:], onehot[:], ALU.mult))
                step(dve.tensor_reduce(fq[:], fqt[:], AX.X, ALU.add))
                dve.wait_ge(scored, i * (NPG + 1) + (NPG + 3))
                dve.scalar_tensor_tensor(st[:, :PAST], S[:HQ, :], fq[:], F[:, :PAST], ALU.add, ALU.subtract)
                step(dve.scalar_tensor_tensor(st[:, PAST:], N[:HQ, 0:TS], fq[:], F[:, PAST:], ALU.add, ALU.subtract))
                step(dve.tensor_tensor(st[:, PAST:], st[:, PAST:], causal[:], ALU.add))
                dve.tensor_reduce(mx[:], st[:], AX.X, ALU.max, negate=True).then_inc(shifted, 1)
                dve.wait_ge(expd, i + 1)
                step(dve.reciprocal(ri[:], rs[:]))
                dve.wait_ge(valued, i + 3)
                dve.scalar_tensor_tensor(om[:], O[:HQ, :], ri[:], headmask.rearrange("p h d -> p (h d)"),
                                         ALU.mult, ALU.mult).then_inc(masked, 1)
                dve.wait_ge(o_turned, i + 1)
                step(dve.tensor_reduce(red[:, :, bass.ds(i * TS, TS)],
                                       psK[0][:, :, :HQ].rearrange("p m (h q) -> p m q h", q=TS), AX.X, ALU.add))
                dve.sem_inc(reduced, 1)
                step.close()
            sequences(dve, body)
            dve.wait_ge(dve_step, NB * step.per)
            dve.tensor_tensor(mixT[:, 0:4, SEQ:], red[:], sgT[:], ALU.mult)



GROUP = 4


def inverse_buffers(ph, T):
    return {n: [ph.sb(f"{n}{g}", [T, GROUP, T]) for g in range(2)] for n in ("NL", "X", "XT", "PX")}


def inverse_sems(ph):
    return {n: ph.sem(n) for n in ("n_level", "p_done", "p_copied", "x_done", "x_added")}


def inverse_pool(pool, C, I, s, NT_, T, levels, i, pace):
    for l in range(levels):
        for g in range(2):
            n = 2 * l + g
            if l:
                pool.wait_ge(s["p_done"], i * (2 * levels) + (n - 1))
            if l == 1:
                pool.wait_ge(s["x_added"], i * (2 * levels) + (n - 1))
            pool.tensor_tensor(I["NL"][g][:], NT_[:, g * GROUP:(g + 1) * GROUP, :],
                               bc(C["join"][:T, l, :T], 1, GROUP), ALU.mult).then_inc(s["n_level"], 1)


def inverse_pe(pe, C, I, s, PS, T, levels, i):
    def heads(ps, lhsT, rhs):
        for h in range(GROUP):
            mm = pe.matmul(ps[:T, h * P:h * P + T], lhsT[:, h, :], rhs(h), start=True, stop=True)
        return mm
    for l in range(levels):
        for g in range(2):
            n = 2 * l + g
            bank = 3 * g
            pe.wait_ge(s["n_level"], i * (2 * levels) + (n + 1))
            if l:
                pe.wait_ge(s["x_added"], i * (2 * levels) + (n - 1))
            ident = C["ident"][:T, :T]
            heads(PS[:, bank], I["NL"][g], lambda h: ident if l == 0 else I["X"][g][:, h, :])\
                .then_inc(s["p_done"], 1)
        for g in range(2):
            if l == 0:
                continue
            n = 2 * l + g
            bank = 3 * g
            pe.wait_ge(s["p_copied"], i * (2 * (levels - 1)) + (n - 1))
            if l < levels - 1:
                heads(PS[:, bank + 1], I["XT"][g], lambda h: I["PX"][g][:, h, :])
            heads(PS[:, bank + 2], I["PX"][g], lambda h: I["XT"][g][:, h, :]).then_inc(s["x_done"], 1)


def inverse_act(act, I, s, PS, T, levels, i):
    for l in range(1, levels):
        for g in range(2):
            n = 2 * l + g
            act.wait_ge(s["p_done"], i * (2 * levels) + (n + 1))
            act.copy(I["PX"][g][:], PS[:T, 3 * g, :].rearrange("p (h t) -> p h t", h=GROUP)[:, :, :T])\
                .then_inc(s["p_copied"], 1)


def inverse_dve(dve, C, I, s, PS, T, levels, i):
    ident = bc(C["ident"][:T, :T], 1, GROUP)

    def bank(n):
        return PS[:T, n, :].rearrange("p (h t) -> p h t", h=GROUP)[:, :, :T]
    for l in range(levels):
        for g in range(2):
            n = 2 * l + g
            X, XT = I["X"][g], I["XT"][g]
            if l == 0:
                dve.wait_ge(s["p_done"], i * (2 * levels) + (n + 1))
                dve.tensor_tensor(X[:], bank(3 * g), ident, ALU.add)
                dve.tensor_tensor(XT[:], I["NL"][g][:], ident, ALU.add).then_inc(s["x_added"], 1)
            else:
                dve.wait_ge(s["x_done"], i * (2 * (levels - 1)) + (n - 1))
                if l < levels - 1:
                    dve.tensor_tensor(X[:], bank(3 * g + 1), X[:], ALU.add)
                dve.tensor_tensor(XT[:], bank(3 * g + 2), XT[:], ALU.add).then_inc(s["x_added"], 1)


def build_join(nc, C):
    with Phase(nc, "join") as ph:
        blocks = ph.sb("blocks", [P, 8, P])
        s = ph.sem("made")
        block = ph.block()

        @block.gpsimd
        def _(pool):
            step = Chain(pool, s)
            step(pool.memset(blocks[:], 1.0))
            for l in range(7):
                w = 2 ** l
                v = blocks[:, l, :].rearrange("p (a t) -> p a t", t=w)
                step(pool.affine_select(v, v, [[-w, P // w], [0, w]], ALU.is_ge, 0.0, base=0, channel_multiplier=1))
                step(pool.affine_select(v, v, [[w, P // w], [0, w]], ALU.is_ge, 0.0, base=w - 1,
                                        channel_multiplier=-1))
            for l in range(7):
                step(pool.tensor_tensor(C["join"][:, l, :], blocks[:, l + 1, :], blocks[:, l, :], ALU.subtract))


def rwkv(nc, C, sample, prw, state_in, shift_in, W, mixT, state_out, shift_out):
    T = NS if sample else P
    NSEQ = NB if sample else 1
    levels = 3 if sample else 7
    n_it = 1 if sample else NT
    tok0 = SEQ if sample else 0
    PR = H // 2
    with Phase(nc, "rs" if sample else "rw") as ph:
        cur = ph.sb("cur", [T, RW_COLS])
        pm = ph.sb("prv_mu", [T, 2 * RW_COLS])
        prv, mu = pm[:, :RW_COLS], pm[:, RW_COLS:]
        par = {n: ph.sb(n, [T, RW_W]) for n in ("k_k", "k_a", "r_k", "ln_w", "ln_b")}
        wa0 = ph.sb("wa0", [T, 2, RW_W])
        wa2 = ph.sb("wa2", [P, 2, RW_W])
        g2 = ph.sb("g2", [P, RW_W])
        cen = ph.sb("cen", [T, T])
        cols = ph.sb("cols", [T, 8])
        mask = ph.sb("mask", [T, 2, T])
        lowT = ph.sb("lowT", [P, 2, T])
        za = ph.sb("za", [T, 2, RW_W])
        g = ph.sb("g", [T, RW_W])
        gp = ph.sb("gp", [T, RW_W])
        e0, e1, e2 = (ph.sb(n, [T, RW_W]) for n in ("e0", "e1", "e2"))
        kk, sq, kf, bb = (ph.sb(n, [T, RW_W]) for n in ("kk", "sq", "kf", "bb"))
        at, rt, bt, kt = (ph.sb(n, [T, RW_W]) for n in ("at", "rt", "bt", "kt"))
        s8, m8, r8, bon = (ph.sb(n, [T, H]) for n in ("s8", "m8", "r8", "bon"))
        ecm = ph.sb("ecm", [P, PR, 8])
        arT = ph.sb("arT", [P, PR, 2, T])
        bT, kT = (ph.sb(n, [P, PR, T]) for n in ("bT", "kT"))
        LB, LK = (ph.sb(n, [T, H, 2, T]) for n in ("LB", "LK"))
        u0, u = (ph.sb(n, [T, RW_W]) for n in ("u0", "u"))
        S = ph.sb("S", [P, NSEQ, PR, P])
        S0 = None if sample else ph.sb("S0", [P, PR, P])
        pre = ph.sb("pre", [P, NSEQ, PR, P])
        y = ph.sb("y", [T, RW_W])
        if sample:
            sT = ph.sb("sT", [P, PR, 2, T])
            ux = pm[:, :2 * NB * P].rearrange("p (n b c) -> p n b c", n=2, b=NB)
        I = inverse_buffers(ph, T)
        PS = ph.ps("PS", [P, 8, 512])
        inv = inverse_sems(ph)
        names = ("par_in pre_in setup rows_in mixed_in shifted tanhd gate_in low_turned low_copied lowrank za_done "
                 "zt_done g_copied logw_done summed gp_done expd squared kk_rooted tilded turned ar_copied bk_copied gram "
                 "masked s0_done u0_sum u0_done u_sum u_done ys_sum s_turned rk_done y_read vr_done y_rooted yn_done y_done y_turned "
                 "tile_done spread state_done st_turned st_copied out").split()
        s = {n: ph.sem(n) for n in names}
        dve_step, pool_step, pace, dve_pace = (ph.sem(n) for n in ("dve_step", "pool_step", "pace", "dve_pace"))
        block = ph.block()
        ident = C["ident"]

        def tiles(eng, body):
            if sample:
                body(0)
            else:
                with eng.Fori(0, n_it) as i:
                    body(i)

        def pairs(ap):
            return ap.rearrange("p (m c) -> p m c", m=PR)

        def heads(ap):
            return ap.rearrange("p (h d) -> p h d", h=H)

        @block.sync
        def _(sp):
            for t, src in ((mu, W["mu"]), (par["k_k"], W["k_k"]), (par["k_a"], W["k_a"]), (par["r_k"], W["r_k"]),
                           (par["ln_w"], W["ln_w"]), (par["ln_b"], W["ln_b"])):
                sp.dma_start(t[:], src.partition_broadcast(T)).then_inc(s["par_in"], 16)
            sp.dma_start(wa0[:, 0, :], W["w0"].partition_broadcast(T)).then_inc(s["par_in"], 16)
            sp.dma_start(wa0[:, 1, :], W["a0"].partition_broadcast(T)).then_inc(s["par_in"], 16)
            sp.wait_ge(s["setup"], 2)
            sp.dma_start(wa2[0:R_W, 0, :], W["w2"]).then_inc(s["par_in"], 16)
            sp.dma_start(wa2[R_W:, 1, :], W["a2"]).then_inc(s["par_in"], 16)
            sp.dma_start(g2[:], W["g2"]).then_inc(s["par_in"], 16)
            if sample:
                for q in range(2):
                    for b in range(NB):
                        sp.dma_start(pre[q * DH:(q + 1) * DH, b, :, q * DH:(q + 1) * DH],
                                     state_in[b].rearrange("(m q) i j -> q i m j", q=2)[q]).then_inc(s["pre_in"], 16)
            sp.dma_start(shift_out, prw[NTOK - NS + TS:NTOK + 1:TS, :] if sample else prw[SEQ:SEQ + 1, :])\
                .then_inc(s["out"], 16)

            def body(i):
                sp.wait_ge(s["tile_done"], i + 1)
                sp.dma_start(cur[:], prw[bass.ds(i * P + (tok0 + 1), T), :]).then_inc(s["rows_in"], 16)
                if sample:
                    sp.dma_start(prv[:], prw[tok0:tok0 + T, :]).then_inc(s["rows_in"], 16)
                    sp.wait_ge(s["rows_in"], 32)
                    sp.dma_start(prv[0:T:TS, :], shift_in).then_inc(s["rows_in"], 16)
                else:
                    sp.dma_start(prv[:], prw[bass.ds(i * P + tok0, T), :]).then_inc(s["rows_in"], 16)
            tiles(sp, body)
            sp.wait_ge(s["st_copied"], NSEQ)
            for q in range(2):
                rows = slice(q * DH, (q + 1) * DH)
                for b in range(NSEQ):
                    dst = state_out[b] if sample else state_out
                    sp.dma_start(dst.rearrange("(m q) i j -> q i m j", q=2)[q], pre[rows, b, :, rows])\
                        .then_inc(s["out"], 16)
            sp.wait_ge(s["out"], 16 * (1 + 2 * NSEQ))

        @block.gpsimd
        def _(pool):
            n_setup = 0

            def made(ins):
                nonlocal n_setup
                ins.then_inc(s["setup"], 1)
                n_setup += 1
                pool.wait_ge(s["setup"], n_setup)
            made(pool.memset(wa2[:], 0.0))
            made(pool.memset(pre[:], 0.0))
            if not sample:
                made(pool.memset(S[:], 0.0))
            made(pool.memset(LB[:], 0.0))
            made(pool.memset(LK[:], 0.0))
            tri = C["blk_tri"] if sample else C["tri"]
            made(pool.tensor_copy(mask[:, 1, :], tri[:T, :T]))
            made(pool.tensor_tensor(mask[:, 0, :], tri[:T, :T], ident[:T, :T], ALU.subtract))
            if sample:
                made(pool.tensor_copy(cen[:], tri[:T, :T]))
                made(pool.tensor_copy(cols[:], C["blk"][:T, 0:T:TS]))
            else:
                made(pool.tensor_copy(cols[:, 0:1], C["tri"][:, 63:64]))
                made(pool.tensor_tensor(cols[:, 1:2], C["ones"][:, 0:1], cols[:, 0:1], ALU.subtract))
                made(pool.memset(cols[:, 2:8], 0.0))
                made(pool.tensor_tensor(cen[:], C["tri"][:], C["tri"][:, 63:64].to_broadcast([P, P]), ALU.subtract))
            pool.wait_ge(s["par_in"], 16 * 11)
            step = Chain(pool, pool_step, per=2)

            def body(i):
                step.turn(i)
                pool.wait_ge(s["rows_in"], i * 32 + (48 if sample else 32))
                step(pool.tensor_tensor(prv[:], prv[:], cur[:], ALU.subtract))
                pool.tensor_tensor(prv[:], prv[:], mu[:], ALU.mult).then_inc(s["mixed_in"], 1)
                pool.wait_ge(s["squared"], i + 1)
                pool.tensor_tensor(r8[:], m8[:], C["half"][:T, :H], ALU.pow).then_inc(s["kk_rooted"], 1)
                pool.wait_ge(s["tilded"], i + 1)
                step(pool.tensor_tensor(prv[:, 0:RW_W], cur[:, 0:RW_W], kf[:], ALU.mult))
                pool.tensor_tensor(prv[:, 0:RW_W], prv[:, 0:RW_W], par["r_k"][:], ALU.mult).then_inc(s["rk_done"], 1)
                pool.wait_ge(s["masked"], i * 4 + 4)
                inverse_pool(pool, C, I, inv, LB[:, :, 0, :], T, levels, i, pace)
                pool.wait_ge(s["vr_done"], i + 1)
                pool.tensor_tensor(r8[:], m8[:], C["half"][:T, :H], ALU.pow).then_inc(s["y_rooted"], 1)
                step.close()
            tiles(pool, body)

        @block.scalar
        def _(act):
            act.sem_inc(s["tile_done"], 1)
            if sample:
                for b in range(NB):
                    act.wait_ge(s["st_turned"], b + 1)
                    act.copy(S[:, b], pairs(PS[:, b % 2, :])).then_inc(s["state_done"], 1)

            def body(i):
                act.wait_ge(s["shifted"], i + 1)
                act.activation(cur[:, 3 * RW_W:3 * RW_W + R_W], cur[:, 3 * RW_W:3 * RW_W + R_W], ACT.Tanh)
                act.activation(cur[:, 3 * RW_W + R_W + R_A:], cur[:, 3 * RW_W + R_W + R_A:], ACT.Tanh, scale=0.5)\
                    .then_inc(s["tanhd"], 1)
                act.wait_ge(s["low_turned"], i + 1)
                act.copy(lowT[:], PS[:, 6, :2 * T].rearrange("p (a t) -> p a t", a=2)).then_inc(s["low_copied"], 1)
                act.wait_ge(s["lowrank"], i + 1)
                act.copy(g[:], PS[:T, 2, :]).then_inc(s["g_copied"], 1)
                act.wait_ge(s["za_done"], i + 1)
                act.activation(za[:], za[:], ACT.Tanh, scale=0.5).then_inc(s["zt_done"], 1)
                act.wait_ge(s["gp_done"], i + 1)
                act.activation(e1[:], PS[:T, 3, :], ACT.Exp)
                act.activation(e2[:], PS[:T, 3, :], ACT.Exp, scale=-1.0)
                act.activation(e0[:], gp[:], ACT.Exp)
                act.activation(ecm[:], PS[:, 7, :PR * 8].rearrange("p (m c) -> p m c", m=PR), ACT.Exp)\
                    .then_inc(s["expd"], 1)
                act.wait_ge(s["turned"], i + 1)
                for n in range(2):
                    ins = act.copy(arT[:, :, n, :], pairs(PS[:, 4 + n, :])[:, :, :T])
                ins.then_inc(s["ar_copied"], 1)
                if sample:
                    act.wait_ge(s["s_turned"], 1)
                    act.copy(sT[:], PS[:, 3, :].rearrange("p (m a t) -> p m a t", m=PR, a=2)).then_inc(s["s0_done"], 1)
                act.wait_ge(s["u0_sum"], i + 1)
                act.copy(u0[:], PS[:T, 6, :]).then_inc(s["u0_done"], 1)
                inverse_act(act, I, inv, PS, T, levels, i)
                act.wait_ge(s["u_sum"], i + 1)
                act.copy(u[:], PS[:T, 7, :]).then_inc(s["u_done"], 1)
                act.wait_ge(s["y_turned"], i + 1)
                act.copy(mixT[:, :, bass.ds(i * P + tok0, T)], pairs(PS[:, 2, :])[:, :, :T]).then_inc(s["tile_done"], 1)
            tiles(act, body)
            for b in range(NSEQ):
                act.wait_ge(s["st_turned"], (NB if sample else 0) + b + 1)
                act.copy(pre[:, b], pairs(PS[:, b % 2, :])).then_inc(s["st_copied"], 1)

        @block.tensor
        def _(pe):
            if sample:
                pe.wait_ge(s["pre_in"], 16 * 2 * NB)
                for b in range(NB):
                    if b >= 2:
                        pe.wait_ge(s["state_done"], b - 1)
                    for m in range(PR):
                        mm = pe.transpose(PS[:, b % 2, m * P:(m + 1) * P], pre[:, b, m, :], ident[:])
                    mm.then_inc(s["st_turned"], 1)
                pe.wait_ge(s["state_done"], NB)
            pe.wait_ge(s["par_in"], 16 * 11)

            def body(i):
                pe.wait_ge(s["gate_in"], i + 1)
                pe.sem_inc(pace, 1)
                for n in range(2):
                    mm = pe.transpose(PS[:, 6, n * T:(n + 1) * T], cur[:, 3 * RW_W + n * P:3 * RW_W + (n + 1) * P],
                                      ident[:T, :T])
                mm.then_inc(s["low_turned"], 1)
                pe.wait_ge(s["low_copied"], i + 1)
                for n in range(2):
                    pe.matmul(PS[:T, n, :], lowT[:, 0, :], wa2[:, n, :], start=True, stop=True)
                pe.matmul(PS[:T, 2, :], lowT[:, 1, :], g2[:], start=True, stop=True).then_inc(s["lowrank"], 1)
                pe.wait_ge(s["logw_done"], i + 1)
                pe.matmul(PS[:T, 3, :], cen[:], gp[:], start=True, stop=True)
                for m in range(PR):
                    mm = pe.matmul(PS[:, 7, m * 8:(m + 1) * 8], gp[:, m * P:(m + 1) * P], cols[:], start=True,
                                   stop=True)
                mm.then_inc(s["summed"], 1)
                pe.wait_ge(s["tilded"], i + 1)
                pe.sem_inc(pace, 1)
                for n, t in enumerate((at, rt, bt, kt)):
                    for m in range(PR):
                        mm = pe.transpose(PS[:, 4 + n, m * P:m * P + T], t[:, m * P:(m + 1) * P], ident[:T, :T])
                mm.then_inc(s["turned"], 1)
                pe.wait_ge(s["ar_copied"], i + 1)
                pe.wait_ge(s["bk_copied"], i + 1)
                if sample:
                    for b in range(NB):
                        for m in range(PR):
                            o = PS[:, 3, m * 2 * T:(m + 1) * 2 * T].rearrange("p (a t) -> p a t", a=2)
                            mm = pe.matmul(o[:, :, b * TS:(b + 1) * TS], S[:, b, m, :],
                                           arT[:, m, :, b * TS:(b + 1) * TS], start=True, stop=True)
                    mm.then_inc(s["s_turned"], 1)
                    pe.wait_ge(s["s0_done"], 1)
                for gr in range(2):
                    for n, t in enumerate((bT, kT)):
                        for hh in range(GROUP):
                            h = gr * GROUP + hh
                            rows = slice((h % 2) * DH, (h % 2 + 1) * DH)
                            mm = pe.matmul(PS[:T, 4 * gr + 2 * n + hh % 2, (hh // 2) * 256:(hh // 2) * 256 + 2 * T],
                                           t[rows, h // 2, :], arT[rows, h // 2, :, :].rearrange("p a t -> p (a t)"),
                                           start=True, stop=True)
                        mm.then_inc(s["gram"], 1)
                pe.wait_ge(s["masked"], i * 4 + 4)
                pe.wait_ge(s["s0_done"], i + 1)

                def with_state(bank, n):
                    for m in range(PR):
                        c = slice(m * P, (m + 1) * P)
                        if sample:
                            pe.matmul(PS[:T, bank, c], sT[:, m, n, :], ident[:], start=True, stop=False)
                        else:
                            pe.matmul(PS[:T, bank, c], arT[:, m, n, :], S0[:, m, :], start=True, stop=False)
                        for h in (2 * m, 2 * m + 1):
                            hc = slice(h * DH, (h + 1) * DH)
                            if n:
                                pe.matmul(PS[:T, bank, hc], LB[:, h, 1, :], u[:, hc], start=False, stop=False)
                            mm = pe.matmul(PS[:T, bank, hc], LK[:, h, n, :],
                                           cur[:, 2 * RW_W + h * DH:2 * RW_W + (h + 1) * DH], start=False,
                                           stop=(h % 2 == 1))
                    return mm
                with_state(6, 0).then_inc(s["u0_sum"], 1)
                inverse_pe(pe, C, I, inv, PS, T, levels, i)
                pe.wait_ge(s["u0_done"], i + 1)
                pe.wait_ge(inv["x_added"], i * (2 * levels) + 2 * levels)
                for h in range(H):
                    hc = slice(h * DH, (h + 1) * DH)
                    mm = pe.matmul(PS[:T, 7, hc], I["XT"][h // GROUP][:, h % GROUP, :], u0[:, hc], start=True,
                                   stop=True)
                mm.then_inc(s["u_sum"], 1)
                pe.wait_ge(s["u_done"], i + 1)
                if sample:
                    with_state(6, 1).then_inc(s["ys_sum"], 1)
                    for m in range(PR):
                        pe.wait_ge(s["spread"], m + 1)
                        for half in range(2):
                            for n, t in enumerate((bt, kt)):
                                mm = pe.matmul(PS[:, half, :], t[:, m * P:(m + 1) * P],
                                               ux[:, n, half * 4:half * 4 + 4, :].rearrange("p b c -> p (b c)"),
                                               start=(n == 0), stop=(n == 1))
                        mm.then_inc(s["ys_sum"], 1)
                else:
                    with_state(6, 1)
                    for m in range(PR):
                        c = slice(m * P, (m + 1) * P)
                        pe.matmul(PS[:, 0, c], bt[:, c], u[:, c], start=True, stop=False)
                        mm = pe.matmul(PS[:, 0, c], kt[:, c], cur[:, 2 * RW_W + m * P:2 * RW_W + (m + 1) * P],
                                       start=False, stop=True)
                    mm.then_inc(s["ys_sum"], 1)
                pe.wait_ge(s["y_done"], i + 1)
                pe.sem_inc(pace, 1)
                for m in range(PR):
                    mm = pe.transpose(PS[:, 2, m * P:m * P + T], y[:, m * P:(m + 1) * P], ident[:T, :T])
                mm.then_inc(s["y_turned"], 1)
            tiles(pe, body)
            pe.wait_ge(s["state_done"], 2 * NB if sample else NT)
            for b in range(NSEQ):
                if b >= 2:
                    pe.wait_ge(s["st_copied"], b - 1)
                for m in range(PR):
                    mm = pe.transpose(PS[:, b % 2, m * P:(m + 1) * P], S[:, b, m, :], ident[:])
                mm.then_inc(s["st_turned"], 1)

        @block.vector
        def _(dve):
            step = Chain(dve, dve_step, per=23 if sample else 21)
            dve.wait_ge(s["par_in"], 16 * 11)
            dve.wait_ge(s["setup"], 8 if sample else 11)
            k_, r_, v_ = cur[:, RW_W:2 * RW_W], cur[:, 0:RW_W], cur[:, 2 * RW_W:3 * RW_W]

            def body(i):
                step.turn(i)
                dve.wait_ge(s["mixed_in"], i + 1)
                dve.tensor_tensor(cur[:], prv[:], cur[:], ALU.add).then_inc(s["shifted"], 1)
                dve.wait_ge(s["shifted"], i + 1)
                step(dve.tensor_tensor(kk[:], k_, par["k_k"][:], ALU.mult))
                step(dve.tensor_tensor(sq[:], kk[:], kk[:], ALU.mult))
                step(dve.tensor_reduce(s8[:], heads(sq[:]), AX.X, ALU.add))
                dve.tensor_scalar(m8[:], s8[:], 1e-6, None, ALU.add).then_inc(s["squared"], 1)
                dve.wait_ge(s["tanhd"], i + 1)
                gd = cur[:, 3 * RW_W + R_W + R_A:]
                dve.tensor_scalar(gd, gd, 0.5, 0.5, ALU.mult, ALU.add).then_inc(s["gate_in"], 1)
                dve.wait_ge(s["kk_rooted"], i + 1)
                step(dve.tensor_tensor(heads(kk[:]), heads(kk[:]), bc(r8[:], 2, DH), ALU.mult))
                dve.wait_ge(s["lowrank"], i + 1)
                dve.tensor_tensor(za[:], PS[:T, 0:2, :], wa0[:], ALU.add).then_inc(s["za_done"], 1)
                dve.wait_ge(s["zt_done"], i + 1)
                dve.tensor_scalar(gp[:], za[:, 0, :], 0.5 * RW_DECAY, 0.5 * RW_DECAY, ALU.mult, ALU.add)\
                    .then_inc(s["logw_done"], 1)
                step(dve.tensor_scalar(za[:, 1, :], za[:, 1, :], 0.5, 0.5, ALU.mult, ALU.add))
                step(dve.scalar_tensor_tensor(kf[:], za[:, 1, :], 1.0, par["k_a"][:], ALU.subtract, ALU.mult))
                step(dve.scalar_tensor_tensor(kf[:], kf[:], 1.0, k_, ALU.add, ALU.mult))
                step(dve.tensor_tensor(bb[:], kk[:], za[:, 1, :], ALU.mult))
                dve.wait_ge(s["summed"], i + 1)
                dve.tensor_tensor(gp[:], PS[:T, 3, :], gp[:], ALU.subtract).then_inc(s["gp_done"], 1)
                dve.wait_ge(s["expd"], i + 1)
                if not sample:
                    dve.tensor_tensor(S0[:], S[:, 0], bc(ecm[:, :, 0], 2, P), ALU.mult).then_inc(s["s0_done"], 1)
                dve.tensor_tensor(rt[:], r_, e1[:], ALU.mult)
                dve.scalar_tensor_tensor(at[:], kk[:], -1.0, e0[:], ALU.mult, ALU.mult)
                dve.tensor_tensor(bt[:], bb[:], e2[:], ALU.mult)
                dve.tensor_tensor(kt[:], kf[:], e2[:], ALU.mult).then_inc(s["tilded"], 1)
                dve.wait_ge(s["turned"], i + 1)
                dve.tensor_copy(bT[:], pairs(PS[:, 6, :])[:, :, :T])
                dve.tensor_copy(kT[:], pairs(PS[:, 7, :])[:, :, :T]).then_inc(s["bk_copied"], 1)
                dve.wait_ge(s["rk_done"], i + 1)
                step(dve.tensor_reduce(bon[:], heads(prv[:, 0:RW_W]), AX.X, ALU.add))
                for n in range(4):
                    gr, t = divmod(n, 2)
                    dve.wait_ge(s["gram"], i * 4 + (n + 1))
                    dve.sem_inc(dve_pace, 1)
                    src = PS[:T, 4 * gr + 2 * t:4 * gr + 2 * t + 2, :].rearrange("p q (m x) -> p q m x", m=2)
                    dst = (LB, LK)[t][:, gr * GROUP:(gr + 1) * GROUP].rearrange("p (m q) a t -> p q m (a t)", q=2)
                    keep = bc(bc(mask.rearrange("p a t -> p (a t)"), 1, 2), 1, 2)
                    dve.copy_predicated(dst, keep.bitcast(I32), src[:, :, :, :2 * T]).then_inc(s["masked"], 1)
                inverse_dve(dve, C, I, inv, PS, T, levels, i)
                dve.wait_ge(s["ys_sum"], i + 1)
                step(dve.tensor_reduce(s8[:], heads(PS[:T, 6, :]), AX.X, ALU.add))
                step(dve.tensor_scalar(s8[:], s8[:], -1.0 / DH, None, ALU.mult))
                step(dve.tensor_tensor(heads(y[:]), heads(PS[:T, 6, :]), bc(s8[:], 2, DH), ALU.add))
                step(dve.tensor_tensor(sq[:], y[:], y[:], ALU.mult))
                step(dve.tensor_reduce(s8[:], heads(sq[:]), AX.X, ALU.add))
                dve.tensor_scalar(m8[:], s8[:], 1.0 / DH, RW_GN_EPS, ALU.mult, ALU.add).then_inc(s["vr_done"], 1)
                step(dve.tensor_tensor(heads(sq[:]), heads(v_), bc(bon[:], 2, DH), ALU.mult))
                dve.wait_ge(s["y_rooted"], i + 1)
                step(dve.tensor_tensor(heads(y[:]), heads(y[:]), bc(r8[:], 2, DH), ALU.mult))
                step(dve.tensor_tensor(y[:], y[:], par["ln_w"][:], ALU.mult))
                step(dve.tensor_tensor(y[:], y[:], par["ln_b"][:], ALU.add))
                step(dve.tensor_tensor(y[:], y[:], sq[:], ALU.add))
                dve.wait_ge(s["g_copied"], i + 1)
                if not sample:
                    for q in range(2):
                        rows = slice(q * DH, (q + 1) * DH)
                        ins = dve.tensor_tensor(S[rows, 0, :, rows], pairs(PS[:, 0, :])[rows, :, rows],
                                                S0[rows, :, rows], ALU.add)
                    step(ins)
                    step(dve.tensor_tensor(S[:, 0], S[:, 0], bc(ecm[:, :, 1], 2, P), ALU.mult))
                    dve.sem_inc(s["state_done"], 1)
                    dve.tensor_tensor(y[:], y[:], g[:], ALU.mult).then_inc(s["y_done"], 1)
                else:
                    seg = bc(cols[:], 2, P)
                    for m in range(PR):
                        if m:
                            dve.wait_ge(s["ys_sum"], m + 1)
                        c = slice(m * P, (m + 1) * P)
                        dve.tensor_tensor(ux[:, 0], bc(u[:, c], 1, NB), seg, ALU.mult)
                        dve.tensor_tensor(ux[:, 1], bc(v_[:, c], 1, NB), seg, ALU.mult).then_inc(s["spread"], 1)
                        dve.wait_ge(s["ys_sum"], m + 2)
                        for q in range(2):
                            rows = slice(q * DH, (q + 1) * DH)
                            src = PS[:, 0:2, :].rearrange("p a (b c) -> p (a b) c", c=P)
                            ins = dve.tensor_tensor(S[rows, :, m, rows], src[rows, :, rows], S[rows, :, m, rows],
                                                    ALU.add)
                        step(ins)
                    for m in range(PR):
                        ins = dve.tensor_tensor(S[:, :, m, :], S[:, :, m, :], bc(ecm[:, m, :], 2, P), ALU.mult)
                    ins.then_inc(s["state_done"], NB)
                    dve.tensor_tensor(y[:], y[:], g[:], ALU.mult).then_inc(s["y_done"], 1)
                step.close()
            tiles(dve, body)


def gdn_gates(nc, C, zba, A_log, dt_bias, beta, gate):
    with Phase(nc, "gg") as ph:
        ba = ph.sb("ba", [P, NT + 1, 2 * H])
        ab = ph.sb("ab", [P, 2, H])
        x, e, l, eb = (ph.sb(n, [P, NT + 1, H]) for n in ("x", "e", "l", "eb"))
        rows_in, loaded, exps, ready, negged = (ph.sem(n) for n in ("rows_in", "loaded", "exps", "ready", "negged"))
        step_sem, zeroed = ph.sem("step"), ph.sem("zeroed")
        block = ph.block()
        cols = slice(GDN_W, GDN_W + 2 * H)

        @block.gpsimd
        def _(pool):
            pool.memset(ba[:], 0.0).then_inc(zeroed, 1)

        @block.sync
        def _(sp):
            sp.wait_ge(zeroed, 1)
            sp.dma_start(ba[:, 0:NT, :], zba[0:SEQ, cols].rearrange("(n p) c -> p n c", p=P)).then_inc(rows_in, 16)
            sp.dma_start(ba[:NS, NT, :], zba[SEQ:, cols]).then_inc(rows_in, 16)
            sp.dma_start(ab[:, 0, :], A_log.partition_broadcast(P)).then_inc(rows_in, 16)
            sp.dma_start(ab[:, 1, :], dt_bias.partition_broadcast(P)).then_inc(rows_in, 16)

        @block.scalar
        def _(act):
            act.wait_ge(rows_in, 64)
            act.activation(ab[:, 0, :], ab[:, 0, :], ACT.Exp)
            act.activation(eb[:], ba[:, :, 0:H], ACT.Exp, scale=-1.0).then_inc(exps, 1)
            act.wait_ge(negged, 1)
            act.activation(e[:], e[:], ACT.Exp).then_inc(exps, 1)
            act.wait_ge(exps, 2)
            act.activation(l[:], e[:], ACT.Ln, bias=1.0).then_inc(exps, 1)

        @block.vector
        def _(dve):
            step = Chain(dve, step_sem)
            dve.wait_ge(rows_in, 64)
            step(dve.tensor_tensor(x[:], ba[:, :, H:], bc(ab[:, 1, :], 1, NT + 1), ALU.add))
            dve.scalar_tensor_tensor(e[:], x[:], -1.0, x[:], ALU.mult, ALU.min).then_inc(negged, 1)
            dve.wait_ge(exps, 1)
            step(dve.tensor_scalar(eb[:], eb[:], 1.0, None, ALU.add))
            step(dve.reciprocal(beta[:], eb[:]))
            dve.wait_ge(exps, 3)
            step(dve.scalar_tensor_tensor(x[:], x[:], 0.0, l[:], ALU.max, ALU.add))
            step(dve.scalar_tensor_tensor(gate[:], x[:], -1.0, bc(ab[:, 0, :], 1, NT + 1), ALU.mult, ALU.mult))


def gdn(nc, C, sample, qkv, zba, beta, gate, norm_w, state_in, mixT, state_out):
    T = NS if sample else P
    NSEQ = NB if sample else 1
    levels = 3 if sample else 7
    tok0 = SEQ if sample else 0
    tile0 = NT if sample else 0
    with Phase(nc, "gs" if sample else "gd") as ph:
        qf = ph.sb("qf", [P, 3 * H, T])
        z = ph.sb("z", [T, GDN_W])
        gain = ph.sb("gain", [T, DK])
        tri = C["blk_tri"] if sample else C["tri"]
        suf = ph.sb("suf", [T, T])
        mneg = ph.sb("mneg", [T, T])
        gt, bt = ph.sb("gt", [T, H]), ph.sb("bt", [T, H])
        gx = ph.sb("gx", [T, NSEQ, H])
        gb = ph.sb("gb", [T, H, T])
        Gs = ph.sb("Gs", [T, H])
        eg = ph.sb("eg", [T, 2, H])
        etot = ph.sb("etot", [P, NSEQ, H])
        gam = ph.sb("gam", [T, H, T])
        sq = ph.sb("sq", [T, 2 * H, DK])
        s16, m16, r16 = (ph.sb(n, [T, 2 * H]) for n in ("s16", "m16", "r16"))
        qn, kn, kb, ke, vb, u0, y0, w = (ph.sb(n, [T, H, DK]) for n in ("qn", "kn", "kb", "ke", "vb", "u0", "y0", "w"))
        y = sq[:, 0:H, :]
        ysq = sq[:, H:, :]
        kT = ph.sb("kT", [P, H, T])
        kqT = ph.sb("kqT", [P, H, 2, T])
        LA = ph.sb("LA", [T, H, 2, T])
        S = ph.sb("S", [P, NSEQ, H, DK])
        if sample:
            sT = ph.sb("sT", [P, H, 2, T])
            ux = ph.sb("ux", [T, NB, DK])
        I = inverse_buffers(ph, T)
        PS = ph.ps("PS", [P, 8, 512])
        inv = inverse_sems(ph)
        names = ("par_in setup q_in z_in gated_in spread_g gates_sum g_copied gates_exp rows_g diffed d_masked gam_done turned "
                 "squared meaned rooted normed scaled v_done t_turned t_copied gram masked st_prod st_copied ks_sum "
                 "ks_done qs_sum qs_done u0_done s_scaled w_sum w_done o_sum s_sum ux_done o_done ysq_done ym_done "
                 "y_rooted y_scaled y_done y_turned tile_done state_done s_in out").split()
        s = {n: ph.sem(n) for n in names}
        dve_step, pool_step, pace, pool_pace = (ph.sem(n) for n in ("dve_step", "pool_step", "pace", "pool_pace"))
        block = ph.block()
        ident = C["ident"]

        def tiles(eng, body):
            if sample:
                body(0)
            else:
                with eng.Fori(0, NT) as i:
                    body(i)

        def two_banks(a, rows=T):
            return PS[:rows, a:a + 2, :].rearrange("p c (h d) -> p (c h) d", d=P)

        @block.sync
        def _(sp):
            sp.dma_start(gain[:], norm_w.partition_broadcast(T)).then_inc(s["par_in"], 16)
            if sample:
                for b in range(NB):
                    sp.dma_start(S[:, b], state_in[b].rearrange("h k v -> k h v")).then_inc(s["s_in"], 16)

            def body(i):
                sp.wait_ge(s["tile_done"], i + 1)
                sp.dma_start(qf[:], qkv[:, :, bass.ds(i * P + tok0, T)].rearrange("f p t -> p f t")).then_inc(s["q_in"], 16)
                sp.dma_start(z[:], zba[bass.ds(i * P + tok0, T), 0:GDN_W]).then_inc(s["z_in"], 16)
            tiles(sp, body)
            sp.wait_ge(s["state_done"], 1 if sample else NT + 1)
            for b in range(NSEQ):
                dst = state_out[b] if sample else state_out
                sp.dma_start(dst.rearrange("h k v -> k h v"), S[:, b]).then_inc(s["out"], 16)
            sp.wait_ge(s["out"], 16 * NSEQ)

        @block.gpsimd
        def _(pool):
            setup = Chain(pool, s["setup"])
            if sample:
                setup(pool.tensor_tensor(suf[:], C["blk_low"][:T, :T], ident[:T, :T], ALU.subtract))
            else:
                setup(pool.tensor_tensor(suf[:], C["ones"][:], C["tri"][:], ALU.subtract))
            setup(pool.tensor_scalar(mneg[:], tri[:T, :T], 1.0, -NEG, ALU.subtract, ALU.mult))
            if not sample:
                setup(pool.memset(S[:], 0.0))

            def body(i):
                pool.wait_ge(s["gated_in"], i + 1)
                pool.sem_inc(pool_pace, 1)
                pool.tensor_copy(gb[:], bc(gt[:], 2, T)).then_inc(s["spread_g"], 1)
                for c in range(2):
                    pool.wait_ge(s["diffed"], i * 2 + (c + 1))
                    pool.tensor_tensor(gam[:, 4 * c:4 * c + 4, :], gam[:, 4 * c:4 * c + 4, :],
                                       bc(mneg[:], 1, GROUP), ALU.add).then_inc(s["d_masked"], 1)
                pool.wait_ge(s["meaned"], i + 1)
                pool.tensor_tensor(r16[:], m16[:], C["half"][:T, :2 * H], ALU.pow).then_inc(s["rooted"], 1)
                pool.wait_ge(s["normed"], i + 1)
                pool.tensor_tensor(kb[:], kn[:], bc(bt[:], 2, DK), ALU.mult).then_inc(s["scaled"], 1)
                pool.wait_ge(s["gates_exp"], i + 1)
                pool.tensor_tensor(ke[:], kn[:], bc(eg[:, 1, :], 2, DK), ALU.mult)
                pool.wait_ge(s["masked"], i * 2 + 2)
                inverse_pool(pool, C, I, inv, LA[:, :, 0, :], T, levels, i, pool_pace)
                pool.wait_ge(s["qs_sum"], i + 1)
                pool.tensor_tensor(S[:], S[:], bc(etot[:], 3, DK), ALU.mult).then_inc(s["s_scaled"], 1)
                pool.wait_ge(s["o_done"], i + 1)
                pool.tensor_tensor(ysq, y, y, ALU.mult).then_inc(s["ysq_done"], 1)
                pool.wait_ge(s["ym_done"], i + 1)
                pool.tensor_tensor(r16[:, 0:H], m16[:, 0:H], C["half"][:T, :H], ALU.pow).then_inc(s["y_rooted"], 1)
            tiles(pool, body)

        @block.scalar
        def _(act):
            act.sem_inc(s["tile_done"], 1)

            def body(i):
                act.wait_ge(s["g_copied"], i + 1)
                act.activation(eg[:], PS[:T, 7, 0:2 * H].rearrange("p (a h) -> p a h", a=2), ACT.Exp)
                act.activation(etot[:], PS[:, 7, 2 * H:(2 + NSEQ) * H].rearrange("p (b h) -> p b h", b=NSEQ), ACT.Exp)\
                    .then_inc(s["gates_exp"], 1)
                act.wait_ge(s["turned"], i + 1)
                act.activation(sq[:], PS[:T, 0:4, :].rearrange("p c (h d) -> p (c h) d", d=DK), ACT.Square)\
                    .then_inc(s["squared"], 1)
                for c in range(2):
                    act.wait_ge(s["d_masked"], i * 2 + (c + 1))
                    ins = act.activation(gam[:, 4 * c:4 * c + 4, :], gam[:, 4 * c:4 * c + 4, :], ACT.Exp)
                ins.then_inc(s["gam_done"], 1)
                for n in range(3):
                    act.wait_ge(s["t_turned"], i * 3 + (n + 1))
                    dst = kT[:] if n == 0 else kqT[:, :, n - 1, :]
                    act.copy(dst, two_banks(2 * n, P)[:, :, :T]).then_inc(s["t_copied"], 1)
                if sample:
                    act.wait_ge(s["st_prod"], 1)
                    act.copy(sT.rearrange("p h a t -> p h (a t)"), two_banks(6, P)).then_inc(s["st_copied"], 1)
                inverse_act(act, I, inv, PS, T, levels, i)
                act.wait_ge(s["w_sum"], i + 1)
                act.copy(w[:], two_banks(6)).then_inc(s["w_done"], 1)
                act.wait_ge(s["y_turned"], i + 1)
                act.copy(mixT[:, :, bass.ds(i * P + tok0, T)], two_banks(4, P)[:, :, :T])\
                    .then_inc(s["tile_done"], 1)
            tiles(act, body)

        @block.tensor
        def _(pe):
            if sample:
                pe.wait_ge(s["s_in"], 16 * NB)

            def body(i):
                pe.wait_ge(s["gated_in"], i + 1)
                pe.wait_ge(s["setup"], 2)
                pe.matmul(PS[:T, 7, 0:H], tri[:T, :T], gt[:], start=True, stop=True)
                pe.matmul(PS[:T, 7, H:2 * H], suf[:], gt[:], start=True, stop=True)
                pe.matmul(PS[:, 7, 2 * H:(2 + NSEQ) * H], C["ones"][:T, :], gx.rearrange("p b h -> p (b h)"),
                          start=True, stop=True).then_inc(s["gates_sum"], 1)
                pe.wait_ge(s["q_in"], i * 16 + 16)
                for f in range(3 * H):
                    mm = pe.transpose(PS[:T, f // 4, (f % 4) * P:(f % 4 + 1) * P], qf[:, f, :], ident[:])
                mm.then_inc(s["turned"], 1)
                pe.wait_ge(s["spread_g"], i + 1)
                pe.wait_ge(s["gates_exp"], i + 1)
                for c in range(2):
                    for h in range(GROUP):
                        mm = pe.matmul(PS[:T, 6 + c, h * P:h * P + T], gb[:, 4 * c + h, :], tri[:T, :T], start=True,
                                       stop=True)
                    mm.then_inc(s["rows_g"], 1)
                pe.wait_ge(s["v_done"], i + 1)
                for n, (t, ready) in enumerate(((kn, "normed"), (kb, "scaled"), (qn, "normed"))):
                    pe.wait_ge(s[ready], i + 1)
                    pe.sem_inc(pace, 1)
                    for h in range(H):
                        mm = pe.transpose(PS[:, 2 * n + h // 4, (h % 4) * P:(h % 4) * P + T], t[:, h, :], ident[:T, :T])
                    mm.then_inc(s["t_turned"], 1)
                pe.wait_ge(s["t_copied"], i * 3 + 3)
                if sample:
                    pe.wait_ge(s["diffed"], 2)
                    for b in range(NB):
                        for h in range(H):
                            o = PS[:, 6 + h // 4, (h % 4) * P:(h % 4 + 1) * P].rearrange("p (a t) -> p a t", a=2)
                            mm = pe.matmul(o[:, :, b * TS:(b + 1) * TS], S[:, b, h, :],
                                           kqT[:, h, :, b * TS:(b + 1) * TS], start=True, stop=True)
                    mm.then_inc(s["st_prod"], 1)
                    pe.wait_ge(s["st_copied"], 1)
                for gr in range(2):
                    for hh in range(GROUP):
                        h = gr * GROUP + hh
                        mm = pe.matmul(PS[:T, 4 * gr + hh // 2, (hh % 2) * 256:(hh % 2) * 256 + 2 * T], kT[:, h, :],
                                       kqT[:, h].rearrange("p a t -> p (a t)"), start=True, stop=True)
                    mm.then_inc(s["gram"], 1)
                pe.wait_ge(s["diffed"], i * 2 + 2)
                if not sample:
                    pe.wait_ge(s["state_done"], i + 1)

                def state_product(n):
                    for h in range(H):
                        o = PS[:T, 6 + h // 4, (h % 4) * P:(h % 4 + 1) * P]
                        if sample:
                            mm = pe.matmul(o, sT[:, h, n, :], ident[:], start=True, stop=True)
                        else:
                            mm = pe.matmul(o, kqT[:, h, n, :], S[:, 0, h, :], start=True, stop=True)
                    return mm
                state_product(0).then_inc(s["ks_sum"], 1)
                pe.wait_ge(s["ks_done"], i + 1)
                state_product(1).then_inc(s["qs_sum"], 1)
                pe.wait_ge(s["masked"], i * 2 + 2)
                inverse_pe(pe, C, I, inv, PS, T, levels, i)
                pe.wait_ge(s["u0_done"], i + 1)
                pe.wait_ge(inv["x_added"], i * (2 * levels) + 2 * levels)
                pe.wait_ge(s["qs_done"], i + 1)
                for h in range(H):
                    mm = pe.matmul(PS[:T, 6 + h // 4, (h % 4) * P:(h % 4 + 1) * P],
                                   I["XT"][h // GROUP][:, h % GROUP, :], u0[:, h, :], start=True, stop=True)
                mm.then_inc(s["w_sum"], 1)
                pe.wait_ge(s["w_done"], i + 1)
                for h in range(H):
                    mm = pe.matmul(PS[:T, h // 4, (h % 4) * P:(h % 4 + 1) * P], LA[:, h, 1, :], w[:, h, :],
                                   start=True, stop=True)
                mm.then_inc(s["o_sum"], 1)
                if sample:
                    for h in range(H):
                        pe.wait_ge(s["ux_done"], h + 1)
                        for half in range(2):
                            mm = pe.matmul(PS[:, 2 + half, :], ke[:, h, :],
                                           ux[:, 4 * half:4 * half + 4, :].rearrange("p b c -> p (b c)"), start=True,
                                           stop=True)
                        mm.then_inc(s["s_sum"], 1)
                else:
                    for h in range(H):
                        mm = pe.matmul(PS[:, 2 + h // 4, (h % 4) * P:(h % 4 + 1) * P], ke[:, h, :], w[:, h, :],
                                       start=True, stop=True)
                    mm.then_inc(s["s_sum"], 1)
                pe.wait_ge(s["y_done"], i + 1)
                pe.sem_inc(pace, 1)
                for h in range(H):
                    mm = pe.transpose(PS[:, 4 + h // 4, (h % 4) * P:(h % 4) * P + T], y[:, h, :], ident[:T, :T])
                mm.then_inc(s["y_turned"], 1)
            tiles(pe, body)

        @block.vector
        def _(dve):
            if not sample:
                dve.sem_inc(s["state_done"], 1)
            step = Chain(dve, dve_step, per=15 if sample else 7)
            dve.wait_ge(s["par_in"], 16)
            dve.wait_ge(s["setup"], 2 if sample else 3)

            def body(i):
                step.turn(i)
                dve.wait_ge(s["tile_done"], i + 1)
                step(dve.tensor_copy(gt[:], gate[:T, bass.ds(i + tile0, 1), :].rearrange("p o h -> p (o h)")))
                dve.tensor_scalar(bt[:], beta[:T, bass.ds(i + tile0, 1), :].rearrange("p o h -> p (o h)"), -1.0, None,
                                  ALU.mult)
                if sample:
                    ins = dve.tensor_tensor(gx[:], bc(gt[:], 1, NB), bc(C["blk"][:T, 0:T:TS], 2, H), ALU.mult)
                else:
                    ins = dve.tensor_copy(gx[:, 0], gt[:])
                ins.then_inc(s["gated_in"], 1)
                dve.wait_ge(s["gates_sum"], i + 1)
                dve.tensor_copy(Gs[:], PS[:T, 7, 0:H]).then_inc(s["g_copied"], 1)
                dve.wait_ge(s["squared"], i + 1)
                step(dve.tensor_reduce(s16[:], sq[:], AX.X, ALU.add))
                dve.tensor_scalar(m16[:], s16[:], 1e-6, None, ALU.add).then_inc(s["meaned"], 1)
                for c in range(2):
                    dve.wait_ge(s["rows_g"], i * 2 + (c + 1))
                    dve.tensor_tensor(gam[:, 4 * c:4 * c + 4, :],
                                      PS[:T, 6 + c, :].rearrange("p (h t) -> p h t", h=GROUP)[:, :, :T],
                                      bc(Gs[:, 4 * c:4 * c + 4], 2, T), ALU.subtract).then_inc(s["diffed"], 1)
                dve.wait_ge(s["rooted"], i + 1)
                step(dve.tensor_scalar(r16[:, 0:H], r16[:, 0:H], DK ** -0.5, None, ALU.mult))
                rows = PS[:T, 0:6, :].rearrange("p c (h d) -> p (c h) d", d=DK)
                dve.tensor_tensor(qn[:], rows[:, 0:H, :], bc(r16[:, 0:H], 2, DK), ALU.mult)
                dve.tensor_tensor(kn[:], rows[:, H:2 * H, :], bc(r16[:, H:], 2, DK), ALU.mult).then_inc(s["normed"], 1)
                step(dve.tensor_tensor(vb[:], rows[:, 2 * H:, :], bc(bt[:], 2, DK), ALU.mult))
                dve.sem_inc(s["v_done"], 1)
                dve.wait_ge(s["gam_done"], i + 1)
                for gr in range(2):
                    dve.wait_ge(s["gram"], i * 2 + (gr + 1))
                    src = PS[:T, 4 * gr:4 * gr + 2, :].rearrange("p c (m x) -> p (c m) x", m=2)[:, :, :2 * T]
                    dve.tensor_tensor(LA[:, 4 * gr:4 * gr + 4], src.rearrange("p h (a t) -> p h a t", a=2),
                                      bc(gam[:, 4 * gr:4 * gr + 4, :], 2, 2), ALU.mult).then_inc(s["masked"], 1)
                dve.wait_ge(s["ks_sum"], i + 1)
                eG = bc(eg[:, 0, :], 2, DK)
                dve.tensor_tensor(u0[:], two_banks(6), eG, ALU.mult).then_inc(s["ks_done"], 1)
                dve.wait_ge(s["ks_done"], i + 1)
                dve.tensor_tensor(u0[:], u0[:], vb[:], ALU.subtract).then_inc(s["u0_done"], 1)
                dve.wait_ge(s["qs_sum"], i + 1)
                dve.tensor_tensor(y0[:], two_banks(6), eG, ALU.mult).then_inc(s["qs_done"], 1)
                inverse_dve(dve, C, I, inv, PS, T, levels, i)
                dve.wait_ge(s["o_sum"], i + 1)
                dve.tensor_tensor(y, two_banks(0), y0[:], ALU.add).then_inc(s["o_done"], 1)
                dve.wait_ge(s["s_scaled"], i + 1)
                if sample:
                    seg = bc(C["blk"][:T, 0:T:TS], 2, DK)
                    for h in range(H):
                        step(dve.tensor_tensor(ux[:], bc(w[:, h, :], 1, NB), seg, ALU.mult))
                        dve.sem_inc(s["ux_done"], 1)
                        dve.wait_ge(s["s_sum"], h + 1)
                        ins = dve.tensor_tensor(S[:, :, h, :], two_banks(2, P), S[:, :, h, :], ALU.add)
                    ins.then_inc(s["state_done"], 1)
                else:
                    dve.wait_ge(s["s_sum"], i + 1)
                    dve.tensor_tensor(S[:, 0], two_banks(2, P), S[:, 0], ALU.add).then_inc(s["state_done"], 1)
                dve.wait_ge(s["ysq_done"], i + 1)
                step(dve.tensor_reduce(s16[:, 0:H], ysq, AX.X, ALU.add))
                dve.tensor_scalar(m16[:, 0:H], s16[:, 0:H], 1.0 / DK, EPS, ALU.mult, ALU.add).then_inc(s["ym_done"], 1)
                dve.wait_ge(s["y_rooted"], i + 1)
                step(dve.tensor_tensor(y, y, bc(r16[:, 0:H], 2, DK), ALU.mult))
                step(dve.tensor_tensor(y, y, bc(gain[:], 1, H), ALU.mult))
                dve.wait_ge(s["z_in"], i * 16 + 16)
                dve.tensor_tensor(y, y, z.rearrange("p (h d) -> p h d", h=H), ALU.mult).then_inc(s["y_done"], 1)
                step.close()
            tiles(dve, body)


def trunk(nc, I, O, scratch):
    pf, prw, qkv, zba = scratch
    Phase.used = []
    with Phase(nc, "trunk") as top:
        C = {k: top.sb(k, [P, P]) for k in ("ident", "ones", "tri", "half", "blk", "blk_low", "blk_tri")}
        C["join"] = top.sb("join", [P, 7, P])
        xT = top.sb("xT", [P, KD, NTOK])
        build_constants(nc, C)
        build_join(nc, C)
        load_x(nc, C, I["x"], xT)

        def parts(ph):
            return (ph.sb(n, [P, KD, NTOK], F32R) for n in ("high", "low"))

        with Phase(nc, "even_in") as ph:
            xh, xl = parts(ph)
            norm(nc, C, "n0", xT, I["norm_mix"][0], xh, xl)
            w = I["ev_w_in"][0]
            zero_row(nc, prw)
            project_rows(nc, "p_qkv", xh, xl, w, 0, FOX_W, 3, pf, 0)
            project_rows(nc, "p_og", xh, xl, w, 3 * FOX_W, FOX_W, 1, pf, 3 * FOX_W, func=ACT.Sigmoid)
            project_rows(nc, "p_fl", xh, xl, w, 4 * FOX_W, H, 1, pf, 4 * FOX_W)
            project_rows(nc, "p_rw", xh, xl, w, FOX_COLS, RW_COLS // 4, 4, prw[1:, :], 0)
        with Phase(nc, "even_mix") as ph:
            foxT = ph.sb("foxT", [P, KD // 2, NTOK])
            with Phase(nc, "fox") as fx:
                sog = fx.sb("sog", [P, NT + 1, FOX_W])
                qTs, kTs = fx.sb("qTs", [P, 4, NS]), fx.sb("kTs", [P, 4, NS])
                lfs = fx.sb("lfs", [NS, H])
                with Phase(nc, "fox_p") as fp:
                    qkA = fp.sb("qkA", [P, 2 * H, SEQ])
                    fox_prep(nc, C, pf, I["fox_q_gain"][0], I["fox_k_gain"][0], I["fox_b_f"][0], qkA, sog, qTs, kTs,
                             lfs, O["fk"], O["fv"], O["flf"])
                    fox_prompt(nc, C, qkA, sog, O["fv"], foxT)
                fox_sample(nc, C, qTs, kTs, lfs, sog, O["fv"], I["cache_fox_k"], I["cache_fox_v"],
                           I["cache_fox_logf"], I["page_table"], foxT)
            rwT = ph.sb("rwT", [P, KD // 2, NTOK])
            W = {n: I["rw_" + n][0] for n in ("mu", "w0", "w2", "a0", "a2", "g2", "k_k", "k_a", "ln_w", "ln_b")}
            W["r_k"] = I["rw_r_k"][0].rearrange("h d -> (h d)")
            rwkv(nc, C, False, prw, None, None, W, rwT, O["rw_p"], O["sh_p"])
            rwkv(nc, C, True, prw, I["state_rwkv"][0], I["state_rwkv_shift"][0], W, rwT, O["rw_s"], O["sh_s"])
            mh, ml = parts(ph)
            split_all(nc, "mix0", (foxT, rwT), mh, ml)
            project_back(nc, "back0", mh, ml, I["ev_w_out"][0], xT)
        conv_ffn(nc, C, 0, I, O, xT, parts)
        with Phase(nc, "odd_in") as ph:
            xh, xl = parts(ph)
            norm(nc, C, "n1", xT, I["norm_mix"][1], xh, xl)
            w = I["od_w_in"][0]
            project_rows(nc, "p_z", xh, xl, w, GDN_QKV, 512, 2, zba, 0, func=ACT.Silu)
            project_rows(nc, "p_ba", xh, xl, w, GDN_QKV + GDN_W, 2 * H, 1, zba, GDN_W)
            n, T1 = GDN_QKV // P, 3
            prev = ph.sb("prev", [P, n, NB * T1])
            tail = ph.sb("tail", [P, n, (NB + 1) * T1])
            taps = ph.sb("taps", [P, n, T1 + 1])
            load_prev(nc, C, "gprev", I["state_gdn_conv"][0], n, T1, prev, I["gdn_conv_w"][0], T1 + 1, taps, None)
            conv_up(nc, C, "gqkv", xh, xl, w, T1 + 1, taps, prev, tail, dst=qkv)
            store_tail(nc, C, "gtail", tail, n, T1, O["gcv_p"], O["gcv_s"])
        with Phase(nc, "odd_mix") as ph:
            mixT = ph.sb("mixT", [P, KD, NTOK])
            with Phase(nc, "odd_gdn") as pg:
                beta, gate = (pg.sb(n, [P, NT + 1, H]) for n in ("beta", "gate"))
                gdn_gates(nc, C, zba, I["gdn_A_log"][0], I["gdn_dt_bias"][0], beta, gate)
                gdn(nc, C, False, qkv, zba, beta, gate, I["gdn_norm_w"][0], None, mixT, O["gdn_p"])
                gdn(nc, C, True, qkv, zba, beta, gate, I["gdn_norm_w"][0], I["state_gdn"][0], mixT, O["gdn_s"])
            mh, ml = parts(ph)
            split_all(nc, "mix1", (mixT,), mh, ml)
            project_back(nc, "back1", mh, ml, I["od_w_out"][0], xT)
        conv_ffn(nc, C, 1, I, O, xT, parts)
        store_y(nc, C, xT, I["norm_out"], O["y"])


def zero_row(nc, prw):
    with Phase(nc, "zero") as ph:
        z = ph.sb("z", [1, RW_COLS])
        made, out = ph.sem("made"), ph.sem("out")
        block = ph.block()

        @block.gpsimd
        def _(pool):
            pool.memset(z[:], 0.0).then_inc(made, 1)

        @block.sync
        def _(sp):
            sp.wait_ge(made, 1)
            sp.dma_start(prw[0:1, :], z[:]).then_inc(out, 16)
            sp.wait_ge(out, 16)


def conv_ffn(nc, C, layer, I, O, xT, parts):
    with Phase(nc, f"ffn{layer}") as ph:
        xh, xl = parts(ph)
        norm(nc, C, f"nf{layer}", xT, I["norm_ffn"][layer], xh, xl)
        n, T1 = 2 * NF, 2
        prev = ph.sb("prev", [P, n, NB * T1])
        tail = ph.sb("tail", [P, n, (NB + 1) * T1])
        taps = ph.sb("taps", [P, n, T1 + 2])
        load_prev(nc, C, f"fprev{layer}", I["state_ffn_conv"][layer], n, T1, prev, I["ffn_conv_w"][layer], T1 + 1,
                  taps, I["ffn_conv_b"][layer])
        conv_up(nc, C, f"fup{layer}", xh, xl, I["ffn_w_up"][layer], T1 + 1, taps, prev, tail,
                wd=I["ffn_w_down"][layer], xT=xT)
        store_tail(nc, C, f"ftail{layer}", tail, n, T1, O["fcv_p"][layer], O["fcv_s"][layer])


_INS = ["x", "cache_fox_k", "cache_fox_v", "cache_fox_logf", "state_rwkv", "state_rwkv_shift", "state_gdn",
        "state_gdn_conv", "state_ffn_conv", "page_table", "norm_mix", "norm_ffn", "norm_out", "ev_w_in", "ev_w_out",
        "fox_b_f", "fox_q_gain", "fox_k_gain", "rw_mu", "rw_w0", "rw_w2", "rw_a0", "rw_a2", "rw_g2", "rw_k_k",
        "rw_k_a", "rw_r_k", "rw_ln_w", "rw_ln_b", "od_w_in", "od_w_out", "gdn_conv_w", "gdn_A_log", "gdn_dt_bias",
        "gdn_norm_w", "ffn_w_up", "ffn_conv_w", "ffn_conv_b", "ffn_w_down"]
_OUTS = {"y": (NTOK, D), "fk": (NTOK, FOX_W), "fv": (NTOK, FOX_W), "flf": (NTOK, H), "rw_p": (H, DH, DH),
         "rw_s": (NB, H, DH, DH), "sh_p": (1, RW_COLS), "sh_s": (NB, RW_COLS), "gdn_p": (H, DK, DK),
         "gdn_s": (NB, H, DK, DK), "gcv_p": (3, GDN_QKV), "gcv_s": (NB, 3, GDN_QKV), "fcv_p": (2, 2, 2 * D_FF),
         "fcv_s": (2, NB, 2, 2 * D_FF)}


def kernel(**inputs):
    import numpy as np
    import concourse.bacc as bacc
    from concourse.bass_utils import run_bass_kernel_spmd

    arrays = {n: np.ascontiguousarray(inputs[n]) for n in _INS if n != "x"}
    arrays["x"] = np.concatenate([np.asarray(inputs["x_prompt"]).reshape(SEQ, D),
                                  np.asarray(inputs["x_sample"]).reshape(NS, D)])
    for n in ("cache_fox_k", "cache_fox_v"):
        arrays[n] = arrays[n].reshape(N_POOL, PAGE, FOX_W)
    arrays["cache_fox_logf"] = arrays["cache_fox_logf"].reshape(N_POOL, PAGE, H)

    nc = bacc.Bacc("TRN2", target_bir_lowering=False, num_devices=1)
    I = {n: nc.dram_tensor("in_" + n, arrays[n].shape, mybir.dt.from_np(arrays[n].dtype), kind="ExternalInput").ap()
         for n in _INS}
    O = {n: nc.dram_tensor("out_" + n, shape, F32, kind="ExternalOutput").ap() for n, shape in _OUTS.items()}
    scratch = [nc.dram_tensor(n, shape, F32, kind="Internal").ap() for n, shape in (
        ("pf", (NTOK, FOX_COLS)), ("prw", (NTOK + 1, RW_COLS)), ("qkv", (GDN_QKV // P, P, NTOK)),
        ("zba", (NTOK, GDN_W + 2 * H)))]
    trunk(nc, I, O, scratch)
    r = run_bass_kernel_spmd(nc, [{"in_" + n: a for n, a in arrays.items()}], core_ids=[0]).results[0]
    r = {n: r["out_" + n] for n in _OUTS}

    def both(a, *tail):
        return a[:SEQ].reshape(1, 1, SEQ, *tail), a[SEQ:].reshape(1, NB, TS, *tail)
    (fk_p, fk_s), (fv_p, fv_s), (fl_p, fl_s) = both(r["fk"], H, DH), both(r["fv"], H, DH), both(r["flf"], H)
    return (r["y"][:SEQ].reshape(1, SEQ, D), r["y"][SEQ:].reshape(NB, TS, D), fk_p, fv_p, fl_p, fk_s, fv_s, fl_s,
            r["rw_p"][None, None], r["rw_s"][None], r["sh_p"][None], r["sh_s"][None],
            r["gdn_p"][None, None], r["gdn_s"][None], r["gcv_p"][None, None], r["gcv_s"][None],
            r["fcv_p"][:, None], r["fcv_s"])
```

```python
from contextlib import ExitStack

import concourse.bass as bass
from concourse import mybir

F32 = mybir.dt.float32
F32R = mybir.dt.float32r
I32 = mybir.dt.int32
ACT = mybir.ActivationFunctionType
ALU = mybir.AluOpType
AX = mybir.AxisListType

P = 128
D = 1024
KD = D // P
SEQ = 1024
NB, TS = 8, 8
NS = NB * TS
NTOK = SEQ + NS
NT = SEQ // P
GROUPS = [(0, 364), (364, 364), (728, 360)]
GW = 364
H, DH = 8, 64
FOX_W = H * DH
FOX_COLS = 4 * FOX_W + H
RW_W = H * DH
R_W, R_A, R_G = 64, 64, 128
RW_COLS = 3 * RW_W + R_W + R_A + R_G
EV_IN = FOX_COLS + RW_COLS
PAST, PAGE = 1024, 128
NPG = PAST // PAGE
N_POOL = NB * NPG + NB * NPG // 4
DK = 128
GDN_W = H * DK
GDN_QKV = 3 * GDN_W
OD_IN = GDN_QKV + GDN_W + 2 * H
D_FF = 2816
NF = D_FF // P
EPS = 1e-6
RW_GN_EPS = 64e-5
RW_DECAY = -0.6065306597126334
NEG = -1e30


class Phase:

    used = []

    def __init__(self, nc, name):
        self.nc, self.name, self.ctx = nc, name, ExitStack()
        self.sems = []

    def __enter__(self):
        self.ctx.__enter__()
        return self

    def __exit__(self, *e):
        Phase.used += self.sems
        return self.ctx.__exit__(*e)

    def sb(self, name, shape, dt=F32):
        return self.ctx.enter_context(self.nc.sbuf_tensor(f"{self.name}_{name}", shape, dt))

    def ps(self, name, shape, dt=F32):
        return self.ctx.enter_context(self.nc.psum_tensor(f"{self.name}_{name}", shape, dt))

    def sem(self, name):
        self.sems.append(self.nc.alloc_semaphore(name=f"{self.name}_{name}"))
        return self.sems[-1]

    def block(self):
        if Phase.used:
            self.nc.clear_and_free_semaphores(Phase.used)
            Phase.used = []
        return self.ctx.enter_context(self.nc.Block())


class Chain:

    def __init__(self, eng, sem, per=0):
        self.eng, self.sem, self.per, self.n, self.base = eng, sem, per, 0, 0

    def turn(self, i):
        self.base, self.n = i * self.per, 0

    def __call__(self, ins):
        self.n += 1
        ins.then_inc(self.sem, 1)
        self.eng.wait_ge(self.sem, self.base + self.n)

    def close(self):
        assert self.n == self.per, (self.n, self.per)


def bc(ap, axis, n):
    shape = list(ap.shape)
    new = ap.unsqueeze(axis)
    shape.insert(axis, n)
    return new.to_broadcast(shape)


def build_constants(nc, C):
    with Phase(nc, "const") as ph:
        s = ph.sem("made")
        block = ph.block()

        @block.gpsimd
        def _(pool):
            step = Chain(pool, s)
            step(pool.memset(C["ident"][:], 0.0))
            step(pool.affine_select(C["ident"][:], C["ident"][:], [[-1, P]], ALU.not_equal, 1.0,
                                    base=0, channel_multiplier=1))
            step(pool.memset(C["ones"][:], 1.0))
            step(pool.affine_select(C["tri"][:], C["ones"][:], [[1, P]], ALU.is_ge, 0.0,
                                    base=0, channel_multiplier=-1))
            step(pool.memset(C["half"][:], -0.5))
            view = C["blk"][:NS, :NS].rearrange("p (a t) -> p a t", t=TS)
            step(pool.memset(C["blk"][:], 1.0))
            step(pool.affine_select(view, view, [[-TS, NB], [0, TS]], ALU.is_ge, 0.0, base=0, channel_multiplier=1))
            step(pool.affine_select(view, view, [[TS, NB], [0, TS]], ALU.is_ge, 0.0, base=TS - 1,
                                    channel_multiplier=-1))
            step(pool.affine_select(C["blk_low"][:NS, :NS], C["blk"][:NS, :NS], [[-1, NS]], ALU.is_ge, 0.0, base=0,
                                    channel_multiplier=1))
            step(pool.affine_select(C["blk_tri"][:NS, :NS], C["blk"][:NS, :NS], [[1, NS]], ALU.is_ge, 0.0, base=0,
                                    channel_multiplier=-1))


def load_x(nc, C, x, xT):
    with Phase(nc, "ldx") as ph:
        xt = ph.sb("xt", [P, 2, D])
        pt = ph.ps("pt", [P, 2, KD, P])
        x_in = [ph.sem(f"x_in{b}") for b in range(2)]
        turned, stored = ph.sem("turned"), ph.sem("stored")
        block = ph.block()

        @block.sync
        def _(sp):
            for i in range(NT + 1):
                rows = P if i < NT else NS
                if i >= 2:
                    sp.wait_ge(turned, i - 1)
                sp.dma_start(xt[:rows, i % 2, :], x[i * P:i * P + rows, :]).then_inc(x_in[i % 2], 16)

        @block.tensor
        def _(pe):
            for i in range(NT + 1):
                rows = P if i < NT else NS
                pe.wait_ge(x_in[i % 2], 16 * (i // 2 + 1))
                if i >= 2:
                    pe.wait_ge(stored, i - 1)
                for k in range(KD):
                    mm = pe.transpose(pt[:, i % 2, k, :rows], xt[:rows, i % 2, k * P:(k + 1) * P],
                                      C["ident"][:rows, :rows])
                mm.then_inc(turned, 1)

        @block.scalar
        def _(act):
            for i in range(NT + 1):
                rows = P if i < NT else NS
                act.wait_ge(turned, i + 1)
                act.copy(xT[:, :, i * P:i * P + rows], pt[:, i % 2, :, :rows]).then_inc(stored, 1)


def store_y(nc, C, xT, gain, y):
    with Phase(nc, "sty") as ph:
        pt = ph.ps("pt", [P, 2, KD, P])
        rows_sb = ph.sb("rows", [P, 2, D])
        junk = ph.sb("junk", [P, D])
        gb = ph.sb("gain_rows", [P, D])
        ss, ms, rstd = (ph.sb(n, [P, NT + 1]) for n in ("ss", "ms", "rstd"))
        gain_in, turned, squared, meaned, rooted, scaled, done = (
            ph.sem(n) for n in ("gain_in", "turned", "squared", "meaned", "rooted", "scaled", "done"))
        out = [ph.sem(f"out{b}") for b in range(2)]
        block = ph.block()
        N = NT + 1

        @block.sync
        def _(sp):
            sp.dma_start(gb[:], gain.unsqueeze(0).partition_broadcast(P)).then_inc(gain_in, 16)
            for i in range(N):
                rows = P if i < NT else NS
                sp.wait_ge(done, i + 1)
                sp.dma_start(y[i * P:i * P + rows, :], rows_sb[:rows, i % 2, :]).then_inc(out[i % 2], 16)
            sp.wait_ge(out[0], 16 * ((N + 1) // 2))
            sp.wait_ge(out[1], 16 * (N // 2))

        @block.tensor
        def _(pe):
            for i in range(N):
                rows = P if i < NT else NS
                if i >= 2:
                    pe.wait_ge(scaled, i - 1)
                for k in range(KD):
                    mm = pe.transpose(pt[:rows, i % 2, k, :], xT[:, k, i * P:i * P + rows], C["ident"][:])
                mm.then_inc(turned, 1)

        @block.scalar
        def _(act):
            for i in range(N):
                rows = P if i < NT else NS
                act.wait_ge(turned, i + 1)
                if i:
                    act.wait_ge(squared, i)
                act.activation(junk[:rows, :], pt[:rows, i % 2].rearrange("p k t -> p (k t)"), ACT.Square,
                               accum_out=ss[:rows, i:i + 1]).then_inc(squared, 1)
                act.wait_ge(rooted, i + 1)
                if i >= 2:
                    act.wait_ge(out[i % 2], 16 * (i // 2))
                act.activation(rows_sb[:rows, i % 2, :], pt[:rows, i % 2].rearrange("p k t -> p (k t)"),
                               ACT.Copy, scale=rstd[:rows, i:i + 1]).then_inc(scaled, 1)

        @block.gpsimd
        def _(pool):
            for i in range(N):
                rows = P if i < NT else NS
                pool.wait_ge(meaned, i + 1)
                pool.tensor_tensor(rstd[:rows, i:i + 1], ms[:rows, i:i + 1], C["half"][:rows, 0:1],
                                   ALU.pow).then_inc(rooted, 1)

        @block.vector
        def _(dve):
            dve.wait_ge(gain_in, 16)
            for i in range(N):
                rows = P if i < NT else NS
                dve.wait_ge(squared, i + 1)
                dve.tensor_scalar(ms[:rows, i:i + 1], ss[:rows, i:i + 1], 1.0 / D, EPS, ALU.mult,
                                  ALU.add).then_inc(meaned, 1)
                dve.wait_ge(scaled, i + 1)
                dve.tensor_tensor(rows_sb[:rows, i % 2, :], rows_sb[:rows, i % 2, :], gb[:rows, :],
                                  ALU.mult).then_inc(done, 1)


def norm(nc, C, name, xT, gain, xh, xl, conv=None):
    with Phase(nc, name) as ph:
        N = NT + 1
        xn = ph.sb("xn", [P, KD, NTOK])
        ms, rstd = ph.sb("ms", [P, N]), ph.sb("rstd", [P, N])
        diag = ph.sb("diag", [P, N, P])
        g = ph.sb("g", [P, KD])
        sums = ph.ps("sums", [P, 512])
        segs = [(c, min(512, NTOK - c)) for c in range(0, NTOK, 512)]
        spread = [ph.ps(f"spread{b}", [P, 512]) for b in range(len(segs))]
        (g_in, filled, squared_a, squared_d, summed, meaned, rooted, diagonal, spreads, normed, high, low) = (
            ph.sem(n) for n in ("g_in", "filled", "squared_a", "squared_d", "summed", "meaned", "rooted",
                                "diagonal", "spreads", "normed", "high", "low"))
        turn = turn_conv(nc, C, ph, *conv) if conv else None
        block = ph.block()
        HK = KD // 2

        @block.sync
        def _(sp):
            with nc.allow_non_contiguous_dma(reason="a gain per partition"):
                sp.dma_start(g[:], gain.rearrange("(k p) -> p k", p=P)).then_inc(g_in, 16)
            if conv:
                turn["sync"](sp)

        @block.scalar
        def _(act):
            for c0, w in segs:
                act.activation(xn[:, :HK, c0:c0 + w], xT[:, :HK, c0:c0 + w], ACT.Square).then_inc(squared_a, 1)
            for i, (c0, w) in enumerate(segs):
                act.wait_ge(normed, i + 1)
                act.copy(xh[:, :, c0:c0 + w], xn[:, :, c0:c0 + w]).then_inc(high, 1)
            if conv:
                turn["scalar"](act)

        @block.tensor
        def _(pe):
            for t in range(N):
                rows = P if t < NT else NS
                if t % 4 == 0:
                    pe.wait_ge(squared_a, t // 4 + 1)
                    pe.wait_ge(squared_d, t // 4 + 1)
                for k in range(KD):
                    mm = pe.matmul(sums[:rows, t:t + 1], xn[:, k, t * P:t * P + rows], C["ones"][:, 0:1],
                                   start=(k == 0), stop=(k == KD - 1))
            mm.then_inc(summed, 1)
            pe.wait_ge(diagonal, 1)
            for t in range(N):
                rows = P if t < NT else NS
                mm = pe.matmul(spread[t // 4][:, t % 4 * P:t % 4 * P + rows], C["ones"][:rows, :],
                               diag[:rows, t, :rows], start=True, stop=True)
                if t % 4 == 3 or t == N - 1:
                    mm.then_inc(spreads, 1)
            if conv:
                turn["tensor"](pe)

        @block.gpsimd
        def _(pool):
            pool.memset(ms[:], 1.0).then_inc(filled, 1)
            pool.wait_ge(meaned, 1)
            pool.tensor_tensor(rstd[:], ms[:], C["half"][:, :N], ALU.pow).then_inc(rooted, 1)

        @block.vector
        def _(dve):
            for c0, w in segs:
                dve.tensor_tensor(xn[:, HK:, c0:c0 + w], xT[:, HK:, c0:c0 + w], xT[:, HK:, c0:c0 + w],
                                  ALU.mult).then_inc(squared_d, 1)
            dve.wait_ge(filled, 1)
            dve.wait_ge(summed, 1)
            dve.tensor_scalar(ms[:, :NT], sums[:, :NT], 1.0 / D, EPS, ALU.mult, ALU.add)
            dve.tensor_scalar(ms[:NS, NT:], sums[:NS, NT:N], 1.0 / D, EPS, ALU.mult, ALU.add).then_inc(meaned, 1)
            dve.wait_ge(rooted, 1)
            dve.tensor_tensor(diag[:], bc(C["ident"][:], 1, N), bc(rstd[:], 2, P), ALU.mult).then_inc(diagonal, 1)
            dve.wait_ge(g_in, 16)

            def low_part(i):
                c0, w = segs[i]
                dve.wait_ge(high, i + 1)
                dve.tensor_tensor(xl[:, :, c0:c0 + w], xn[:, :, c0:c0 + w], xh[:, :, c0:c0 + w],
                                  ALU.subtract).then_inc(low, 1)
            for i, (c0, w) in enumerate(segs):
                dve.wait_ge(spreads, i + 1)
                for k in range(KD):
                    ins = dve.scalar_tensor_tensor(xn[:, k, c0:c0 + w], xT[:, k, c0:c0 + w], g[:, k:k + 1],
                                                   spread[i][:, :w], ALU.mult, ALU.mult)
                ins.then_inc(normed, 1)
                if i:
                    low_part(i - 1)
            low_part(len(segs) - 1)


def project_rows(nc, name, xh, xl, w, cw, n, dst):
    with Phase(nc, name) as ph:
        loops, ragged = divmod(n, 2)
        NBUF, NACC = 2, 3
        ws = ph.sb("ws", [P, KD, cw])
        wh = ph.sb("wh", [P, NBUF, KD, cw], F32R)
        wl = ph.sb("wl", [P, NBUF, KD, cw], F32R)
        o = ph.sb("o", [P, NACC, cw])
        acc = [ph.ps(f"acc{b}", [P, 512]) for b in range(NACC)]
        w_in = ph.sem("w_in")
        high, low, summed, evicted, pace = (ph.sem(s) for s in ("high", "low", "summed", "evicted", "pace"))
        out = [ph.sem(f"out{b}") for b in range(NACC)]
        block = ph.block()
        wv = w.rearrange("(k p) c -> p k c", p=P)
        N = NT + 1

        def chunks(eng, body):
            if loops > 1:
                with eng.Fori(0, loops) as j:
                    for b in range(2):
                        body(j * 2 + b, b, j)
            elif loops:
                body(0, 0, 0)
                body(1, 1, 0)
            if ragged:
                body(n - 1, 0, loops)

        @block.sync
        def _(sp):
            def body(c, b, j):
                sp.wait_ge(low, c + 1)
                sp.dma_start(ws[:], wv[:, :, bass.ds(c * cw, cw)]).then_inc(w_in, 16)
            chunks(sp, body)

        @block.gpsimd
        def _(pool):
            pool.sem_inc(low, 1)

            def body(c, b, j):
                pool.wait_ge(w_in, c * 16 + 16)
                pool.wait_ge(summed, c * N + N)
                pool.sem_inc(pace, 1)
                pool.tensor_copy(wh[:, b], ws[:]).then_inc(high, 1)
                pool.wait_ge(high, c + 1)
                pool.tensor_tensor(wl[:, b], ws[:], wh[:, b], ALU.subtract).then_inc(low, 1)
            chunks(pool, body)

        @block.tensor
        def _(pe):
            pe.sem_inc(summed, NBUF * N)

            def body(c, b, j):
                pe.wait_ge(low, c + 2)
                for t in range(N):
                    rows = P if t < NT else NS
                    cols = slice(t * P, t * P + rows)
                    ps = acc[t % NACC][:rows, :cw]
                    pe.wait_ge(evicted, c * N + (t + 1))
                    for k in range(KD):
                        pe.matmul(ps, xh[:, k, cols], wh[:, b, k], start=(k == 0), stop=False)
                        pe.matmul(ps, xh[:, k, cols], wl[:, b, k], start=False, stop=False)
                        mm = pe.matmul(ps, xl[:, k, cols], wh[:, b, k], start=False, stop=(k == KD - 1))
                    mm.then_inc(summed, 1)
            chunks(pe, body)

        def free_buffers(eng):
            eng.sem_inc(evicted, NACC)
            for b in range(NACC):
                eng.sem_inc(out[b], 16)

        def evict(eng, c, t):
            rows = P if t < NT else NS
            eng.wait_ge(summed, c * N + (NBUF * N + t + 1))
            eng.wait_ge(out[t % NACC], c * (16 * N // NACC) + (16 * (t // NACC) + 16))
            dst_, src = o[:rows, t % NACC, :], acc[t % NACC][:rows, :cw]
            eng.tensor_copy(dst_, src).then_inc(evicted, 1)

        @block.vector
        def _(dve):
            free_buffers(dve)

            def body(c, b, j):
                for t in range(N):
                    evict(dve, c, t)
            chunks(dve, body)

        @block.scalar
        def _(act):
            def body(c, b, j):
                for t in range(N):
                    rows = P if t < NT else NS
                    act.wait_ge(evicted, c * N + (NACC + t + 1))
                    act.dma_start(dst[t * P:t * P + rows, bass.ds(c * cw, cw)],
                                  o[:rows, t % NACC, :]).then_inc(out[t % NACC], 16)
            chunks(act, body)
            for b in range(NACC):
                act.wait_ge(out[b], 16 * N // NACC * n + 16)


def project_back(nc, name, srcs, mh, ml, w, xT):
    with Phase(nc, name) as ph:
        G = len(GROUPS)
        ws = ph.sb("ws", [P, 2, KD, P])
        wh = ph.sb("wh", [P, 2, KD, P], F32R)
        wl = ph.sb("wl", [P, 2, KD, P], F32R)
        acc = [ph.ps(f"acc{b}", [P, 512]) for b in range(2 * G)]
        w_in = [ph.sem(f"w_in{b}") for b in range(2)]
        high, low, summed, added, pace = (ph.sem(n) for n in ("high", "low", "summed", "added", "pace"))
        m_high, m_low = ph.sem("m_high"), ph.sem("m_low")
        block = ph.block()
        wv = w.rearrange("(k p) c -> p k c", p=P)

        def mix_tiles(c0, w_):
            n = KD // len(srcs)
            return [(slice(s * n, (s + 1) * n), src[:, :, c0:c0 + w_]) for s, src in enumerate(srcs)]

        def tiles(eng, body):
            with eng.Fori(0, KD // 2) as j:
                for b in range(2):
                    body(j * 2 + b, b, j)

        @block.sync
        def _(sp):
            def body(c, b, j):
                sp.wait_ge(low, c + 1)
                sp.dma_start(ws[:, b], wv[:, :, bass.ds(c * P, P)]).then_inc(w_in[b], 16)
            tiles(sp, body)

        @block.gpsimd
        def _(pool):
            pool.sem_inc(low, 2)

            def body(c, b, j):
                pool.wait_ge(w_in[b], j * 16 + 16)
                pool.wait_ge(summed, c * G + G)
                pool.sem_inc(pace, 1)
                pool.tensor_copy(wh[:, b], ws[:, b]).then_inc(high, 1)
                pool.wait_ge(high, c + 1)
                pool.tensor_tensor(wl[:, b], ws[:, b], wh[:, b], ALU.subtract).then_inc(low, 1)
            tiles(pool, body)

        @block.tensor
        def _(pe):
            pe.sem_inc(summed, 2 * G)

            def body(c, b, j):
                pe.wait_ge(low, c + 3)
                for g, (c0, w_) in enumerate(GROUPS):
                    pe.wait_ge(m_low, g + 1)
                    pe.wait_ge(added, c * G + (g + 1))
                    ps = acc[G * b + g][:, :w_]
                    for k in range(KD):
                        pe.matmul(ps, wh[:, b, k], mh[:, k, c0:c0 + w_], start=(k == 0), stop=False)
                        pe.matmul(ps, wh[:, b, k], ml[:, k, c0:c0 + w_], start=False, stop=False)
                        mm = pe.matmul(ps, wl[:, b, k], mh[:, k, c0:c0 + w_], start=False, stop=(k == KD - 1))
                    mm.then_inc(summed, 1)
            tiles(pe, body)

        @block.scalar
        def _(act):
            for c0, w_ in GROUPS:
                for k, src in mix_tiles(c0, w_):
                    ins = act.copy(mh[:, k, c0:c0 + w_], src)
                ins.then_inc(m_high, 1)

        @block.vector
        def _(dve):
            dve.sem_inc(added, 2 * G)
            for g, (c0, w_) in enumerate(GROUPS):
                dve.wait_ge(m_high, g + 1)
                for k, src in mix_tiles(c0, w_):
                    ins = dve.tensor_tensor(ml[:, k, c0:c0 + w_], src, mh[:, k, c0:c0 + w_], ALU.subtract)
                ins.then_inc(m_low, 1)

            def body(c, b, j):
                for g, (c0, w_) in enumerate(GROUPS):
                    dve.wait_ge(summed, c * G + (2 * G + g + 1))
                    x = xT[:, bass.ds(c, 1), c0:c0 + w_].rearrange("p o t -> p (o t)")
                    dve.tensor_tensor(x, acc[G * b + g][:, :w_], x, ALU.add).then_inc(added, 1)
            tiles(dve, body)


def turn_conv(nc, C, ph, state, conv_w, conv_b, T1, prev, cw_sb):
    rows, taps = NB * T1, T1 + 1
    n_tiles = prev.shape[1]
    nw = taps + (1 if conv_b is not None else 0)
    per = 512 // rows
    banks = -(-n_tiles // per)
    assert n_tiles * nw <= 512
    st = ph.sb("st", [rows, n_tiles * P])
    wr = ph.sb("wr", [nw, n_tiles * P])
    pp = ph.ps("pp", [P, banks * 512])
    pw = ph.ps("pw", [P, 512])
    got, turned = ph.sem("conv_in"), ph.sem("conv_turned")

    def sync(sp):
        sp.dma_start(st[:], state.rearrange("b r f -> (b r) f")).then_inc(got, 16)
        sp.dma_start(wr[:taps, :], conv_w).then_inc(got, 16)
        if conv_b is not None:
            sp.dma_start(wr[taps:taps + 1, :], conv_b.unsqueeze(0)).then_inc(got, 16)

    def tensor(pe):
        pe.wait_ge(got, 16 * (3 if conv_b is not None else 2))
        for f in range(n_tiles):
            at = f // per * 512 + f % per * rows
            pe.transpose(pp[:, at:at + rows], st[:, f * P:(f + 1) * P], C["ident"][:rows, :rows])
            mm = pe.transpose(pw[:, f * nw:f * nw + nw], wr[:nw, f * P:(f + 1) * P], C["ident"][:nw, :nw])
        mm.then_inc(turned, 1)

    def scalar(act):
        act.wait_ge(turned, 1)
        for f0 in range(0, n_tiles, per):
            m = min(per, n_tiles - f0)
            at = f0 // per * 512
            act.copy(prev[:, f0:f0 + m, :], pp[:, at:at + m * rows].rearrange("p (f r) -> p f r", r=rows))
        act.copy(cw_sb[:], pw[:, :n_tiles * nw].rearrange("p (f r) -> p f r", r=nw))
    return {"sync": sync, "tensor": tensor, "scalar": scalar}


def store_tail(nc, C, name, tail, n_tiles, T1, new_p, new_s):
    rows = T1 * (1 + NB)
    with Phase(nc, name) as ph:
        tr = ph.sb("tr", [rows, n_tiles * P])
        pt = [ph.ps(f"pt{b}", [P, 512]) for b in range(2)]
        turned, copied, out = ph.sem("turned"), ph.sem("copied"), ph.sem("out")
        block = ph.block()
        n4 = n_tiles // 4

        @block.tensor
        def _(pe):
            for q in range(n4):
                if q >= 2:
                    pe.wait_ge(copied, q - 1)
                for f in range(4):
                    mm = pe.transpose(pt[q % 2][:rows, f * P:(f + 1) * P], tail[:, 4 * q + f, :], C["ident"][:])
                mm.then_inc(turned, 1)

        @block.scalar
        def _(act):
            for q in range(n4):
                act.wait_ge(turned, q + 1)
                act.copy(tr[:, q * 512:(q + 1) * 512], pt[q % 2][:rows, :]).then_inc(copied, 1)

        @block.sync
        def _(sp):
            sp.wait_ge(copied, n4)
            sp.dma_start(new_p, tr[:T1, :]).then_inc(out, 16)
            sp.dma_start(new_s.rearrange("b r f -> (b r) f"), tr[T1:, :]).then_inc(out, 16)
            sp.wait_ge(out, 32)


def conv_up(nc, C, name, xh, xl, w, taps, cw_sb, prev, tail, dst=None, wd=None, xT=None):
    ffn = wd is not None
    T1 = taps - 1
    turns = (NF if ffn else GDN_QKV // P) // 2
    slots = [(s, half) for s in range(2) for half in range(2 if ffn else 1)]
    R = len(slots)
    SW = T1 + TS
    G = len(GROUPS)
    nw = taps + (1 if ffn else 0)
    with Phase(nc, name) as ph:
        ws = ph.sb("ws", [P, 2, KD, P])
        wh = ph.sb("wh", [P, 2, KD, P], F32R)
        wl = ph.sb("wl", [P, 2, KD, P], F32R)
        hp = ph.sb("hp", [P, 2, T1 + SEQ])
        hs = ph.sb("hs", [P, 2, NB, SW])
        cur = ph.sb("cur", [P, 2, nw])
        conv = ph.sb("conv", [P, 2, NTOK])
        if ffn:
            gate = ph.sb("gate", [P, NTOK])
            gh = ph.sb("gh", [P, 2, NTOK], F32R)
            gl = ph.sb("gl", [P, 2, NTOK], F32R)
            ds = ph.sb("ds", [P, 2, D])
            dh = ph.sb("dh", [P, 2, D], F32R)
            dl = ph.sb("dl", [P, 2, D], F32R)
        acc = [ph.ps(f"acc{b}", [P, 512]) for b in range(2 * G)]
        dn = [ph.ps(f"dn{b}", [P, 512]) for b in range(2)]
        w_in = [ph.sem(f"w_in{b}") for b in range(2)]
        out = [ph.sem(f"out{b}") for b in range(2)]
        (high, low, staged, summed, evicted, tap0, tapped, silued, gated, g_high, g_low, d_in, d_high, d_low,
         down, added, zeroed, pace, step_sem) = (ph.sem(s) for s in (
             "high", "low", "staged", "summed", "evicted", "tap0", "tapped", "silued", "gated", "g_high", "g_low",
             "d_in", "d_high", "d_low", "down", "added", "zeroed", "pace", "tap_step"))
        block = ph.block()
        wv = w.rearrange("(k p) c -> p k c", p=P)

        def turned_loop(eng, body):
            body(0, True)
            with eng.Fori(1, turns) as i:
                body(i, False)

        @block.sync
        def _(sp):
            def body(i, first):
                for r, (s, half) in enumerate(slots):
                    sp.wait_ge(low, i * R + (r + 1))
                    sp.dma_start(ws[:, r % 2], wv[:, :, bass.ds(i * (2 * P) + (s * P + half * D_FF), P)])\
                        .then_inc(w_in[r % 2], 16)
                if ffn:
                    sp.wait_ge(d_low, i + 1)
                    sp.dma_start(ds[:], wd[bass.ds(i * (2 * P), 2 * P), :].rearrange("(s p) c -> p s c", p=P))\
                        .then_inc(d_in, 16)
            turned_loop(sp, body)

        @block.gpsimd
        def _(pool):
            pool.sem_inc(low, 2)
            pool.sem_inc(d_low, 1)
            pool.memset(hp[:, :, 0:T1], 0.0).then_inc(zeroed, 1)

            def body(i, first):
                for r, (s, half) in enumerate(slots):
                    b = r % 2
                    pool.wait_ge(w_in[b], i * (8 * R) + (16 * (r // 2) + 16))
                    pool.wait_ge(summed, i * (R * G) + (r + 1) * G)
                    pool.sem_inc(pace, 1)
                    pool.tensor_copy(wh[:, b], ws[:, b]).then_inc(high, 1)
                    pool.wait_ge(high, i * R + (r + 1))
                    pool.tensor_tensor(wl[:, b], ws[:, b], wh[:, b], ALU.subtract).then_inc(low, 1)
                    pool.wait_ge(tapped, i * R + (r + 1))
                    pool.sem_inc(pace, 1)
                    tile = bass.ds(i * 2 + (s + half * NF), 1)
                    pool.tensor_copy(cur[:, b:b + 1, :], cw_sb[:, tile, :])
                    pool.tensor_copy(hs[:, b:b + 1, :, 0:T1], prev[:, tile, :].rearrange(
                        "p o (b r) -> p o b r", r=T1)).then_inc(staged, 1)
                if ffn:
                    pool.wait_ge(d_in, i * 16 + 16)
                    if not first:
                        pool.wait_ge(down, i * (KD * G))
                    pool.sem_inc(pace, 1)
                    pool.tensor_copy(dh[:], ds[:]).then_inc(d_high, 1)
                    pool.wait_ge(d_high, i + 1)
                    pool.tensor_tensor(dl[:], ds[:], dh[:], ALU.subtract).then_inc(d_low, 1)
            turned_loop(pool, body)

        @block.tensor
        def _(pe):
            pe.sem_inc(summed, 2 * G)

            def up(i, r):
                b = r % 2
                pe.wait_ge(low, i * R + (r + 3))
                for g, (c0, w_) in enumerate(GROUPS):
                    pe.wait_ge(evicted, i * (R * G) + (r * G + g + 1))
                    ps = acc[G * b + g][:, :w_]
                    for k in range(KD):
                        pe.matmul(ps, wh[:, b, k], xh[:, k, c0:c0 + w_], start=(k == 0), stop=False)
                        pe.matmul(ps, wh[:, b, k], xl[:, k, c0:c0 + w_], start=False, stop=False)
                        mm = pe.matmul(ps, wl[:, b, k], xh[:, k, c0:c0 + w_], start=False, stop=(k == KD - 1))
                    mm.then_inc(summed, 1)

            def down_products(i):
                pe.wait_ge(d_low, i + 2)
                pe.wait_ge(g_low, i * 2 + 2)
                for t in range(KD):
                    for g, (c0, w_) in enumerate(GROUPS):
                        m = t * G + g
                        pe.wait_ge(added, i * (KD * G) + (m + 1))
                        ps = dn[m % 2][:, :w_]
                        for s in range(2):
                            cols = slice(t * P, (t + 1) * P)
                            pe.matmul(ps, dh[:, s, cols], gh[:, s, c0:c0 + w_], start=(s == 0), stop=False)
                            pe.matmul(ps, dh[:, s, cols], gl[:, s, c0:c0 + w_], start=False, stop=False)
                            mm = pe.matmul(ps, dl[:, s, cols], gh[:, s, c0:c0 + w_], start=False, stop=(s == 1))
                        mm.then_inc(down, 1)

            def body(i, first):
                for r in range(R):
                    if ffn and r == 2 and not first:
                        down_products(i - 1)
                    up(i, r)
            turned_loop(pe, body)
            if ffn:
                down_products(turns - 1)

        @block.scalar
        def _(act):
            act.sem_inc(evicted, 2 * G)
            for b in range(2):
                act.sem_inc(out[b], 16)
            act.wait_ge(zeroed, 1)

            def body(i, first):
                for r, (s, half) in enumerate(slots):
                    b = r % 2
                    act.wait_ge(tapped, i * R + (r + 1))
                    for g, (c0, w_) in enumerate(GROUPS):
                        act.wait_ge(summed, i * (R * G) + (2 * G + r * G + g + 1))
                        wp = min(w_, SEQ - c0)
                        ins = act.copy(hp[:, b, T1 + c0:T1 + c0 + wp], acc[G * b + g][:, :wp])
                        if wp < w_:
                            ins = act.copy(hs[:, b, :, T1:], acc[G * b + g][:, wp:w_].rearrange(
                                "p (b t) -> p b t", t=TS))
                        ins.then_inc(evicted, 1)
                    act.wait_ge(evicted, i * (R * G) + (2 * G + (r + 1) * G))
                    act.wait_ge(staged, i * R + (r + 1))
                    if ffn:
                        act.wait_ge(gated, i * 2 + (s + 1))
                    else:
                        act.wait_ge(out[b], i * 16 + 16)
                    bias = cur[:, b, taps:taps + 1] if ffn else 0.0
                    act.activation(conv[:, b, 0:SEQ], hp[:, b, 0:SEQ], ACT.Identity, bias=bias,
                                   scale=cur[:, b, 0:1])
                    act.activation(conv[:, b, SEQ:].rearrange("p (b t) -> p b t", t=TS), hs[:, b, :, 0:TS],
                                   ACT.Identity, bias=bias, scale=cur[:, b, 0:1]).then_inc(tap0, 1)
                    if not ffn:
                        act.wait_ge(tapped, i * R + (r + 3))
                        act.activation(conv[:, b, :], conv[:, b, :], ACT.Silu).then_inc(silued, 1)
                        act.wait_ge(silued, i * R + (r + 1))
                        act.dma_start(dst[bass.ds(i * 2 + r, 1), :, :].rearrange("o p t -> p (o t)"),
                                      conv[:, b, :]).then_inc(out[b], 16)
                    elif half:
                        act.wait_ge(tapped, i * R + (r + 3))
                        act.activation(gate[:], conv[:, 1, :], ACT.Silu).then_inc(silued, 1)
                        act.wait_ge(gated, i * 2 + (s + 2))
                        if not first:
                            act.wait_ge(down, i * (KD * G))
                        act.copy(gh[:, s, :], gate[:]).then_inc(g_high, 1)
            turned_loop(act, body)
            if not ffn:
                for b in range(2):
                    act.wait_ge(out[b], 16 * turns + 16)

        @block.vector
        def _(dve):
            dve.sem_inc(tapped, 2)
            if ffn:
                dve.sem_inc(gated, 1)
                dve.sem_inc(added, 2)
            step = Chain(dve, step_sem, per=R * (T1 - 1))

            def taps_of(i, r, s, half):
                b = r % 2
                dve.wait_ge(tap0, i * R + (r + 1))
                tile = bass.ds(i * 2 + (s + half * NF), 1)
                dve.tensor_copy(tail[:, tile, 0:T1], hp[:, b:b + 1, SEQ:SEQ + T1])
                dve.tensor_copy(tail[:, tile, T1:].rearrange("p o (b r) -> p o b r", r=T1),
                                hs[:, b:b + 1, :, TS:TS + T1])
                cp, cs = conv[:, b, 0:SEQ], conv[:, b, SEQ:].rearrange("p (b t) -> p b t", t=TS)
                for j in range(1, taps):
                    dve.scalar_tensor_tensor(cp, hp[:, b, j:j + SEQ], cur[:, b, j:j + 1], cp, ALU.mult, ALU.add)
                    ins = dve.scalar_tensor_tensor(cs, hs[:, b, :, j:j + TS], cur[:, b, j:j + 1], cs,
                                                   ALU.mult, ALU.add)
                    if j < taps - 1:
                        step(ins)
                ins.then_inc(tapped, 1)

            def add_down(i):
                for m in range(KD * G):
                    t, g = divmod(m, G)
                    c0, w_ = GROUPS[g]
                    dve.wait_ge(down, i * (KD * G) + (m + 1))
                    dve.tensor_tensor(xT[:, t, c0:c0 + w_], dn[m % 2][:, :w_], xT[:, t, c0:c0 + w_],
                                      ALU.add).then_inc(added, 1)

            def body(i, first):
                step.turn(i)
                for r, (s, half) in enumerate(slots):
                    if ffn and r == 1 and not first:
                        add_down(i - 1)
                    taps_of(i, r, s, half)
                    if half:
                        dve.wait_ge(silued, i * 2 + (s + 1))
                        if s or not first:
                            dve.wait_ge(g_low, i * 2 + s)
                        dve.tensor_tensor(gate[:], gate[:], conv[:, 0, :], ALU.mult).then_inc(gated, 1)
                        dve.wait_ge(g_high, i * 2 + (s + 1))
                        dve.tensor_tensor(gl[:, s, :], gate[:], gh[:, s, :], ALU.subtract).then_inc(g_low, 1)
                step.close()
            turned_loop(dve, body)
            if ffn:
                add_down(turns - 1)


def fox_prep(nc, C, p, q_gain, k_gain, b_f, qkA, sog, qTs, kTs, lfs, fk, fv, flf):
    A = DH + 2
    N = NT + 1
    with Phase(nc, "fxp") as ph:
        pf = ph.sb("pf", [P, 2, 2 * FOX_W])
        gains = ph.sb("gains", [P, 2, DH])
        bf = ph.sb("bf", [P, H])
        sq = ph.sb("sq", [P, 2, 2 * H * DH])
        ss, ms, rstd = (ph.sb(n, [P, 2 * H]) for n in ("ss", "ms", "rstd"))
        fl, nab, l1, lf = (ph.sb(n, [P, N, H]) for n in ("fl", "nab", "l1", "lf"))
        qa = ph.sb("qa", [P, 2, 2 * H, A])
        qs = ph.sb("qs", [P, 2 * H, DH])
        ps = ph.ps("ps", [P, 4, 4, P])
        psF = ph.ps("psF", [P, 512])
        F = ph.sb("F", [P, 2, NT, H])
        pf_in = [ph.sem(f"pf_in{b}") for b in range(2)]
        outs = [ph.sem(f"outs{b}") for b in range(2)]
        (params_in, fv_out, sog_in, fl_in, zeroed, nabbed, logged, lf_done, lf_out, summed, squared, meaned,
         rooted, scaled, gained, turned, stored_a, stored_d, dve_step, act_step) = (ph.sem(s) for s in (
             "params_in", "fv_out", "sog_in", "fl_in", "zeroed", "nabbed", "logged", "lf_done", "lf_out", "summed",
             "squared", "meaned", "rooted", "scaled", "gained", "turned", "stored_a", "stored_d",
             "dve_step", "act_step"))
        block = ph.block()

        def rows_of(i):
            return P if i < NT else NS

        def rows_out(i):
            return qa[:, i % 2] if i < NT else qs[:NS]

        @block.sync
        def _(sp):
            sp.dma_start(gains[:, 0, :], q_gain.partition_broadcast(P)).then_inc(params_in, 16)
            sp.dma_start(gains[:, 1, :], k_gain.partition_broadcast(P)).then_inc(params_in, 16)
            for i in range(N):
                r = rows_of(i)
                if i >= 2:
                    sp.wait_ge(scaled, i - 1)
                sp.dma_start(pf[:r, i % 2, :], p[i * P:i * P + r, 0:2 * FOX_W]).then_inc(pf_in[i % 2], 16)
                if i == 1:
                    sp.dma_start(fv, p[:, 2 * FOX_W:3 * FOX_W]).then_inc(fv_out, 16)
                    sp.dma_start(sog[:, 0:NT, :], p[0:SEQ, 3 * FOX_W:4 * FOX_W].rearrange("(n p) c -> p n c", p=P))\
                        .then_inc(sog_in, 16)
                    sp.dma_start(sog[:NS, NT, :], p[SEQ:, 3 * FOX_W:4 * FOX_W]).then_inc(sog_in, 16)
            sp.wait_ge(lf_done, 1)
            sp.dma_start(flf[0:SEQ].rearrange("(n p) c -> p n c", p=P), lf[:, 0:NT, :]).then_inc(lf_out, 16)
            sp.dma_start(flf[SEQ:], lf[:NS, NT, :]).then_inc(lf_out, 16)
            sp.wait_ge(fv_out, 16)
            sp.wait_ge(lf_out, 32)

        @block.gpsimd
        def _(pool):
            pool.memset(fl[:], 0.0).then_inc(zeroed, 1)
            pool.wait_ge(params_in, 32)
            pool.tensor_scalar(gains[:, 0, :], gains[:, 0, :], DH ** -0.5, None, ALU.mult).then_inc(params_in, 1)
            pool.wait_ge(params_in, 33)
            for i in range(N):
                r = rows_of(i)
                pool.wait_ge(meaned, i + 1)
                pool.tensor_tensor(rstd[:r], ms[:r], C["half"][:r, :2 * H], ALU.pow).then_inc(rooted, 1)
                pool.wait_ge(scaled, i + 1)
                for n in range(2):
                    t = rows_out(i)[:, n * H:(n + 1) * H, 0:DH]
                    ins = pool.tensor_tensor(t, t, bc(gains[:r, n, :], 1, H), ALU.mult)
                ins.then_inc(gained, 1)

        @block.scalar
        def _(act):
            forget = p[:, 4 * FOX_W:4 * FOX_W + H]
            act.dma_start(bf[:], b_f.partition_broadcast(P)).then_inc(fl_in, 16)
            act.wait_ge(zeroed, 1)
            act.dma_start(fl[:, 0:NT, :], forget[0:SEQ].rearrange("(n p) c -> p n c", p=P)).then_inc(fl_in, 16)
            act.dma_start(fl[:NS, NT, :], forget[SEQ:]).then_inc(fl_in, 16)
            act.wait_ge(nabbed, 1)
            act.activation(nab[:], nab[:], ACT.Exp).then_inc(act_step, 1)
            act.wait_ge(act_step, 1)
            act.activation(l1[:], nab[:], ACT.Ln, bias=1.0).then_inc(logged, 1)

            def finish(i):
                act.wait_ge(turned, i + 1)
                if i < NT:
                    ins = act.copy(qkA[:A, 0:8, i * P:(i + 1) * P], ps[:A, 0:2].rearrange("p a b t -> p (a b) t"))
                else:
                    ins = act.copy(qTs[:], ps[:, 0, :, :NS])
                ins.then_inc(stored_a, 1)
                act.dma_start(fk[i * P:i * P + rows_of(i), :].rearrange("t (h d) -> t h d", d=DH),
                              rows_out(i)[:, H:, 0:DH]).then_inc(outs[i % 2], 16)
            for i in range(N):
                r = rows_of(i)
                act.wait_ge(pf_in[i % 2], 16 * (i // 2 + 1))
                if i >= 2:
                    act.wait_ge(meaned, i - 1)
                act.activation(sq[:r, i % 2], pf[:r, i % 2], ACT.Square).then_inc(squared, 1)
                if i:
                    finish(i - 1)
            finish(NT)
            act.wait_ge(sog_in, 32)
            act.activation(sog[:, 0:NT, :], sog[:, 0:NT, :], ACT.Sigmoid)
            act.activation(sog[:NS, NT, :], sog[:NS, NT, :], ACT.Sigmoid)
            act.wait_ge(outs[0], 16 * ((N + 1) // 2))
            act.wait_ge(outs[1], 16 * (N // 2))

        @block.tensor
        def _(pe):
            pe.wait_ge(lf_done, 1)
            for i in range(NT):
                o = psF[:, i * H:(i + 1) * H]
                for j in range(i):
                    pe.matmul(o, C["ones"][:], lf[:, j, :], start=(j == 0), stop=False)
                mm = pe.matmul(o, C["tri"][:], lf[:, i, :], start=(i == 0), stop=True)
            mm.then_inc(summed, 1)
            for i in range(N):
                pe.wait_ge(gained, i + 1)
                if i:
                    pe.wait_ge(stored_a, i)
                    pe.wait_ge(stored_d, i)
                if i < NT:
                    for n in range(2 * H):
                        mm = pe.transpose(ps[:A, n // 4, n % 4, :], qa[:, i % 2, n, :], C["ident"][:])
                else:
                    for n in range(H):
                        mm = pe.transpose(ps[:, n // 4, n % 4, :NS],
                                          qs[:NS, 2 * n:2 * n + 2, :].rearrange("p a d -> p (a d)"),
                                          C["ident"][:NS, :NS])
                mm.then_inc(turned, 1)

        @block.vector
        def _(dve):
            step = Chain(dve, dve_step)
            step(dve.memset(qa[:], 1.0))
            dve.wait_ge(fl_in, 48)
            step(dve.tensor_tensor(fl[:], fl[:], bc(bf[:], 1, N), ALU.add))
            dve.scalar_tensor_tensor(nab[:], fl[:], -1.0, fl[:], ALU.mult, ALU.min).then_inc(nabbed, 1)
            dve.wait_ge(logged, 1)
            dve.scalar_tensor_tensor(lf[:], fl[:], 0.0, l1[:], ALU.min, ALU.subtract).then_inc(lf_done, 1)
            dve.wait_ge(lf_done, 1)
            dve.tensor_copy(lfs[:], lf[:NS, NT, :])
            dve.wait_ge(summed, 1)
            dve.tensor_copy(F[:, 0], psF[:, :NT * H].rearrange("p (n h) -> p n h", h=H))
            step(dve.tensor_scalar(F[:, 1], psF[:, :NT * H].rearrange("p (n h) -> p n h", h=H), -1.0, None, ALU.mult))
            dve.wait_ge(params_in, 33)

            def finish(i):
                dve.wait_ge(turned, i + 1)
                if i < NT:
                    ins = dve.tensor_copy(qkA[:A, 8:16, i * P:(i + 1) * P], ps[:A, 2:4].rearrange(
                        "p a b t -> p (a b) t"))
                else:
                    ins = dve.tensor_copy(kTs[:], ps[:, 1, :, :NS])
                ins.then_inc(stored_d, 1)
            for i in range(N):
                r, b = rows_of(i), i % 2
                dve.wait_ge(squared, i + 1)
                step(dve.tensor_reduce(ss[:r], sq[:r, b].rearrange("p (h d) -> p h d", d=DH), AX.X, ALU.add))
                dve.tensor_scalar(ms[:r], ss[:r], 1.0 / DH, EPS, ALU.mult, ALU.add).then_inc(meaned, 1)
                if 2 <= i < NT:
                    dve.wait_ge(outs[b], 16 * (i // 2))
                if i < NT:
                    dve.tensor_copy(qa[:, b, 0:H, DH], F[:, 0, i, :])
                    dve.tensor_copy(qa[:, b, H:, DH + 1], F[:, 1, i, :])
                dve.wait_ge(rooted, i + 1)
                dve.tensor_tensor(rows_out(i)[:, :, 0:DH], pf[:r, b].rearrange("p (h d) -> p h d", d=DH),
                                  bc(rstd[:r], 2, DH), ALU.mult).then_inc(scaled, 1)
                if i:
                    finish(i - 1)
            finish(NT)


def fox_prompt(nc, C, qkA, sog, fv, mixT):
    A = DH + 2
    U = 2 * NT
    with Phase(nc, "fx") as ph:
        v = ph.sb("v", [P, NT, FOX_W])
        qh = ph.sb("qh", [P, 2, SEQ])
        kh = ph.sb("kh", [P, 2, SEQ])
        mask = ph.sb("mask", [P, P])
        pr = ph.sb("pr", [P, 2, SEQ])
        pT = ph.sb("pT", [P, 2, NT, P])
        o = ph.sb("o", [P, NT, 2, DH])
        vh = ph.sb("vh", [P, 2, NT, DH])
        mx, rs, ri = (ph.sb(n, [P, 2 * NT]) for n in ("mx", "rs", "ri"))
        S = [ph.ps(f"S{b}", [P, 2, 512]) for b in range(2)]
        psT = ph.ps("psT", [P, NT, P])
        psO = ph.ps("psO", [P, 512])
        psM = ph.ps("psM", [P, 4, P])
        (v_in, masked, staged, scored, maxed, expd, turned, copied, valued, rinv, gated, o_turned, mixed) = (
            ph.sem(s) for s in ("v_in", "masked", "staged", "scored", "maxed", "expd", "turned", "copied",
                                "valued", "rinv", "gated", "o_turned", "mixed"))
        block = ph.block()
        turns = H // 2

        @block.sync
        def _(sp):
            sp.dma_start(v[:], fv[0:SEQ, :].rearrange("(t p) c -> p t c", p=P)).then_inc(v_in, 16)

        @block.gpsimd
        def _(pool):
            pool.memset(mask[:], 0.0).then_inc(masked, 1)
            pool.wait_ge(masked, 1)
            pool.affine_select(mask[:], mask[:], [[-1, P]], ALU.is_ge, NEG, base=0,
                               channel_multiplier=1).then_inc(masked, 1)

        @block.tensor
        def _(pe):
            pe.sem_inc(scored, 2)
            pe.sem_inc(valued, 2)
            pe.sem_inc(o_turned, 2)
            pe.wait_ge(masked, 2)

            def score(i, u):
                hb, qt = divmod(u, NT)
                if qt == 0:
                    pe.wait_ge(staged, i * 2 + (hb + 1))
                pe.wait_ge(expd, i * U + (u + 1))
                L = (qt + 1) * P
                for c0 in range(0, L, 512):
                    w = min(512, L - c0)
                    diag = c0 + w == L
                    mm = pe.matmul(S[u % 2][:, c0 // 512, :w], qh[:A, hb, qt * P:(qt + 1) * P],
                                   kh[:A, hb, c0:c0 + w], start=True, stop=not diag)
                    if diag:
                        mm = pe.matmul(S[u % 2][:, c0 // 512, w - P:w], C["ident"][:], mask[:], start=False,
                                       stop=True)
                mm.then_inc(scored, 1)

            def value(i, u):
                hb, qt = divmod(u, NT)
                pe.wait_ge(copied, i * U + (u + 2))
                pe.wait_ge(gated, i * U + (u + 1))
                for kt in range(qt + 1):
                    mm = pe.matmul(psO[:, 0:DH], pT[:, u % 2, kt, :], vh[:, hb, kt, :], start=(kt == 0),
                                   stop=(kt == qt))
                mm.then_inc(valued, 1)

            def body(i):
                score(i, 0)
                for u in range(U):
                    qt = u % NT
                    if u + 1 < U:
                        score(i, u + 1)
                    pe.wait_ge(expd, i * U + (u + 3))
                    pe.wait_ge(copied, i * U + (u + 1))
                    for kt in range(qt + 1):
                        mm = pe.transpose(psT[:, kt, :], pr[:, u % 2, kt * P:(kt + 1) * P], C["ident"][:])
                    mm.then_inc(turned, 1)
                    if u:
                        value(i, u - 1)
                value(i, U - 1)
                pe.wait_ge(gated, i * U + (U + 1))
                for half in range(2):
                    pe.wait_ge(mixed, i * 2 + (half + 1))
                    for t in range(4):
                        mm = pe.transpose(psM[:, t, :], o[:, half * 4 + t].rearrange("p h d -> p (h d)"),
                                          C["ident"][:])
                    mm.then_inc(o_turned, 1)
            with pe.Fori(0, turns) as i:
                body(i)

        @block.scalar
        def _(act):
            act.sem_inc(expd, 2)
            act.sem_inc(mixed, 1)

            def exp(i, u):
                L = (u % NT + 1) * P
                act.wait_ge(maxed, i * U + (u + 1))
                act.activation(pr[:, u % 2, :L], S[u % 2].rearrange("p a b -> p (a b)")[:, :L], ACT.Exp,
                               bias=mx[:, u:u + 1], accum_out=rs[:, u:u + 1]).then_inc(expd, 1)

            def body(i):
                exp(i, 0)
                for u in range(U):
                    qt = u % NT
                    if u + 1 < U:
                        exp(i, u + 1)
                    act.wait_ge(turned, i * U + (u + 1))
                    act.wait_ge(valued, i * U + (u + 1))
                    act.copy(pT[:, u % 2, :qt + 1, :], psT[:, :qt + 1, :]).then_inc(copied, 1)
                for half in range(2):
                    act.wait_ge(o_turned, i * 2 + (half + 3))
                    act.copy(mixT[:, bass.ds(i, 1), half * 512:(half + 1) * 512].rearrange("p o t -> p (o t)"),
                             psM.rearrange("p a b -> p (a b)")).then_inc(mixed, 1)
            act.sem_inc(copied, 1)
            with act.Fori(0, turns) as i:
                body(i)

        @block.vector
        def _(dve):
            dve.sem_inc(gated, 1)
            dve.wait_ge(v_in, 16)

            def stage(i, hb):
                dve.wait_ge(valued, i * U + 2)
                h = i * 2 + hb
                dve.tensor_copy(qh[:A, hb:hb + 1, :], qkA[:A, bass.ds(h, 1), :])
                dve.tensor_copy(kh[:A, hb:hb + 1, :], qkA[:A, bass.ds(h + H, 1), :])
                dve.tensor_copy(vh[:, hb], v[:, :, bass.ds(h * DH, DH)]).then_inc(staged, 1)

            def maximum(i, u):
                L = (u % NT + 1) * P
                dve.wait_ge(scored, i * U + (u + 3))
                dve.tensor_reduce(mx[:, u:u + 1], S[u % 2].rearrange("p a b -> p (a b)")[:, :L], AX.X, ALU.max,
                                  negate=True).then_inc(maxed, 1)

            def body(i):
                stage(i, 0)
                maximum(i, 0)
                for u in range(U):
                    if u == 1:
                        stage(i, 1)
                    if u + 1 < U:
                        maximum(i, u + 1)
                    if u:
                        finish(i, u - 1)
                finish(i, U - 1)

            def finish(i, u):
                hb, qt = divmod(u, NT)
                b = u
                dve.wait_ge(expd, i * U + (u + 3))
                dve.reciprocal(ri[:, b:b + 1], rs[:, b:b + 1]).then_inc(rinv, 1)
                dve.wait_ge(rinv, i * U + (u + 1))
                dve.wait_ge(valued, i * U + (u + 3))
                if qt == 0 and hb == 0:
                    dve.wait_ge(o_turned, i * 2 + 2)
                dve.scalar_tensor_tensor(o[:, qt, hb, :], psO[:, 0:DH], ri[:, b:b + 1],
                                         sog[:, qt, bass.ds((i * 2 + hb) * DH, DH)], ALU.mult, ALU.mult)\
                    .then_inc(gated, 1)
            with dve.Fori(0, turns) as i:
                body(i)


def fox_sample(nc, C, qTs, kTs, lfs, sog, fv, pool_k, pool_v, pool_lf, page_table, mixT):
    HQ = H * TS
    NK = PAST + TS
    with Phase(nc, "fs") as ph:
        table = ph.sb("table", [1, NB * NPG], I32)
        kp = ph.sb("kp", [P, 2, NPG, FOX_W])
        vp = ph.sb("vp", [P, 2, NPG, FOX_W])
        lp = ph.sb("lp", [P, 2, NPG, H])
        vn = ph.sb("vn", [TS, 2, FOX_W])
        qx_all = ph.sb("qx_all", [P, NB, 4, HQ])
        qx = ph.sb("qx", [P, 4, HQ])
        kn = ph.sb("kn", [P, 4, TS])
        lx = ph.sb("lx", [P, NPG, H, TS])
        lnx = ph.sb("lnx", [NS, H, TS])
        sel = ph.sb("sel", [NS, TS])
        kT = ph.sb("kT", [P, 2, 4, P])
        ones_row = ph.sb("ones_row", [HQ, PAST])
        onehot = ph.sb("onehot", [HQ, TS])
        causal = ph.sb("causal", [HQ, TS])
        F = ph.sb("F", [HQ, NK])
        fq = ph.sb("fq", [HQ, 1])
        fqt = ph.sb("fqt", [HQ, TS])
        st = ph.sb("st", [HQ, NK])
        pr = ph.sb("pr", [HQ, NK])
        mx, rs, ri = (ph.sb(n, [HQ, 1]) for n in ("mx", "rs", "ri"))
        pT = ph.sb("pT", [P, NPG + 1, HQ])
        headmask = ph.sb("headmask", [HQ, H, DH])
        om = ph.sb("om", [HQ, FOX_W])
        red = ph.sb("red", [P, 4, NS])
        sgT = ph.sb("sgT", [P, 4, NS])
        psK = [ph.ps(f"psK{b}", [P, 4, P]) for b in range(2)]
        S = ph.ps("S", [P, 1024])
        L = ph.ps("L", [P, 1024])
        N = ph.ps("N", [P, 512])
        O = ph.ps("O", [P, 512])
        k_in = [ph.sem(f"k_in{b}") for b in range(2)]
        v_in = [ph.sem(f"v_in{b}") for b in range(2)]
        l_in = [ph.sem(f"l_in{b}") for b in range(2)]
        (table_in, consts, staged, k_turned, k_copied, scored, l_turned, scanned, shifted, expd, p_turned,
         p_copied, valued, masked, o_turned, reduced, gate_turned) = (ph.sem(s) for s in (
             "table_in", "consts", "staged", "k_turned", "k_copied", "scored", "l_turned", "scanned", "shifted",
             "expd", "p_turned", "p_copied", "valued", "masked", "o_turned", "reduced", "gate_turned"))
        dve_step, pace = ph.sem("dve_step"), ph.sem("pace")
        block = ph.block()

        def sequences(eng, body):
            with eng.Fori(0, NB // 2) as j:
                for b in range(2):
                    body(j * 2 + b, b, j)

        @block.sync
        def _(sp):
            sp.dma_start(table[:], page_table.rearrange("b n -> (b n)").unsqueeze(0)).then_inc(table_in, 16)
            sp.wait_ge(table_in, 16)

            def body(i, b, j):
                sp.wait_ge(l_turned, i + 1)
                sp.wait_ge(k_turned, i * NPG + NPG)
                sp.wait_ge(valued, i + 1)
                for g in range(NPG):
                    page = sp.value_load(table[0:1, bass.ds(i * NPG + g, 1)], min_val=0, max_val=N_POOL - 1)
                    sp.dma_start(lp[:, b, g, :], pool_lf[bass.ds(page, 1)].rearrange("o p h -> p (o h)"))\
                        .then_inc(l_in[b], 16)
                    sp.dma_start(kp[:, b, g, :], pool_k[bass.ds(page, 1)].rearrange("o p c -> p (o c)"))\
                        .then_inc(k_in[b], 16)
                    sp.dma_start(vp[:, b, g, :], pool_v[bass.ds(page, 1)].rearrange("o p c -> p (o c)"))\
                        .then_inc(v_in[b], 16)
                sp.dma_start(vn[:, b, :], fv[bass.ds(i * TS + SEQ, TS), :]).then_inc(v_in[b], 16)
            sequences(sp, body)

        @block.gpsimd
        def _(pool):
            step = Chain(pool, consts)
            step(pool.memset(qx_all[:], 0.0))
            step(pool.memset(headmask[:], 1.0))
            step(pool.affine_select(headmask[:], headmask[:], [[-TS, H], [0, DH]], ALU.is_ge, 0.0, base=0,
                                    channel_multiplier=1))
            step(pool.affine_select(headmask[:], headmask[:], [[TS, H], [0, DH]], ALU.is_ge, 0.0, base=TS - 1,
                                    channel_multiplier=-1))
            step(pool.memset(ones_row[:], 1.0))

        @block.tensor
        def _(pe):
            pe.sem_inc(l_turned, 2)
            pe.sem_inc(k_turned, 2 * NPG)
            pe.sem_inc(valued, 2)
            for m in range(4):
                mm = pe.transpose(psK[0][:, m, :NS], sog[:NS, NT, m * P:(m + 1) * P], C["ident"][:NS, :NS])
            mm.then_inc(gate_turned, 1)
            pe.wait_ge(k_copied, 2)

            def body(i, b, j):
                pe.wait_ge(staged, i + 1)
                pe.wait_ge(scanned, i + 1)
                pe.sem_inc(pace, 1)
                for g in range(NPG):
                    pe.transpose(L[:HQ, g * P:(g + 1) * P], lx[:, g].rearrange("p h q -> p (h q)"), C["ident"][:])
                pe.matmul(N[:HQ, TS:2 * TS], lnx.rearrange("p h q -> p (h q)"), sel[:], start=True, stop=True)\
                    .then_inc(l_turned, 1)
                pe.wait_ge(k_in[b], j * (16 * NPG) + 16 * NPG)
                pe.wait_ge(shifted, i + 1)
                for g in range(NPG + 1):
                    if g < NPG:
                        pe.wait_ge(k_copied, i * NPG + (g + 1))
                        for m in range(4):
                            mm = pe.transpose(psK[g % 2][:, m, :], kp[:, b, g, m * P:(m + 1) * P], C["ident"][:])
                        mm.then_inc(k_turned, 1)
                    if g:
                        pe.wait_ge(k_copied, i * NPG + (g + 2))
                        for m in range(4):
                            mm = pe.matmul(S[:HQ, (g - 1) * P:g * P], qx[:, m, :], kT[:, (g - 1) % 2, m, :],
                                           start=(m == 0), stop=(m == 3))
                        mm.then_inc(scored, 1)
                pe.wait_ge(scanned, i + 2)
                for m in range(4):
                    mm = pe.matmul(N[:HQ, 0:TS], qx[:, m, :], kn[:, m, :], start=(m == 0), stop=(m == 3))
                mm.then_inc(scored, 1)
                pe.wait_ge(expd, i + 1)
                pe.sem_inc(pace, 1)
                for g in range(NPG):
                    mm = pe.transpose(psK[0].rearrange("p a b -> p (a b)")[:, g * HQ:(g + 1) * HQ],
                                      pr[:, g * P:(g + 1) * P], C["ident"][:HQ, :HQ])
                mm = pe.transpose(N[:TS, P:P + HQ], pr[:, PAST:], C["ident"][:HQ, :HQ])
                mm.then_inc(p_turned, 1)
                pe.wait_ge(p_copied, i + 1)
                pe.wait_ge(v_in[b], j * (16 * NPG + 16) + (16 * NPG + 16))
                for g in range(NPG):
                    pe.matmul(O[:HQ, :], pT[:, g, :], vp[:, b, g, :], start=(g == 0), stop=False)
                pe.matmul(O[:HQ, :], pT[:TS, NPG, :], vn[:, b, :], start=False, stop=True).then_inc(valued, 1)
                pe.wait_ge(masked, i + 1)
                pe.sem_inc(pace, 1)
                for m in range(4):
                    mm = pe.transpose(psK[0][:, m, :HQ], om[:, m * P:(m + 1) * P], C["ident"][:HQ, :HQ])
                mm.then_inc(o_turned, 1)
                pe.wait_ge(reduced, i + 1)
            sequences(pe, body)

        @block.scalar
        def _(act):
            act.wait_ge(gate_turned, 1)
            act.copy(sgT[:], psK[0][:, :, :NS]).then_inc(k_copied, 2)

            def body(i, b, j):
                for g in range(NPG):
                    act.wait_ge(k_turned, i * NPG + (2 * NPG + g + 1))
                    act.wait_ge(scored, i * (NPG + 1) + (g + 1))
                    act.copy(kT[:, g % 2], psK[g % 2][:]).then_inc(k_copied, 1)
                act.wait_ge(shifted, i + 2)
                act.activation(pr[:], st[:], ACT.Exp, bias=mx[:], accum_out=rs[:]).then_inc(expd, 1)
                act.wait_ge(p_turned, i + 1)
                act.copy(pT[:, 0:NPG, :].rearrange("p g q -> p (g q)"), psK[0].rearrange("p a b -> p (a b)"))
                act.copy(pT[:TS, NPG, :], N[:TS, P:P + HQ]).then_inc(p_copied, 1)
            act.sem_inc(scored, 2)
            sequences(act, body)

        @block.vector
        def _(dve):
            dve.sem_inc(scanned, 1)
            dve.sem_inc(shifted, 1)
            step = Chain(dve, dve_step, per=7)
            dve.wait_ge(consts, 5)
            for m in range(4):
                for q in range(2):
                    rows = slice(q * DH, (q + 1) * DH)
                    h = 2 * m + q
                    dve.tensor_copy(qx_all[rows, :, m, h * TS:(h + 1) * TS],
                                    qTs[rows, m, :].rearrange("p (b t) -> p b t", t=TS))
            dve.tensor_copy(lnx[:], bc(lfs[:], 2, TS))
            dve.tensor_reduce(onehot[:], C["ident"][:HQ, :HQ].rearrange("p (a t) -> p t a", t=TS), AX.X, ALU.add)
            dve.tensor_reduce(causal[:], C["blk_low"][:HQ, :HQ].rearrange("p (a t) -> p t a", t=TS), AX.X, ALU.add)\
                .then_inc(consts, 1)
            dve.wait_ge(consts, 6)
            dve.tensor_scalar(causal[:], causal[:], 1.0, -NEG, ALU.subtract, ALU.mult).then_inc(consts, 1)
            dve.wait_ge(consts, 7)

            def body(i, b, j):
                step.turn(i)
                dve.wait_ge(l_in[b], j * (16 * NPG) + 16 * NPG)
                dve.tensor_copy(lx.rearrange("p g h q -> p (g h) q"),
                                bc(lp[:, b].rearrange("p g h -> p (g h)"), 2, TS))
                dve.tensor_copy(sel[:], C["ident"][:NS, bass.ds(i * TS, TS)])
                dve.tensor_copy(kn[:], kTs[:, :, bass.ds(i * TS, TS)])
                dve.tensor_copy(qx[:], qx_all[:, bass.ds(i, 1)].rearrange("p o m q -> p (o m) q")).then_inc(staged, 1)
                dve.wait_ge(l_turned, i + 3)
                step(dve.tensor_tensor_scan(F[:, :PAST], ones_row[:], L[:HQ, :], 0.0, ALU.mult, ALU.add))
                dve.tensor_tensor_scan(F[:, PAST:], ones_row[:, :TS], N[:HQ, TS:2 * TS], F[:, PAST - 1:PAST],
                                       ALU.mult, ALU.add).then_inc(scanned, 1)
                dve.wait_ge(scanned, i + 2)
                step(dve.tensor_tensor(fqt[:], F[:, PAST:], onehot[:], ALU.mult))
                step(dve.tensor_reduce(fq[:], fqt[:], AX.X, ALU.add))
                dve.wait_ge(scored, i * (NPG + 1) + (NPG + 3))
                dve.scalar_tensor_tensor(st[:, :PAST], S[:HQ, :], fq[:], F[:, :PAST], ALU.add, ALU.subtract)
                step(dve.scalar_tensor_tensor(st[:, PAST:], N[:HQ, 0:TS], fq[:], F[:, PAST:], ALU.add, ALU.subtract))
                step(dve.tensor_tensor(st[:, PAST:], st[:, PAST:], causal[:], ALU.add))
                dve.tensor_reduce(mx[:], st[:], AX.X, ALU.max, negate=True).then_inc(shifted, 1)
                dve.wait_ge(expd, i + 1)
                step(dve.reciprocal(ri[:], rs[:]))
                dve.wait_ge(valued, i + 3)
                dve.scalar_tensor_tensor(om[:], O[:HQ, :], ri[:], headmask.rearrange("p h d -> p (h d)"),
                                         ALU.mult, ALU.mult).then_inc(masked, 1)
                dve.wait_ge(o_turned, i + 1)
                step(dve.tensor_reduce(red[:, :, bass.ds(i * TS, TS)],
                                       psK[0][:, :, :HQ].rearrange("p m (h q) -> p m q h", q=TS), AX.X, ALU.add))
                dve.sem_inc(reduced, 1)
                step.close()
            sequences(dve, body)
            dve.wait_ge(dve_step, NB * step.per)
            dve.tensor_tensor(mixT[:, 0:4, SEQ:], red[:], sgT[:], ALU.mult)



GROUP = 4


def inverse_buffers(ph, T):
    return {n: [ph.sb(f"{n}{g}", [T, GROUP, T]) for g in range(2)] for n in ("NL", "X", "XT", "PX")}


def inverse_sems(ph):
    return {n: ph.sem(n) for n in ("n_level", "p_done", "p_copied", "x_done", "x_added")}


def half_columns(ap, l, second, T):
    w = 2 ** l
    if len(ap.shape) == 2:
        return ap.rearrange("p (a q w) -> p a q w", q=2, w=w)[:, :, second, :]
    return ap.rearrange("p h (a q w) -> p h a q w", q=2, w=w)[:, :, :, second, :]


def inverse_pool(pool, C, I, s, NT_, T, levels, i):
    for l in range(levels):
        for g in range(2):
            n = 2 * l + g
            if l:
                pool.wait_ge(s["p_done"], i * (2 * levels) + (n - 1))
            if l == 1:
                pool.wait_ge(s["x_added"], i * (2 * levels) + (n - 1))
            pool.tensor_tensor(I["NL"][g][:], NT_[:, g * GROUP:(g + 1) * GROUP, :],
                               bc(C["join"][:T, l, :T], 1, GROUP), ALU.mult).then_inc(s["n_level"], 1)


def inverse_pe(pe, C, I, s, PS, T, levels, i, between):
    def heads(ps, lhsT, rhs):
        for h in range(GROUP):
            mm = pe.matmul(ps[:T, h * P:h * P + T], lhsT[:, h, :], rhs(h), start=True, stop=True)
        return mm

    def half_heads(ps, lhsT, rhs, l, second):
        for h in range(GROUP):
            mm = pe.matmul(half_columns(ps[:T, h * P:h * P + T], l, second, T), lhsT[:, h, :],
                           half_columns(rhs[:, h, :], l, second, T), start=True, stop=True)
        return mm
    for l in range(levels):
        for g in range(2):
            n = 2 * l + g
            bank = 3 * g
            pe.wait_ge(s["n_level"], i * (2 * levels) + (n + 1))
            if l:
                pe.wait_ge(s["x_added"], i * (2 * levels) + (n - 1))
            ident = C["ident"][:T, :T]
            heads(PS[:, bank], I["NL"][g], lambda h: ident if l == 0 else I["X"][g][:, h, :])\
                .then_inc(s["p_done"], 1)
        for g in range(2):
            if l == 0:
                continue
            n = 2 * l + g
            bank = 3 * g
            pe.wait_ge(s["p_copied"], i * (2 * (levels - 1)) + (n - 1))
            if l < levels - 1:
                half_heads(PS[:, bank + 1], I["XT"][g], I["PX"][g], l, 0)
            half_heads(PS[:, bank + 2], I["PX"][g], I["XT"][g], l, 1).then_inc(s["x_done"], 1)
        between(l)


def inverse_act(act, I, s, PS, T, levels, i):
    for l in range(1, levels):
        for g in range(2):
            n = 2 * l + g
            act.wait_ge(s["p_done"], i * (2 * levels) + (n + 1))
            act.copy(I["PX"][g][:], PS[:T, 3 * g, :].rearrange("p (h t) -> p h t", h=GROUP)[:, :, :T])\
                .then_inc(s["p_copied"], 1)


def inverse_dve(dve, C, I, s, PS, T, levels, i, between=None):
    ident = bc(C["ident"][:T, :T], 1, GROUP)

    def bank(n):
        return PS[:T, n, :].rearrange("p (h t) -> p h t", h=GROUP)[:, :, :T]
    for l in range(levels):
        for g in range(2):
            n = 2 * l + g
            X, XT = I["X"][g], I["XT"][g]
            if l == 0:
                dve.wait_ge(s["p_done"], i * (2 * levels) + (n + 1))
                dve.tensor_tensor(X[:], bank(3 * g), ident, ALU.add)
                dve.tensor_tensor(XT[:], I["NL"][g][:], ident, ALU.add).then_inc(s["x_added"], 1)
            else:
                dve.wait_ge(s["x_done"], i * (2 * (levels - 1)) + (n - 1))
                if l < levels - 1:
                    x = half_columns(X[:], l, 0, T)
                    dve.tensor_tensor(x, half_columns(bank(3 * g + 1), l, 0, T), x, ALU.add)
                x = half_columns(XT[:], l, 1, T)
                dve.tensor_tensor(x, half_columns(bank(3 * g + 2), l, 1, T), x, ALU.add).then_inc(s["x_added"], 1)
        if between:
            between(l)


def build_join(nc, C):
    with Phase(nc, "join") as ph:
        blocks = ph.sb("blocks", [P, 8, P])
        s = ph.sem("made")
        block = ph.block()

        @block.gpsimd
        def _(pool):
            step = Chain(pool, s)
            step(pool.memset(blocks[:], 1.0))
            for l in range(7):
                w = 2 ** l
                v = blocks[:, l, :].rearrange("p (a t) -> p a t", t=w)
                step(pool.affine_select(v, v, [[-w, P // w], [0, w]], ALU.is_ge, 0.0, base=0, channel_multiplier=1))
                step(pool.affine_select(v, v, [[w, P // w], [0, w]], ALU.is_ge, 0.0, base=w - 1,
                                        channel_multiplier=-1))
            for l in range(7):
                step(pool.tensor_tensor(C["join"][:, l, :], blocks[:, l + 1, :], blocks[:, l, :], ALU.subtract))


def rwkv_weights(ph):
    R = {n: ph.sb(n, [P, RW_W]) for n in ("k_k", "k_a", "r_k", "ln_w", "ln_b", "g2")}
    R["mu"] = ph.sb("mu", [P, RW_COLS])
    R["wa0"] = ph.sb("wa0", [P, 2, RW_W])
    R["wa2"] = ph.sb("wa2", [P, 2, RW_W])
    return R


def rwkv(nc, C, sample, R, prw, state_in, shift_in, W, mixT, state_out, shift_out):
    T = NS if sample else P
    NSEQ = NB if sample else 1
    levels = 3 if sample else 7
    n_it = 1 if sample else NT
    tok0 = SEQ if sample else 0
    PR = H // 2
    with Phase(nc, "rs" if sample else "rw") as ph:
        cur = ph.sb("cur", [T, RW_COLS])
        pm = ph.sb("prv", [T, 2 * NB * P if sample else RW_COLS])
        prv, mu = pm[:, :RW_COLS], R["mu"][:T]
        raw = cur if sample else ph.sb("raw", [T, RW_COLS])
        rk = prv[:, 0:RW_W] if sample else ph.sb("rk", [T, RW_W])
        par = {n: R[n][:T] for n in ("k_k", "k_a", "r_k", "ln_w", "ln_b")}
        wa0, wa2, g2 = R["wa0"][:T], R["wa2"], R["g2"]
        cen = ph.sb("cen", [T, T])
        cols = ph.sb("cols", [T, 8])
        mask = ph.sb("mask", [T, 2, T])
        lowT = ph.sb("lowT", [P, 2, T])
        za = ph.sb("za", [T, 2, RW_W])
        g = ph.sb("g", [T, RW_W])
        gp = ph.sb("gp", [T, RW_W])
        e0, e1, e2 = (ph.sb(n, [T, RW_W]) for n in ("e0", "e1", "e2"))
        kk, sq, kf, bb = (ph.sb(n, [T, RW_W]) for n in ("kk", "sq", "kf", "bb"))
        at, rt = e0, e1
        bt, kt = (ph.sb(n, [T, RW_W]) for n in ("bt", "kt"))
        s8, m8, r8, bon = (ph.sb(n, [T, H]) for n in ("s8", "m8", "r8", "bon"))
        ecm = ph.sb("ecm", [P, PR, 8])
        arT = ph.sb("arT", [P, PR, 2, T])
        bT, kT = (ph.sb(n, [P, PR, T]) for n in ("bT", "kT"))
        LB, LK = (ph.sb(n, [T, H, 2, T]) for n in ("LB", "LK"))
        u0, u = (ph.sb(n, [T, RW_W]) for n in ("u0", "u"))
        S = ph.sb("S", [P, NSEQ, PR, P])
        S0 = None if sample else ph.sb("S0", [P, PR, P])
        pre = ph.sb("pre", [P, NSEQ, PR, P])
        y = ph.sb("y", [T, RW_W])
        if sample:
            sT = ph.sb("sT", [P, PR, 2, T])
            ux = pm.rearrange("p (n b c) -> p n b c", n=2, b=NB)
        I = inverse_buffers(ph, T)
        PS = ph.ps("PS", [P, 8, 512])
        inv = inverse_sems(ph)
        names = ("par_in pre_in setup rows_in differed mixed_in shifted tanhd gate_in low_turned low_copied lowrank za_done "
                 "zt_done g_copied logw_done summed gp_done expd squared kk_rooted tilded turned ar_copied bk_copied gram "
                 "masked s0_done u0_sum u0_done u_sum u_done ys_sum s_turned rk_done centred y_squared vr_done y_rooted vg_done low_shifted y_done y_turned "
                 "tile_done spread state_done st_turned st_copied out").split()
        s = {n: ph.sem(n) for n in names}
        dve_step, pool_step, pace, dve_pace = (ph.sem(n) for n in ("dve_step", "pool_step", "pace", "dve_pace"))
        block = ph.block()
        ident = C["ident"]

        n_setup = 7 if sample else 11

        def tiles(eng, body):
            if sample:
                body(0)
            else:
                with eng.Fori(0, n_it) as i:
                    body(i)

        def pairs(ap):
            return ap.rearrange("p (m c) -> p m c", m=PR)

        def heads(ap):
            return ap.rearrange("p (h d) -> p h d", h=H)

        @block.sync
        def _(sp):
            def load(i):
                sp.dma_start(raw[:], prw[bass.ds(i * P + (tok0 + 1), T), :]).then_inc(s["rows_in"], 16)
                sp.dma_start(prv[:], prw[bass.ds(i * P + tok0, T), :]).then_inc(s["rows_in"], 16)
            load(0)
            if not sample:
                sp.dma_start(mu[:], W["mu"].partition_broadcast(T)).then_inc(s["par_in"], 16)
                for n in ("k_k", "k_a", "r_k"):
                    sp.dma_start(par[n][:], W[n].partition_broadcast(T)).then_inc(s["par_in"], 16)
            if sample:
                sp.wait_ge(s["rows_in"], 32)
                sp.dma_start(prv[0:T:TS, :], shift_in).then_inc(s["rows_in"], 16)
            sp.wait_ge(s["setup"], 1 if sample else 2)
            if not sample:
                sp.dma_start(wa2[0:R_W, 0, :], W["w2"]).then_inc(s["par_in"], 16)
                sp.dma_start(wa2[R_W:, 1, :], W["a2"]).then_inc(s["par_in"], 16)
            if sample:
                for q in range(2):
                    for b in range(NB):
                        sp.dma_start(pre[q * DH:(q + 1) * DH, b, :, q * DH:(q + 1) * DH],
                                     state_in[b].rearrange("(m q) i j -> q i m j", q=2)[q]).then_inc(s["pre_in"], 16)
            sp.dma_start(shift_out, prw[NTOK - NS + TS:NTOK + 1:TS, :] if sample else prw[SEQ:SEQ + 1, :])\
                .then_inc(s["out"], 16)

            if not sample:
                with sp.Fori(0, NT - 1) as i:
                    sp.wait_ge(s["shifted"], i + 1)
                    load(i + 1)
            sp.wait_ge(s["st_copied"], NSEQ)
            for q in range(2):
                rows = slice(q * DH, (q + 1) * DH)
                for b in range(NSEQ):
                    dst = state_out[b] if sample else state_out
                    sp.dma_start(dst.rearrange("(m q) i j -> q i m j", q=2)[q], pre[rows, b, :, rows])\
                        .then_inc(s["out"], 16)
            sp.wait_ge(s["out"], 16 * (1 + 2 * NSEQ))

        @block.gpsimd
        def _(pool):
            made = Chain(pool, s["setup"])
            if not sample:
                made(pool.memset(wa2[:], 0.0))
            made(pool.memset(pre[:], 0.0))

            def mix(i):
                pool.wait_ge(s["rows_in"], i * 32 + (48 if sample else 32))
                pool.tensor_tensor(prv[:], prv[:], raw[:], ALU.subtract).then_inc(s["differed"], 1)
                pool.wait_ge(s["differed"], i + 1)
                pool.tensor_tensor(prv[:], prv[:], mu[:], ALU.mult).then_inc(s["mixed_in"], 1)

            if not sample:
                pool.wait_ge(s["par_in"], 16 * 11)
            mix(0)
            if not sample:
                made(pool.memset(S[:], 0.0))
            made(pool.memset(LB[:], 0.0))
            made(pool.memset(LK[:], 0.0))
            tri = C["blk_tri"] if sample else C["tri"]
            made(pool.tensor_copy(mask[:, 1, :], tri[:T, :T]))
            made(pool.tensor_tensor(mask[:, 0, :], tri[:T, :T], ident[:T, :T], ALU.subtract))
            if sample:
                made(pool.tensor_copy(cen[:], tri[:T, :T]))
                made(pool.tensor_copy(cols[:], C["blk"][:T, 0:T:TS]))
            else:
                made(pool.tensor_copy(cols[:, 0:1], C["tri"][:, 63:64]))
                made(pool.tensor_tensor(cols[:, 1:2], C["ones"][:, 0:1], cols[:, 0:1], ALU.subtract))
                made(pool.memset(cols[:, 2:8], 0.0))
                made(pool.tensor_tensor(cen[:], C["tri"][:], C["tri"][:, 63:64].to_broadcast([P, P]), ALU.subtract))
            assert made.n == n_setup
            step = Chain(pool, pool_step, per=3)

            def body(i, last):
                step.turn(i)
                pool.wait_ge(s["squared"], i + 1)
                pool.tensor_tensor(r8[:], m8[:], C["half"][:T, :H], ALU.pow).then_inc(s["kk_rooted"], 1)
                pool.wait_ge(s["tilded"], i + 1)
                step(pool.tensor_tensor(rk[:], cur[:, 0:RW_W], kf[:], ALU.mult))
                pool.tensor_tensor(rk[:], rk[:], par["r_k"][:], ALU.mult).then_inc(s["rk_done"], 1)
                if not last:
                    mix(i + 1)
                pool.wait_ge(s["masked"], i * 4 + 4)
                inverse_pool(pool, C, I, inv, LB[:, :, 0, :], T, levels, i)
                pool.wait_ge(s["g_copied"], i + 1)
                pool.tensor_tensor(gp[:], g[:], par["ln_w"][:], ALU.mult)
                step(pool.tensor_tensor(heads(kk[:]), heads(cur[:, 2 * RW_W:3 * RW_W]), bc(bon[:], 2, DH), ALU.mult))
                step(pool.tensor_tensor(kk[:], kk[:], par["ln_b"][:], ALU.add))
                pool.tensor_tensor(kk[:], kk[:], g[:], ALU.mult).then_inc(s["vg_done"], 1)
                pool.wait_ge(s["vr_done"], i + 1)
                pool.tensor_tensor(r8[:], m8[:], C["half"][:T, :H], ALU.pow).then_inc(s["y_rooted"], 1)
                step.close()
            if not sample:
                with pool.Fori(0, NT - 1) as i:
                    body(i, False)
            body(n_it - 1, True)

        @block.scalar
        def _(act):
            act.sem_inc(s["tile_done"], 1)
            if not sample:
                act.dma_start(wa0[:, 0, :], W["w0"].partition_broadcast(T)).then_inc(s["par_in"], 16)
                act.dma_start(wa0[:, 1, :], W["a0"].partition_broadcast(T)).then_inc(s["par_in"], 16)
                act.dma_start(g2[:], W["g2"]).then_inc(s["par_in"], 16)
                for n in ("ln_w", "ln_b"):
                    act.dma_start(par[n][:], W[n].partition_broadcast(T)).then_inc(s["par_in"], 16)
            if sample:
                for b in range(NB):
                    act.wait_ge(s["st_turned"], b + 1)
                    act.copy(S[:, b], pairs(PS[:, b % 2, :])).then_inc(s["state_done"], 1)

            def body(i):
                act.wait_ge(s["low_shifted"], i + 1)
                act.activation(cur[:, 3 * RW_W:3 * RW_W + R_W], cur[:, 3 * RW_W:3 * RW_W + R_W], ACT.Tanh)
                act.activation(cur[:, 3 * RW_W + R_W + R_A:], cur[:, 3 * RW_W + R_W + R_A:], ACT.Tanh, scale=0.5)\
                    .then_inc(s["tanhd"], 1)
                act.wait_ge(s["low_turned"], i + 1)
                act.copy(lowT[:], PS[:, 6, :2 * T].rearrange("p (a t) -> p a t", a=2)).then_inc(s["low_copied"], 1)
                for n in range(2):
                    act.wait_ge(s["za_done"], i * 2 + (n + 1))
                    act.activation(za[:, n, :], za[:, n, :], ACT.Tanh, scale=0.5).then_inc(s["zt_done"], 1)
                act.wait_ge(s["lowrank"], i * 3 + 3)
                act.copy(g[:], PS[:T, 2, :]).then_inc(s["g_copied"], 1)
                act.wait_ge(s["gp_done"], i + 1)
                act.activation(e1[:], PS[:T, 3, :], ACT.Exp).then_inc(s["expd"], 1)
                act.activation(e2[:], PS[:T, 3, :], ACT.Exp, scale=-1.0).then_inc(s["expd"], 1)
                act.activation(e0[:], gp[:], ACT.Exp).then_inc(s["expd"], 1)
                act.activation(ecm[:], PS[:, 7, :PR * 8].rearrange("p (m c) -> p m c", m=PR), ACT.Exp)\
                    .then_inc(s["expd"], 1)
                act.wait_ge(s["turned"], i + 1)
                for n in range(2):
                    ins = act.copy(arT[:, :, n, :], pairs(PS[:, 4 + n, :])[:, :, :T])
                ins.then_inc(s["ar_copied"], 1)
                if sample:
                    act.wait_ge(s["s_turned"], 1)
                    act.copy(sT[:], PS[:, 3, :].rearrange("p (m a t) -> p m a t", m=PR, a=2)).then_inc(s["s0_done"], 1)
                act.wait_ge(s["u0_sum"], i + 1)
                act.copy(u0[:], PS[:T, 6, :]).then_inc(s["u0_done"], 1)
                inverse_act(act, I, inv, PS, T, levels, i)
                act.wait_ge(s["u_sum"], i + 1)
                act.copy(u[:], PS[:T, 7, :]).then_inc(s["u_done"], 1)
                act.wait_ge(s["centred"], i + 1)
                act.activation(sq[:], y[:], ACT.Square).then_inc(s["y_squared"], 1)
                act.wait_ge(s["y_turned"], i + 1)
                act.copy(mixT[:, :, bass.ds(i * P + tok0, T)], pairs(PS[:, 2, :])[:, :, :T]).then_inc(s["tile_done"], 1)
            tiles(act, body)
            for b in range(NSEQ):
                act.wait_ge(s["st_turned"], (NB if sample else 0) + b + 1)
                act.copy(pre[:, b], pairs(PS[:, b % 2, :])).then_inc(s["st_copied"], 1)

        @block.tensor
        def _(pe):
            if sample:
                pe.wait_ge(s["pre_in"], 16 * 2 * NB)
                for b in range(NB):
                    if b >= 2:
                        pe.wait_ge(s["state_done"], b - 1)
                    for m in range(PR):
                        mm = pe.transpose(PS[:, b % 2, m * P:(m + 1) * P], pre[:, b, m, :], ident[:])
                    mm.then_inc(s["st_turned"], 1)
                pe.wait_ge(s["state_done"], NB)
            if not sample:
                pe.wait_ge(s["par_in"], 16 * 11)

            def body(i):
                pe.wait_ge(s["gate_in"], i + 1)
                pe.sem_inc(pace, 1)
                for n in range(2):
                    mm = pe.transpose(PS[:, 6, n * T:(n + 1) * T], cur[:, 3 * RW_W + n * P:3 * RW_W + (n + 1) * P],
                                      ident[:T, :T])
                mm.then_inc(s["low_turned"], 1)
                pe.wait_ge(s["low_copied"], i + 1)
                for n in range(2):
                    pe.matmul(PS[:T, n, :], lowT[:, 0, :], wa2[:, n, :], start=True, stop=True)\
                        .then_inc(s["lowrank"], 1)
                pe.matmul(PS[:T, 2, :], lowT[:, 1, :], g2[:], start=True, stop=True).then_inc(s["lowrank"], 1)
                pe.wait_ge(s["setup"], n_setup)
                pe.wait_ge(s["logw_done"], i + 1)
                pe.matmul(PS[:T, 3, :], cen[:], gp[:], start=True, stop=True)
                for m in range(PR):
                    mm = pe.matmul(PS[:, 7, m * 8:(m + 1) * 8], gp[:, m * P:(m + 1) * P], cols[:], start=True,
                                   stop=True)
                mm.then_inc(s["summed"], 1)
                pe.wait_ge(s["tilded"], i + 1)
                pe.wait_ge(s["expd"], i * 4 + 4)
                pe.sem_inc(pace, 1)
                for n, t in enumerate((at, rt, bt, kt)):
                    for m in range(PR):
                        mm = pe.transpose(PS[:, 4 + n, m * P:m * P + T], t[:, m * P:(m + 1) * P], ident[:T, :T])
                mm.then_inc(s["turned"], 1)
                pe.wait_ge(s["ar_copied"], i + 1)
                pe.wait_ge(s["bk_copied"], i + 1)
                if sample:
                    for b in range(NB):
                        for m in range(PR):
                            o = PS[:, 3, m * 2 * T:(m + 1) * 2 * T].rearrange("p (a t) -> p a t", a=2)
                            mm = pe.matmul(o[:, :, b * TS:(b + 1) * TS], S[:, b, m, :],
                                           arT[:, m, :, b * TS:(b + 1) * TS], start=True, stop=True)
                    mm.then_inc(s["s_turned"], 1)
                    pe.wait_ge(s["s0_done"], 1)
                for gr in range(2):
                    for n, t in enumerate((bT, kT)):
                        for hh in range(GROUP):
                            h = gr * GROUP + hh
                            rows = slice((h % 2) * DH, (h % 2 + 1) * DH)
                            mm = pe.matmul(PS[:T, 4 * gr + 2 * n + hh % 2, (hh // 2) * 256:(hh // 2) * 256 + 2 * T],
                                           t[rows, h // 2, :], arT[rows, h // 2, :, :].rearrange("p a t -> p (a t)"),
                                           start=True, stop=True)
                        mm.then_inc(s["gram"], 1)
                pe.wait_ge(s["masked"], i * 4 + 4)
                pe.wait_ge(s["s0_done"], i + 1)

                def with_state(bank, n):
                    for m in range(PR):
                        c = slice(m * P, (m + 1) * P)
                        if sample:
                            pe.matmul(PS[:T, bank, c], sT[:, m, n, :], ident[:], start=True, stop=False)
                        else:
                            pe.matmul(PS[:T, bank, c], arT[:, m, n, :], S0[:, m, :], start=True, stop=False)
                        for h in (2 * m, 2 * m + 1):
                            hc = slice(h * DH, (h + 1) * DH)
                            if n:
                                pe.matmul(PS[:T, bank, hc], LB[:, h, 1, :], u[:, hc], start=False, stop=False)
                            mm = pe.matmul(PS[:T, bank, hc], LK[:, h, n, :],
                                           cur[:, 2 * RW_W + h * DH:2 * RW_W + (h + 1) * DH], start=False,
                                           stop=(h % 2 == 1))
                    return mm
                def between(l):
                    if l == 0:
                        with_state(6, 0).then_inc(s["u0_sum"], 1)
                inverse_pe(pe, C, I, inv, PS, T, levels, i, between)
                pe.wait_ge(s["u0_done"], i + 1)
                pe.wait_ge(inv["x_added"], i * (2 * levels) + 2 * levels)
                for h in range(H):
                    hc = slice(h * DH, (h + 1) * DH)
                    mm = pe.matmul(PS[:T, 7, hc], I["XT"][h // GROUP][:, h % GROUP, :], u0[:, hc], start=True,
                                   stop=True)
                mm.then_inc(s["u_sum"], 1)
                pe.wait_ge(s["u_done"], i + 1)
                if sample:
                    with_state(6, 1).then_inc(s["ys_sum"], 1)
                    for m in range(PR):
                        pe.wait_ge(s["spread"], m + 1)
                        for half in range(2):
                            for n, t in enumerate((bt, kt)):
                                mm = pe.matmul(PS[:, half, :], t[:, m * P:(m + 1) * P],
                                               ux[:, n, half * 4:half * 4 + 4, :].rearrange("p b c -> p (b c)"),
                                               start=(n == 0), stop=(n == 1))
                        mm.then_inc(s["ys_sum"], 1)
                else:
                    with_state(6, 1)
                    for m in range(PR):
                        c = slice(m * P, (m + 1) * P)
                        pe.matmul(PS[:, 0, c], bt[:, c], u[:, c], start=True, stop=False)
                        mm = pe.matmul(PS[:, 0, c], kt[:, c], cur[:, 2 * RW_W + m * P:2 * RW_W + (m + 1) * P],
                                       start=False, stop=True)
                    mm.then_inc(s["ys_sum"], 1)
                pe.wait_ge(s["y_done"], i + 1)
                pe.sem_inc(pace, 1)
                for m in range(PR):
                    mm = pe.transpose(PS[:, 2, m * P:m * P + T], y[:, m * P:(m + 1) * P], ident[:T, :T])
                mm.then_inc(s["y_turned"], 1)
            tiles(pe, body)
            pe.wait_ge(s["state_done"], 2 * NB if sample else NT)
            for b in range(NSEQ):
                if b >= 2:
                    pe.wait_ge(s["st_copied"], b - 1)
                for m in range(PR):
                    mm = pe.transpose(PS[:, b % 2, m * P:(m + 1) * P], S[:, b, m, :], ident[:])
                mm.then_inc(s["st_turned"], 1)

        @block.vector
        def _(dve):
            step = Chain(dve, dve_step, per=18 if sample else 16)
            if not sample:
                dve.wait_ge(s["par_in"], 16 * 11)
            k_, r_, v_ = cur[:, RW_W:2 * RW_W], cur[:, 0:RW_W], cur[:, 2 * RW_W:3 * RW_W]

            def body(i):
                step.turn(i)
                dve.wait_ge(s["mixed_in"], i + 1)
                dve.wait_ge(s["tile_done"], i + 1)
                low = slice(3 * RW_W, RW_COLS)
                dve.tensor_tensor(cur[:, low], prv[:, low], raw[:, low], ALU.add).then_inc(s["low_shifted"], 1)
                rkv = slice(0, 3 * RW_W)
                dve.tensor_tensor(cur[:, rkv], prv[:, rkv], raw[:, rkv], ALU.add).then_inc(s["shifted"], 1)
                dve.wait_ge(s["shifted"], i + 1)
                step(dve.tensor_tensor(kk[:], k_, par["k_k"][:], ALU.mult))
                step(dve.tensor_tensor(sq[:], kk[:], kk[:], ALU.mult))
                step(dve.tensor_reduce(s8[:], heads(sq[:]), AX.X, ALU.add))
                dve.tensor_scalar(m8[:], s8[:], 1e-6, None, ALU.add).then_inc(s["squared"], 1)
                dve.wait_ge(s["tanhd"], i + 1)
                gd = cur[:, 3 * RW_W + R_W + R_A:]
                dve.tensor_scalar(gd, gd, 0.5, 0.5, ALU.mult, ALU.add).then_inc(s["gate_in"], 1)
                dve.wait_ge(s["kk_rooted"], i + 1)
                step(dve.tensor_tensor(heads(kk[:]), heads(kk[:]), bc(r8[:], 2, DH), ALU.mult))
                for n in range(2):
                    dve.wait_ge(s["lowrank"], i * 3 + (n + 1))
                    dve.tensor_tensor(za[:, n, :], PS[:T, n, :], wa0[:, n, :], ALU.add).then_inc(s["za_done"], 1)
                dve.wait_ge(s["zt_done"], i * 2 + 1)
                dve.tensor_scalar(gp[:], za[:, 0, :], 0.5 * RW_DECAY, 0.5 * RW_DECAY, ALU.mult, ALU.add)\
                    .then_inc(s["logw_done"], 1)
                dve.wait_ge(s["zt_done"], i * 2 + 2)
                step(dve.tensor_scalar(za[:, 1, :], za[:, 1, :], 0.5, 0.5, ALU.mult, ALU.add))
                step(dve.scalar_tensor_tensor(kf[:], za[:, 1, :], 1.0, par["k_a"][:], ALU.subtract, ALU.mult))
                step(dve.scalar_tensor_tensor(kf[:], kf[:], 1.0, k_, ALU.add, ALU.mult))
                step(dve.tensor_tensor(bb[:], kk[:], za[:, 1, :], ALU.mult))
                dve.wait_ge(s["summed"], i + 1)
                dve.tensor_tensor(gp[:], PS[:T, 3, :], gp[:], ALU.subtract).then_inc(s["gp_done"], 1)
                dve.wait_ge(s["setup"], n_setup)
                dve.wait_ge(s["expd"], i * 4 + 1)
                dve.tensor_tensor(rt[:], r_, e1[:], ALU.mult)
                dve.wait_ge(s["expd"], i * 4 + 2)
                dve.tensor_tensor(bt[:], bb[:], e2[:], ALU.mult)
                dve.tensor_tensor(kt[:], kf[:], e2[:], ALU.mult)
                dve.wait_ge(s["expd"], i * 4 + 3)
                dve.scalar_tensor_tensor(at[:], kk[:], -1.0, e0[:], ALU.mult, ALU.mult).then_inc(s["tilded"], 1)
                dve.wait_ge(s["expd"], i * 4 + 4)
                if not sample:
                    dve.tensor_tensor(S0[:], S[:, 0], bc(ecm[:, :, 0], 2, P), ALU.mult).then_inc(s["s0_done"], 1)
                dve.wait_ge(s["turned"], i + 1)
                dve.tensor_copy(bT[:], pairs(PS[:, 6, :])[:, :, :T])
                dve.tensor_copy(kT[:], pairs(PS[:, 7, :])[:, :, :T]).then_inc(s["bk_copied"], 1)
                dve.wait_ge(s["rk_done"], i + 1)
                step(dve.tensor_reduce(bon[:], heads(rk[:]), AX.X, ALU.add))
                for n in range(4):
                    gr, t = divmod(n, 2)
                    dve.wait_ge(s["gram"], i * 4 + (n + 1))
                    dve.sem_inc(dve_pace, 1)
                    src = PS[:T, 4 * gr + 2 * t:4 * gr + 2 * t + 2, :].rearrange("p q (m x) -> p q m x", m=2)
                    dst = (LB, LK)[t][:, gr * GROUP:(gr + 1) * GROUP].rearrange("p (m q) a t -> p q m (a t)", q=2)
                    keep = bc(bc(mask.rearrange("p a t -> p (a t)"), 1, 2), 1, 2)
                    dve.copy_predicated(dst, keep.bitcast(I32), src[:, :, :, :2 * T]).then_inc(s["masked"], 1)
                inverse_dve(dve, C, I, inv, PS, T, levels, i)
                dve.wait_ge(s["ys_sum"], i + 1)
                step(dve.tensor_reduce(s8[:], heads(PS[:T, 6, :]), AX.X, ALU.add))
                step(dve.tensor_scalar(s8[:], s8[:], -1.0 / DH, None, ALU.mult))
                dve.tensor_tensor(heads(y[:]), heads(PS[:T, 6, :]), bc(s8[:], 2, DH), ALU.add).then_inc(s["centred"], 1)
                if not sample:
                    for q in range(2):
                        rows = slice(q * DH, (q + 1) * DH)
                        ins = dve.tensor_tensor(S[rows, 0, :, rows], pairs(PS[:, 0, :])[rows, :, rows],
                                                S0[rows, :, rows], ALU.add)
                    step(ins)
                    step(dve.tensor_tensor(S[:, 0], S[:, 0], bc(ecm[:, :, 1], 2, P), ALU.mult))
                    dve.sem_inc(s["state_done"], 1)
                else:
                    seg = bc(cols[:], 2, P)
                    for m in range(PR):
                        if m:
                            dve.wait_ge(s["ys_sum"], m + 1)
                        c = slice(m * P, (m + 1) * P)
                        dve.tensor_tensor(ux[:, 0], bc(u[:, c], 1, NB), seg, ALU.mult)
                        dve.tensor_tensor(ux[:, 1], bc(v_[:, c], 1, NB), seg, ALU.mult).then_inc(s["spread"], 1)
                        dve.wait_ge(s["ys_sum"], m + 2)
                        for q in range(2):
                            rows = slice(q * DH, (q + 1) * DH)
                            src = PS[:, 0:2, :].rearrange("p a (b c) -> p (a b) c", c=P)
                            ins = dve.tensor_tensor(S[rows, :, m, rows], src[rows, :, rows], S[rows, :, m, rows],
                                                    ALU.add)
                        step(ins)
                    for m in range(PR):
                        ins = dve.tensor_tensor(S[:, :, m, :], S[:, :, m, :], bc(ecm[:, m, :], 2, P), ALU.mult)
                    ins.then_inc(s["state_done"], NB)
                dve.wait_ge(s["y_squared"], i + 1)
                step(dve.tensor_reduce(s8[:], heads(sq[:]), AX.X, ALU.add))
                dve.tensor_scalar(m8[:], s8[:], 1.0 / DH, RW_GN_EPS, ALU.mult, ALU.add).then_inc(s["vr_done"], 1)
                dve.wait_ge(s["y_rooted"], i + 1)
                step(dve.tensor_tensor(heads(y[:]), heads(y[:]), bc(r8[:], 2, DH), ALU.mult))
                dve.wait_ge(s["vg_done"], i + 1)
                step(dve.tensor_tensor(y[:], y[:], gp[:], ALU.mult))
                dve.tensor_tensor(y[:], y[:], kk[:], ALU.add).then_inc(s["y_done"], 1)
                step.close()
            tiles(dve, body)


def gdn_gates(nc, C, zba, A_log, dt_bias, beta, gate):
    with Phase(nc, "gg") as ph:
        ba = ph.sb("ba", [P, NT + 1, 2 * H])
        ab = ph.sb("ab", [P, 2, H])
        x, e, l, eb = (ph.sb(n, [P, NT + 1, H]) for n in ("x", "e", "l", "eb"))
        rows_in, exps, negged = (ph.sem(n) for n in ("rows_in", "exps", "negged"))
        step_sem, zeroed = ph.sem("step"), ph.sem("zeroed")
        block = ph.block()
        cols = slice(GDN_W, GDN_W + 2 * H)

        @block.gpsimd
        def _(pool):
            pool.memset(ba[:], 0.0).then_inc(zeroed, 1)

        @block.sync
        def _(sp):
            sp.wait_ge(zeroed, 1)
            sp.dma_start(ba[:, 0:NT, :], zba[0:SEQ, cols].rearrange("(n p) c -> p n c", p=P)).then_inc(rows_in, 16)
            sp.dma_start(ba[:NS, NT, :], zba[SEQ:, cols]).then_inc(rows_in, 16)
            sp.dma_start(ab[:, 0, :], A_log.partition_broadcast(P)).then_inc(rows_in, 16)
            sp.dma_start(ab[:, 1, :], dt_bias.partition_broadcast(P)).then_inc(rows_in, 16)

        @block.scalar
        def _(act):
            act.wait_ge(rows_in, 64)
            act.activation(ab[:, 0, :], ab[:, 0, :], ACT.Exp)
            act.activation(eb[:], ba[:, :, 0:H], ACT.Exp, scale=-1.0).then_inc(exps, 1)
            act.wait_ge(negged, 1)
            act.activation(e[:], e[:], ACT.Exp).then_inc(exps, 1)
            act.wait_ge(exps, 2)
            act.activation(l[:], e[:], ACT.Ln, bias=1.0).then_inc(exps, 1)

        @block.vector
        def _(dve):
            step = Chain(dve, step_sem)
            dve.wait_ge(rows_in, 64)
            step(dve.tensor_tensor(x[:], ba[:, :, H:], bc(ab[:, 1, :], 1, NT + 1), ALU.add))
            dve.scalar_tensor_tensor(e[:], x[:], -1.0, x[:], ALU.mult, ALU.min).then_inc(negged, 1)
            dve.wait_ge(exps, 1)
            step(dve.tensor_scalar(eb[:], eb[:], 1.0, None, ALU.add))
            step(dve.reciprocal(beta[:], eb[:]))
            dve.wait_ge(exps, 3)
            step(dve.scalar_tensor_tensor(x[:], x[:], 0.0, l[:], ALU.max, ALU.add))
            step(dve.scalar_tensor_tensor(gate[:], x[:], -1.0, bc(ab[:, 0, :], 1, NT + 1), ALU.mult, ALU.mult))


def gdn(nc, C, sample, qkv, zba, beta, gate, norm_w, state_in, mixT, state_out):
    T = NS if sample else P
    NSEQ = NB if sample else 1
    levels = 3 if sample else 7
    tok0 = SEQ if sample else 0
    tile0 = NT if sample else 0
    with Phase(nc, "gs" if sample else "gd") as ph:
        qf = ph.sb("qf", [P, 3 * H, T])
        z = ph.sb("z", [T, GDN_W])
        zt = ph.sb("zt", [T, GDN_W])
        gain = ph.sb("gain", [T, DK])
        tri = C["blk_tri"] if sample else C["tri"]
        suf = ph.sb("suf", [T, T])
        mneg = ph.sb("mneg", [T, T])
        gt, bt = ph.sb("gt", [T, H]), ph.sb("bt", [T, H])
        gx = ph.sb("gx", [T, NSEQ, H])
        gb = ph.sb("gb", [T, H, T])
        Gs = ph.sb("Gs", [T, H])
        eg = ph.sb("eg", [T, 2, H])
        etot = ph.sb("etot", [P, NSEQ, H])
        gam = ph.sb("gam", [T, H, T])
        sq = ph.sb("sq", [T, 2 * H, DK])
        s16, m16, r16 = (ph.sb(n, [T, 2 * H]) for n in ("s16", "m16", "r16"))
        qn, kn, kb, ke, vb, u0, y0, w = (ph.sb(n, [T, H, DK]) for n in ("qn", "kn", "kb", "ke", "vb", "u0", "y0", "w"))
        y = sq[:, 0:H, :]
        ysq = sq[:, H:, :]
        kT = ph.sb("kT", [P, H, T])
        kqT = ph.sb("kqT", [P, H, 2, T])
        LA = ph.sb("LA", [T, H, 2, T])
        S = ph.sb("S", [P, NSEQ, H, DK])
        if sample:
            sT = ph.sb("sT", [P, H, 2, T])
            ux = ph.sb("ux", [T, NB, DK])
        I = inverse_buffers(ph, T)
        PS = ph.ps("PS", [P, 8, 512])
        inv = inverse_sems(ph)
        names = ("par_in setup q_in z_in gated_in spread_g gates_sum g_copied gates_exp rows_g diffed d_masked gam_done turned "
                 "squared meaned rooted normed scaled v_done t_turned t_copied gram masked st_prod st_copied ks_sum "
                 "ks_done qs_sum qs_done u0_done s_scaled w_sum w_done o_sum s_sum ux_done o_done ysq_done ym_done "
                 "y_rooted z_tanh z_done y_done y_turned tile_done state_done s_in out").split()
        s = {n: ph.sem(n) for n in names}
        dve_step, pool_step, pace, pool_pace = (ph.sem(n) for n in ("dve_step", "pool_step", "pace", "pool_pace"))
        block = ph.block()
        ident = C["ident"]

        def tiles(eng, body):
            if sample:
                body(0)
            else:
                with eng.Fori(0, NT) as i:
                    body(i)

        def two_banks(a, rows=T):
            return PS[:rows, a:a + 2, :].rearrange("p c (h d) -> p (c h) d", d=P)

        @block.sync
        def _(sp):
            sp.dma_start(gain[:], norm_w.partition_broadcast(T)).then_inc(s["par_in"], 16)
            def load_q(i):
                sp.dma_start(qf[:], qkv[:, :, bass.ds(i * P + tok0, T)].rearrange("f p t -> p f t")).then_inc(s["q_in"], 16)

            def load_z(i):
                sp.dma_start(z[:], zba[bass.ds(i * P + tok0, T), 0:GDN_W]).then_inc(s["z_in"], 16)
            load_q(0)
            load_z(0)
            if sample:
                for b in range(NB):
                    sp.dma_start(S[:, b], state_in[b].rearrange("h k v -> k h v")).then_inc(s["s_in"], 16)
            else:
                with sp.Fori(0, NT - 1) as i:
                    sp.wait_ge(s["turned"], i + 1)
                    load_q(i + 1)
                    sp.wait_ge(s["z_done"], i + 1)
                    load_z(i + 1)
            sp.wait_ge(s["state_done"], 1 if sample else NT + 1)
            for b in range(NSEQ):
                dst = state_out[b] if sample else state_out
                sp.dma_start(dst.rearrange("h k v -> k h v"), S[:, b]).then_inc(s["out"], 16)
            sp.wait_ge(s["out"], 16 * NSEQ)

        @block.gpsimd
        def _(pool):
            setup = Chain(pool, s["setup"])
            if sample:
                setup(pool.tensor_tensor(suf[:], C["blk_low"][:T, :T], ident[:T, :T], ALU.subtract))
            else:
                setup(pool.tensor_tensor(suf[:], C["ones"][:], C["tri"][:], ALU.subtract))
            setup(pool.tensor_scalar(mneg[:], tri[:T, :T], 1.0, -NEG, ALU.subtract, ALU.mult))
            if not sample:
                setup(pool.memset(S[:], 0.0))

            zstep = Chain(pool, pool_step, per=2)
            pool.wait_ge(s["par_in"], 17)

            def body(i):
                zstep.turn(i)
                pool.wait_ge(s["gated_in"], i + 1)
                pool.sem_inc(pool_pace, 1)
                pool.tensor_copy(gb[:], bc(gt[:], 2, T)).then_inc(s["spread_g"], 1)
                for c in range(2):
                    pool.wait_ge(s["diffed"], i * 2 + (c + 1))
                    pool.tensor_tensor(gam[:, 4 * c:4 * c + 4, :], gam[:, 4 * c:4 * c + 4, :],
                                       bc(mneg[:], 1, GROUP), ALU.add).then_inc(s["d_masked"], 1)
                pool.wait_ge(s["meaned"], i + 1)
                pool.tensor_tensor(r16[:], m16[:], C["half"][:T, :2 * H], ALU.pow).then_inc(s["rooted"], 1)
                pool.wait_ge(s["normed"], i + 1)
                pool.tensor_tensor(kb[:], kn[:], bc(bt[:], 2, DK), ALU.mult).then_inc(s["scaled"], 1)
                pool.wait_ge(s["gates_exp"], i + 1)
                pool.tensor_tensor(ke[:], kn[:], bc(eg[:, 1, :], 2, DK), ALU.mult)
                pool.wait_ge(s["z_tanh"], i + 1)
                zstep(pool.tensor_tensor(zt[:], zt[:], z[:], ALU.mult))
                zstep(pool.tensor_tensor(zt[:], zt[:], z[:], ALU.add))
                zh = zt.rearrange("p (h d) -> p h d", h=H)
                pool.tensor_tensor(zh, zh, bc(gain[:], 1, H), ALU.mult).then_inc(s["z_done"], 1)
                pool.wait_ge(s["masked"], i * 2 + 2)
                inverse_pool(pool, C, I, inv, LA[:, :, 0, :], T, levels, i)
                pool.wait_ge(s["qs_sum"], i + 1)
                pool.tensor_tensor(S[:], S[:], bc(etot[:], 3, DK), ALU.mult).then_inc(s["s_scaled"], 1)
                pool.wait_ge(s["ym_done"], i + 1)
                pool.tensor_tensor(r16[:, 0:H], m16[:, 0:H], C["half"][:T, :H], ALU.pow).then_inc(s["y_rooted"], 1)
            tiles(pool, body)

        @block.scalar
        def _(act):
            act.sem_inc(s["tile_done"], 1)

            def body(i):
                act.wait_ge(s["z_in"], i * 16 + 16)
                act.activation(zt[:], z[:], ACT.Tanh, scale=0.5).then_inc(s["z_tanh"], 1)
                act.wait_ge(s["g_copied"], i + 1)
                act.activation(eg[:], PS[:T, 7, 0:2 * H].rearrange("p (a h) -> p a h", a=2), ACT.Exp)
                act.activation(etot[:], PS[:, 7, 2 * H:(2 + NSEQ) * H].rearrange("p (b h) -> p b h", b=NSEQ), ACT.Exp)\
                    .then_inc(s["gates_exp"], 1)
                act.wait_ge(s["turned"], i + 1)
                act.activation(sq[:], PS[:T, 0:4, :].rearrange("p c (h d) -> p (c h) d", d=DK), ACT.Square)\
                    .then_inc(s["squared"], 1)
                for c in range(2):
                    act.wait_ge(s["d_masked"], i * 2 + (c + 1))
                    ins = act.activation(gam[:, 4 * c:4 * c + 4, :], gam[:, 4 * c:4 * c + 4, :], ACT.Exp)
                ins.then_inc(s["gam_done"], 1)
                for n in range(3):
                    act.wait_ge(s["t_turned"], i * 3 + (n + 1))
                    dst = kT[:] if n == 0 else kqT[:, :, n - 1, :]
                    act.copy(dst, two_banks(2 * n, P)[:, :, :T]).then_inc(s["t_copied"], 1)
                if sample:
                    act.wait_ge(s["st_prod"], 1)
                    act.copy(sT.rearrange("p h a t -> p h (a t)"), two_banks(6, P)).then_inc(s["st_copied"], 1)
                inverse_act(act, I, inv, PS, T, levels, i)
                act.wait_ge(s["w_sum"], i + 1)
                act.copy(w[:], two_banks(6)).then_inc(s["w_done"], 1)
                act.wait_ge(s["o_done"], i + 1)
                act.activation(ysq, y, ACT.Square).then_inc(s["ysq_done"], 1)
                act.wait_ge(s["y_turned"], i + 1)
                act.copy(mixT[:, :, bass.ds(i * P + tok0, T)], two_banks(4, P)[:, :, :T])\
                    .then_inc(s["tile_done"], 1)
            tiles(act, body)

        @block.tensor
        def _(pe):
            def body(i):
                pe.wait_ge(s["gated_in"], i + 1)
                pe.wait_ge(s["setup"], 2)
                pe.matmul(PS[:T, 7, 0:H], tri[:T, :T], gt[:], start=True, stop=True)
                pe.matmul(PS[:T, 7, H:2 * H], suf[:], gt[:], start=True, stop=True)
                pe.matmul(PS[:, 7, 2 * H:(2 + NSEQ) * H], C["ones"][:T, :], gx.rearrange("p b h -> p (b h)"),
                          start=True, stop=True).then_inc(s["gates_sum"], 1)
                pe.wait_ge(s["q_in"], i * 16 + 16)
                for f in range(3 * H):
                    mm = pe.transpose(PS[:T, f // 4, (f % 4) * P:(f % 4 + 1) * P], qf[:, f, :], ident[:])
                mm.then_inc(s["turned"], 1)
                pe.wait_ge(s["spread_g"], i + 1)
                pe.wait_ge(s["gates_exp"], i + 1)
                for c in range(2):
                    for h in range(GROUP):
                        mm = pe.matmul(PS[:T, 6 + c, h * P:h * P + T], gb[:, 4 * c + h, :], tri[:T, :T], start=True,
                                       stop=True)
                    mm.then_inc(s["rows_g"], 1)
                pe.wait_ge(s["v_done"], i + 1)
                for n, (t, ready) in enumerate(((kn, "normed"), (kb, "scaled"), (qn, "normed"))):
                    pe.wait_ge(s[ready], i + 1)
                    pe.sem_inc(pace, 1)
                    for h in range(H):
                        mm = pe.transpose(PS[:, 2 * n + h // 4, (h % 4) * P:(h % 4) * P + T], t[:, h, :], ident[:T, :T])
                    mm.then_inc(s["t_turned"], 1)
                pe.wait_ge(s["t_copied"], i * 3 + 3)
                if sample:
                    pe.wait_ge(s["diffed"], 2)
                    pe.wait_ge(s["s_in"], 16 * NB)
                    for b in range(NB):
                        for h in range(H):
                            o = PS[:, 6 + h // 4, (h % 4) * P:(h % 4 + 1) * P].rearrange("p (a t) -> p a t", a=2)
                            mm = pe.matmul(o[:, :, b * TS:(b + 1) * TS], S[:, b, h, :],
                                           kqT[:, h, :, b * TS:(b + 1) * TS], start=True, stop=True)
                    mm.then_inc(s["st_prod"], 1)
                    pe.wait_ge(s["st_copied"], 1)
                for gr in range(2):
                    for hh in range(GROUP):
                        h = gr * GROUP + hh
                        mm = pe.matmul(PS[:T, 4 * gr + hh // 2, (hh % 2) * 256:(hh % 2) * 256 + 2 * T], kT[:, h, :],
                                       kqT[:, h].rearrange("p a t -> p (a t)"), start=True, stop=True)
                    mm.then_inc(s["gram"], 1)
                pe.wait_ge(s["diffed"], i * 2 + 2)
                if not sample:
                    pe.wait_ge(s["state_done"], i + 1)

                def state_product(n):
                    for h in range(H):
                        o = PS[:T, 6 + h // 4, (h % 4) * P:(h % 4 + 1) * P]
                        if sample:
                            mm = pe.matmul(o, sT[:, h, n, :], ident[:], start=True, stop=True)
                        else:
                            mm = pe.matmul(o, kqT[:, h, n, :], S[:, 0, h, :], start=True, stop=True)
                    return mm
                def between(l):
                    if l == 0:
                        state_product(0).then_inc(s["ks_sum"], 1)
                    elif l == 1:
                        pe.wait_ge(s["ks_done"], i + 1)
                        state_product(1).then_inc(s["qs_sum"], 1)
                pe.wait_ge(s["masked"], i * 2 + 2)
                inverse_pe(pe, C, I, inv, PS, T, levels, i, between)
                pe.wait_ge(s["u0_done"], i + 1)
                pe.wait_ge(inv["x_added"], i * (2 * levels) + 2 * levels)
                pe.wait_ge(s["qs_done"], i + 1)
                for h in range(H):
                    mm = pe.matmul(PS[:T, 6 + h // 4, (h % 4) * P:(h % 4 + 1) * P],
                                   I["XT"][h // GROUP][:, h % GROUP, :], u0[:, h, :], start=True, stop=True)
                mm.then_inc(s["w_sum"], 1)
                pe.wait_ge(s["w_done"], i + 1)
                for h in range(H):
                    mm = pe.matmul(PS[:T, h // 4, (h % 4) * P:(h % 4 + 1) * P], LA[:, h, 1, :], w[:, h, :],
                                   start=True, stop=True)
                mm.then_inc(s["o_sum"], 1)
                if sample:
                    for h in range(H):
                        pe.wait_ge(s["ux_done"], h + 1)
                        for half in range(2):
                            mm = pe.matmul(PS[:, 2 + half, :], ke[:, h, :],
                                           ux[:, 4 * half:4 * half + 4, :].rearrange("p b c -> p (b c)"), start=True,
                                           stop=True)
                        mm.then_inc(s["s_sum"], 1)
                else:
                    for h in range(H):
                        mm = pe.matmul(PS[:, 2 + h // 4, (h % 4) * P:(h % 4 + 1) * P], ke[:, h, :], w[:, h, :],
                                       start=True, stop=True)
                    mm.then_inc(s["s_sum"], 1)
                pe.wait_ge(s["y_done"], i + 1)
                pe.sem_inc(pace, 1)
                for h in range(H):
                    mm = pe.transpose(PS[:, 4 + h // 4, (h % 4) * P:(h % 4) * P + T], y[:, h, :], ident[:T, :T])
                mm.then_inc(s["y_turned"], 1)
            tiles(pe, body)

        @block.vector
        def _(dve):
            if not sample:
                dve.sem_inc(s["state_done"], 1)
            step = Chain(dve, dve_step, per=14 if sample else 6)
            dve.wait_ge(s["par_in"], 16)
            dve.tensor_scalar(gain[:], gain[:], 0.5, None, ALU.mult).then_inc(s["par_in"], 1)
            dve.wait_ge(s["par_in"], 17)
            dve.wait_ge(s["setup"], 2 if sample else 3)

            def body(i):
                step.turn(i)
                dve.wait_ge(s["tile_done"], i + 1)
                step(dve.tensor_copy(gt[:], gate[:T, bass.ds(i + tile0, 1), :].rearrange("p o h -> p (o h)")))
                dve.tensor_scalar(bt[:], beta[:T, bass.ds(i + tile0, 1), :].rearrange("p o h -> p (o h)"), -1.0, None,
                                  ALU.mult)
                if sample:
                    ins = dve.tensor_tensor(gx[:], bc(gt[:], 1, NB), bc(C["blk"][:T, 0:T:TS], 2, H), ALU.mult)
                else:
                    ins = dve.tensor_copy(gx[:, 0], gt[:])
                ins.then_inc(s["gated_in"], 1)
                dve.wait_ge(s["gates_sum"], i + 1)
                dve.tensor_copy(Gs[:], PS[:T, 7, 0:H]).then_inc(s["g_copied"], 1)
                dve.wait_ge(s["squared"], i + 1)
                step(dve.tensor_reduce(s16[:], sq[:], AX.X, ALU.add))
                dve.tensor_scalar(m16[:], s16[:], 1e-6, None, ALU.add).then_inc(s["meaned"], 1)
                for c in range(2):
                    dve.wait_ge(s["rows_g"], i * 2 + (c + 1))
                    dve.tensor_tensor(gam[:, 4 * c:4 * c + 4, :],
                                      PS[:T, 6 + c, :].rearrange("p (h t) -> p h t", h=GROUP)[:, :, :T],
                                      bc(Gs[:, 4 * c:4 * c + 4], 2, T), ALU.subtract).then_inc(s["diffed"], 1)
                dve.wait_ge(s["rooted"], i + 1)
                step(dve.tensor_scalar(r16[:, 0:H], r16[:, 0:H], DK ** -0.5, None, ALU.mult))
                rows = PS[:T, 0:6, :].rearrange("p c (h d) -> p (c h) d", d=DK)
                dve.tensor_tensor(qn[:], rows[:, 0:H, :], bc(r16[:, 0:H], 2, DK), ALU.mult)
                dve.tensor_tensor(kn[:], rows[:, H:2 * H, :], bc(r16[:, H:], 2, DK), ALU.mult).then_inc(s["normed"], 1)
                step(dve.tensor_tensor(vb[:], rows[:, 2 * H:, :], bc(bt[:], 2, DK), ALU.mult))
                dve.sem_inc(s["v_done"], 1)
                dve.wait_ge(s["gam_done"], i + 1)
                for gr in range(2):
                    dve.wait_ge(s["gram"], i * 2 + (gr + 1))
                    src = PS[:T, 4 * gr:4 * gr + 2, :].rearrange("p c (m x) -> p (c m) x", m=2)[:, :, :2 * T]
                    dve.tensor_tensor(LA[:, 4 * gr:4 * gr + 4], src.rearrange("p h (a t) -> p h a t", a=2),
                                      bc(gam[:, 4 * gr:4 * gr + 4, :], 2, 2), ALU.mult).then_inc(s["masked"], 1)
                eG = bc(eg[:, 0, :], 2, DK)

                def between(l):
                    if l == 0:
                        dve.wait_ge(s["ks_sum"], i + 1)
                        dve.tensor_tensor(u0[:], two_banks(6), eG, ALU.mult).then_inc(s["ks_done"], 1)
                        dve.wait_ge(s["ks_done"], i + 1)
                        dve.tensor_tensor(u0[:], u0[:], vb[:], ALU.subtract).then_inc(s["u0_done"], 1)
                    elif l == 1:
                        dve.wait_ge(s["qs_sum"], i + 1)
                        dve.tensor_tensor(y0[:], two_banks(6), eG, ALU.mult).then_inc(s["qs_done"], 1)
                inverse_dve(dve, C, I, inv, PS, T, levels, i, between)
                dve.wait_ge(s["o_sum"], i + 1)
                dve.tensor_tensor(y, two_banks(0), y0[:], ALU.add).then_inc(s["o_done"], 1)
                dve.wait_ge(s["s_scaled"], i + 1)
                if sample:
                    seg = bc(C["blk"][:T, 0:T:TS], 2, DK)
                    for h in range(H):
                        step(dve.tensor_tensor(ux[:], bc(w[:, h, :], 1, NB), seg, ALU.mult))
                        dve.sem_inc(s["ux_done"], 1)
                        dve.wait_ge(s["s_sum"], h + 1)
                        ins = dve.tensor_tensor(S[:, :, h, :], two_banks(2, P), S[:, :, h, :], ALU.add)
                    ins.then_inc(s["state_done"], 1)
                else:
                    dve.wait_ge(s["s_sum"], i + 1)
                    dve.tensor_tensor(S[:, 0], two_banks(2, P), S[:, 0], ALU.add).then_inc(s["state_done"], 1)
                dve.wait_ge(s["ysq_done"], i + 1)
                step(dve.tensor_reduce(s16[:, 0:H], ysq, AX.X, ALU.add))
                dve.tensor_scalar(m16[:, 0:H], s16[:, 0:H], 1.0 / DK, EPS, ALU.mult, ALU.add).then_inc(s["ym_done"], 1)
                dve.wait_ge(s["y_rooted"], i + 1)
                step(dve.tensor_tensor(y, y, bc(r16[:, 0:H], 2, DK), ALU.mult))
                dve.wait_ge(s["z_done"], i + 1)
                dve.tensor_tensor(y, y, zt.rearrange("p (h d) -> p h d", h=H), ALU.mult).then_inc(s["y_done"], 1)
                step.close()
            tiles(dve, body)


def trunk(nc, I, O, scratch):
    ev, qkv, zba = scratch
    pf, prw = ev[1:, 0:FOX_COLS], ev[:, FOX_COLS:]
    Phase.used = []
    with Phase(nc, "trunk") as top:
        C = {k: top.sb(k, [P, P]) for k in ("ident", "ones", "tri", "half", "blk", "blk_low", "blk_tri")}
        C["join"] = top.sb("join", [P, 7, P])
        xT = top.sb("xT", [P, KD, NTOK])
        build_constants(nc, C)
        build_join(nc, C)
        load_x(nc, C, I["x"], xT)

        def parts(ph):
            return (ph.sb(n, [P, KD, NTOK], F32R) for n in ("high", "low"))

        with Phase(nc, "even_in") as ph:
            xh, xl = parts(ph)
            norm(nc, C, "n0", xT, I["norm_mix"][0], xh, xl)
            w = I["ev_w_in"][0]
            zero_row(nc, prw)
            project_rows(nc, "p_ev", xh, xl, w, EV_IN // 13, 13, ev[1:, :])
        with Phase(nc, "even_mix") as ph:
            foxT = ph.sb("foxT", [P, KD // 2, NTOK])
            with Phase(nc, "fox") as fx:
                sog = fx.sb("sog", [P, NT + 1, FOX_W])
                qTs, kTs = fx.sb("qTs", [P, 4, NS]), fx.sb("kTs", [P, 4, NS])
                lfs = fx.sb("lfs", [NS, H])
                with Phase(nc, "fox_p") as fp:
                    qkA = fp.sb("qkA", [P, 2 * H, SEQ])
                    fox_prep(nc, C, pf, I["fox_q_gain"][0], I["fox_k_gain"][0], I["fox_b_f"][0], qkA, sog, qTs, kTs,
                             lfs, O["fk"], O["fv"], O["flf"])
                    fox_prompt(nc, C, qkA, sog, O["fv"], foxT)
                fox_sample(nc, C, qTs, kTs, lfs, sog, O["fv"], I["cache_fox_k"], I["cache_fox_v"],
                           I["cache_fox_logf"], I["page_table"], foxT)
            rwT = ph.sb("rwT", [P, KD // 2, NTOK])
            W = {n: I["rw_" + n][0] for n in ("mu", "w0", "w2", "a0", "a2", "g2", "k_k", "k_a", "ln_w", "ln_b")}
            W["r_k"] = I["rw_r_k"][0].rearrange("h d -> (h d)")
            with Phase(nc, "rwt") as rp:
                R = rwkv_weights(rp)
                rwkv(nc, C, False, R, prw, None, None, W, rwT, O["rw_p"], O["sh_p"])
                rwkv(nc, C, True, R, prw, I["state_rwkv"][0], I["state_rwkv_shift"][0], W, rwT, O["rw_s"], O["sh_s"])
            mh, ml = parts(ph)
            project_back(nc, "back0", (foxT, rwT), mh, ml, I["ev_w_out"][0], xT)
        conv_ffn(nc, C, 0, I, O, xT, parts)
        with Phase(nc, "odd_in") as ph:
            xh, xl = parts(ph)
            w = I["od_w_in"][0]
            n, T1 = GDN_QKV // P, 3
            prev = ph.sb("prev", [P, n, NB * T1])
            tail = ph.sb("tail", [P, n, (NB + 1) * T1])
            taps = ph.sb("taps", [P, n, T1 + 1])
            norm(nc, C, "n1", xT, I["norm_mix"][1], xh, xl,
                 conv=(I["state_gdn_conv"][0], I["gdn_conv_w"][0], None, T1, prev, taps))
            conv_up(nc, C, "gqkv", xh, xl, w, T1 + 1, taps, prev, tail, dst=qkv)
            store_tail(nc, C, "gtail", tail, n, T1, O["gcv_p"], O["gcv_s"])
            project_rows(nc, "p_zba", xh, xl, w[:, GDN_QKV:], (GDN_W + 2 * H) // 4, 4, zba)
        with Phase(nc, "odd_mix") as ph:
            mixT = ph.sb("mixT", [P, KD, NTOK])
            with Phase(nc, "odd_gdn") as pg:
                beta, gate = (pg.sb(n, [P, NT + 1, H]) for n in ("beta", "gate"))
                gdn_gates(nc, C, zba, I["gdn_A_log"][0], I["gdn_dt_bias"][0], beta, gate)
                gdn(nc, C, False, qkv, zba, beta, gate, I["gdn_norm_w"][0], None, mixT, O["gdn_p"])
                gdn(nc, C, True, qkv, zba, beta, gate, I["gdn_norm_w"][0], I["state_gdn"][0], mixT, O["gdn_s"])
            mh, ml = parts(ph)
            project_back(nc, "back1", (mixT,), mh, ml, I["od_w_out"][0], xT)
        conv_ffn(nc, C, 1, I, O, xT, parts)
        store_y(nc, C, xT, I["norm_out"], O["y"])


def zero_row(nc, prw):
    with Phase(nc, "zero") as ph:
        z = ph.sb("z", [1, RW_COLS])
        made, out = ph.sem("made"), ph.sem("out")
        block = ph.block()

        @block.gpsimd
        def _(pool):
            pool.memset(z[:], 0.0).then_inc(made, 1)

        @block.sync
        def _(sp):
            sp.wait_ge(made, 1)
            sp.dma_start(prw[0:1, :], z[:]).then_inc(out, 16)
            sp.wait_ge(out, 16)


def conv_ffn(nc, C, layer, I, O, xT, parts):
    with Phase(nc, f"ffn{layer}") as ph:
        xh, xl = parts(ph)
        n, T1 = 2 * NF, 2
        prev = ph.sb("prev", [P, n, NB * T1])
        tail = ph.sb("tail", [P, n, (NB + 1) * T1])
        taps = ph.sb("taps", [P, n, T1 + 2])
        norm(nc, C, f"nf{layer}", xT, I["norm_ffn"][layer], xh, xl,
             conv=(I["state_ffn_conv"][layer], I["ffn_conv_w"][layer], I["ffn_conv_b"][layer], T1, prev, taps))
        conv_up(nc, C, f"fup{layer}", xh, xl, I["ffn_w_up"][layer], T1 + 1, taps, prev, tail,
                wd=I["ffn_w_down"][layer], xT=xT)
        store_tail(nc, C, f"ftail{layer}", tail, n, T1, O["fcv_p"][layer], O["fcv_s"][layer])


_INS = ["x", "cache_fox_k", "cache_fox_v", "cache_fox_logf", "state_rwkv", "state_rwkv_shift", "state_gdn",
        "state_gdn_conv", "state_ffn_conv", "page_table", "norm_mix", "norm_ffn", "norm_out", "ev_w_in", "ev_w_out",
        "fox_b_f", "fox_q_gain", "fox_k_gain", "rw_mu", "rw_w0", "rw_w2", "rw_a0", "rw_a2", "rw_g2", "rw_k_k",
        "rw_k_a", "rw_r_k", "rw_ln_w", "rw_ln_b", "od_w_in", "od_w_out", "gdn_conv_w", "gdn_A_log", "gdn_dt_bias",
        "gdn_norm_w", "ffn_w_up", "ffn_conv_w", "ffn_conv_b", "ffn_w_down"]
_OUTS = {"y": (NTOK, D), "fk": (NTOK, FOX_W), "fv": (NTOK, FOX_W), "flf": (NTOK, H), "rw_p": (H, DH, DH),
         "rw_s": (NB, H, DH, DH), "sh_p": (1, RW_COLS), "sh_s": (NB, RW_COLS), "gdn_p": (H, DK, DK),
         "gdn_s": (NB, H, DK, DK), "gcv_p": (3, GDN_QKV), "gcv_s": (NB, 3, GDN_QKV), "fcv_p": (2, 2, 2 * D_FF),
         "fcv_s": (2, NB, 2, 2 * D_FF)}


def kernel(**inputs):
    import numpy as np
    import concourse.bacc as bacc
    from concourse.bass_utils import run_bass_kernel_spmd

    arrays = {n: np.ascontiguousarray(inputs[n]) for n in _INS if n != "x"}
    arrays["x"] = np.concatenate([np.asarray(inputs["x_prompt"]).reshape(SEQ, D),
                                  np.asarray(inputs["x_sample"]).reshape(NS, D)])
    for n in ("cache_fox_k", "cache_fox_v"):
        arrays[n] = arrays[n].reshape(N_POOL, PAGE, FOX_W)
    arrays["cache_fox_logf"] = arrays["cache_fox_logf"].reshape(N_POOL, PAGE, H)

    nc = bacc.Bacc("TRN2", target_bir_lowering=False, num_devices=1)
    I = {n: nc.dram_tensor("in_" + n, arrays[n].shape, mybir.dt.from_np(arrays[n].dtype), kind="ExternalInput").ap()
         for n in _INS}
    O = {n: nc.dram_tensor("out_" + n, shape, F32, kind="ExternalOutput").ap() for n, shape in _OUTS.items()}
    scratch = [nc.dram_tensor(n, shape, F32, kind="Internal").ap() for n, shape in (
        ("ev", (NTOK + 1, EV_IN)), ("qkv", (GDN_QKV // P, P, NTOK)),
        ("zba", (NTOK, GDN_W + 2 * H)))]
    trunk(nc, I, O, scratch)
    r = run_bass_kernel_spmd(nc, [{"in_" + n: a for n, a in arrays.items()}], core_ids=[0]).results[0]
    r = {n: r["out_" + n] for n in _OUTS}

    def both(a, *tail):
        return a[:SEQ].reshape(1, 1, SEQ, *tail), a[SEQ:].reshape(1, NB, TS, *tail)
    (fk_p, fk_s), (fv_p, fv_s), (fl_p, fl_s) = both(r["fk"], H, DH), both(r["fv"], H, DH), both(r["flf"], H)
    return (r["y"][:SEQ].reshape(1, SEQ, D), r["y"][SEQ:].reshape(NB, TS, D), fk_p, fv_p, fl_p, fk_s, fv_s, fl_s,
            r["rw_p"][None, None], r["rw_s"][None], r["sh_p"][None], r["sh_s"][None],
            r["gdn_p"][None, None], r["gdn_s"][None], r["gcv_p"][None, None], r["gcv_s"][None],
            r["fcv_p"][:, None], r["fcv_s"])
```
